# Optimizing a Trainium2 kernel written in Bass

```python
import jax, jax.numpy as jnp
from jax import lax
import numpy as np
import math

D_MODEL = 1024
BATCH = 1
SEQ = 256
DEPTH = 2

D_MIX = D_MODEL
HEAD_DIM = 64
A_HEADS = 6
A_DIM = A_HEADS * HEAD_DIM
IDX_HEADS = 4
IDX_DIM = 64
TOPK_MAX = 256
Q_BLOCK = 128
B_HEADS = 6
B_DK = 64
B_DV = 64
B_DIM = B_HEADS * B_DV
HGRN_CHUNK = 64
C_GROUPS = 4
C_DIM = D_MIX - A_DIM - B_DIM
C_GROUP_DIM = C_DIM // C_GROUPS
C_CHUNK = 128
ROPE_THETA = 10000.0
F_DENSE = 2816
N_EXPERTS = 8
TOP_K = 2
F_EXPERT = 3584
N_DENSE = (DEPTH + 1) // 2
N_MOE = DEPTH // 2
EPS = 1e-6
IN_WIDTHS = (A_DIM, HEAD_DIM, HEAD_DIM, IDX_HEADS * IDX_DIM, IDX_DIM, IDX_HEADS, B_HEADS * B_DK, B_HEADS * B_DK, B_HEADS * B_DV, B_HEADS * B_DV, 2 * C_DIM)
IN_DIM = sum(IN_WIDTHS)


def rms_norm(x, g):
    xf = x.astype(jnp.float32)
    y = xf * lax.rsqrt(jnp.mean(xf * xf, axis=-1, keepdims=True) + EPS)
    return (y * g.astype(jnp.float32)).astype(x.dtype)

def layer_norm(x, g, b):
    xf = x.astype(jnp.float32)
    mu = jnp.mean(xf, axis=-1, keepdims=True)
    var = jnp.mean(jnp.square(xf - mu), axis=-1, keepdims=True)
    y = (xf - mu) * lax.rsqrt(var + EPS)
    return (y * g.astype(jnp.float32) + b.astype(jnp.float32)).astype(x.dtype)

def rope(x, pos):
    d = x.shape[-1]
    inv = ROPE_THETA ** (-jnp.arange(0, d, 2, dtype=jnp.float32) / d)
    ang = pos.astype(jnp.float32)[..., None] * inv
    cos = jnp.cos(ang)[:, :, None, :]
    sin = jnp.sin(ang)[:, :, None, :]
    xf = x.astype(jnp.float32)
    x1, x2 = xf[..., : d // 2], xf[..., d // 2:]
    return jnp.concatenate([x1 * cos - x2 * sin, x2 * cos + x1 * sin], axis=-1).astype(x.dtype)

def dsa_mixer(q, k, v, iq, ik, iw, positions):
    Bn, S = q.shape[0], q.shape[1]
    q = rope(q, positions)
    k = rope(k[:, :, None, :], positions)[:, :, 0, :]
    iq = rope(iq, positions)
    ik = rope(ik[:, :, None, :], positions)[:, :, 0, :]
    n_top = min(TOPK_MAX, S // 4)
    nb = S // Q_BLOCK
    to_blocks = lambda a: jnp.swapaxes(a.reshape((Bn, nb, Q_BLOCK) + a.shape[2:]), 0, 1)
    s_idx = jnp.arange(S)

    def one_block(args):
        qj, iqj, iwj, j = args
        t = j * Q_BLOCK + jnp.arange(Q_BLOCK)
        rel = jax.nn.relu(jnp.einsum('bqhd,bsd->bqhs', iqj, ik).astype(jnp.float32) * IDX_DIM ** -0.5)
        score = jnp.einsum('bqh,bqhs->bqs', iwj.astype(jnp.float32) * IDX_HEADS ** -0.5, rel)
        causal = s_idx[None, :] <= t[:, None]
        score = jnp.where(causal[None], score, -jnp.inf)
        _, idx = lax.top_k(score, n_top)
        flat = idx.reshape(Bn, Q_BLOCK * n_top, 1)
        kg = jnp.take_along_axis(k, flat, axis=1).reshape(Bn, Q_BLOCK, n_top, HEAD_DIM)
        vg = jnp.take_along_axis(v, flat, axis=1).reshape(Bn, Q_BLOCK, n_top, HEAD_DIM)
        logits = jnp.einsum('bqhd,bqkd->bqhk', qj, kg).astype(jnp.float32) * HEAD_DIM ** -0.5
        valid = idx <= t[None, :, None]
        logits = jnp.where(valid[:, :, None, :], logits, -jnp.inf)
        p = jax.nn.softmax(logits, axis=-1).astype(v.dtype)
        return jnp.einsum('bqhk,bqkd->bqhd', p, vg)

    out = lax.map(one_block, (to_blocks(q), to_blocks(iq), to_blocks(iw), jnp.arange(nb)))
    return jnp.swapaxes(out, 0, 1).reshape(Bn, S, A_HEADS * HEAD_DIM)

def hgrn2_mixer(q, f_logit, i, g, lb, onorm_g):
    Bn, S, H, dk = q.shape
    dv = i.shape[-1]
    lb = lb.reshape(H, dk).astype(jnp.float32)
    log_f = jnp.logaddexp(jnp.log(lb), jnp.log1p(-lb) + jax.nn.log_sigmoid(f_logit.astype(jnp.float32)))
    kk = -jnp.expm1(log_f)
    nc = S // HGRN_CHUNK
    chunk = lambda a: a.astype(jnp.float32).reshape(Bn, nc, HGRN_CHUNK, H, a.shape[-1]).transpose(1, 0, 3, 2, 4)
    qc, kc, vc, lfc = chunk(q), chunk(kk), chunk(i), chunk(log_f)
    bc = jnp.cumsum(lfc, axis=3)
    tril = jnp.arange(HGRN_CHUNK)[:, None] >= jnp.arange(HGRN_CHUNK)[None, :]

    def step(state, xs):
        qj, kj, vj, bj = xs
        diff = bj[:, :, :, None, :] - bj[:, :, None, :, :]
        decay = jnp.exp(jnp.where(tril[:, :, None], diff, -jnp.inf))
        attn = jnp.einsum('bhtd,bhsd,bhtsd->bhts', qj, kj, decay)
        o = jnp.einsum('bhts,bhsv->bhtv', attn, vj) + jnp.einsum('bhtd,bhdv->bhtv', qj * jnp.exp(bj), state)
        b_last = bj[:, :, -1:, :]
        new_state = jnp.exp(b_last[:, :, 0, :])[..., None] * state + jnp.einsum('bhsd,bhsv->bhdv', kj * jnp.exp(b_last - bj), vj)
        return new_state, o

    s0 = jnp.zeros((Bn, H, dk, dv), jnp.float32)
    _, o = lax.scan(step, s0, (qc, kc, vc, bc))
    o = o.transpose(1, 0, 3, 2, 4).reshape(Bn, S, H, dv)
    o = rms_norm(o, onorm_g) * jax.nn.silu(g.astype(jnp.float32))
    return o.reshape(Bn, S, H * dv).astype(q.dtype)

def gmlp_mixer(uv, vn_g, vn_b, ws, bs):
    Bn, S = uv.shape[0], uv.shape[1]
    uv = jax.nn.gelu(uv, approximate=False)
    u, v = uv[..., :C_DIM], uv[..., C_DIM:]
    v = layer_norm(v, vn_g, vn_b)
    nc = S // C_CHUNK
    v = v.reshape(Bn, nc, C_CHUNK, C_GROUPS, C_GROUP_DIM)
    mask = jnp.tril(jnp.ones((C_CHUNK, C_CHUNK), ws.dtype))
    w = ws * mask[None]
    mixed = jnp.einsum('gts,bnsgd->bntgd', w, v) + bs.T[None, None, :, :, None]
    return u * mixed.reshape(Bn, S, C_DIM)

def swiglu(h, w_gate, w_up, w_down):
    return (jax.nn.silu(h @ w_gate) * (h @ w_up)) @ w_down

def moe_swiglu(h, w_router, w_gate, w_up, w_down):
    logits = jnp.einsum('bsd,de->bse', h, w_router).astype(jnp.float32)
    top_v, top_i = lax.top_k(logits, TOP_K)
    wts = jax.nn.softmax(top_v, axis=-1)
    gates = jnp.sum(jax.nn.one_hot(top_i, N_EXPERTS, dtype=jnp.float32) * wts[..., None], axis=-2)

    def per_seq(args):
        hb, gb = args
        a = jnp.einsum('sd,edf->sef', hb, w_gate)
        u = jnp.einsum('sd,edf->sef', hb, w_up)
        act = jax.nn.silu(a) * u * gb[:, :, None]
        return jnp.einsum('sef,efd->sd', act, w_down)

    return lax.map(per_seq, (h, gates.astype(h.dtype)))

def first_inputs(seed: int = 0) -> dict:
    key = jax.random.key(seed)
    ks = jax.random.split(key, 24)
    nrm = lambda k, shape, s: jax.random.normal(k, shape, jnp.float32) * s
    x = nrm(ks[0], (BATCH, SEQ, D_MODEL), 1.0)
    c = nrm(ks[1], (BATCH, D_MODEL), 1.0)
    offsets = jax.random.randint(ks[2], (BATCH, 1), 0, 4096, dtype=jnp.int32)
    positions = offsets + jnp.arange(SEQ, dtype=jnp.int32)[None, :]
    return {
        "x": x,
        "c": c,
        "positions": positions,
        "w_ada": nrm(ks[3], (DEPTH, D_MODEL, 6 * D_MODEL), 0.5 * D_MODEL ** -0.5),
        "b_ada": nrm(ks[4], (DEPTH, 6 * D_MODEL), 0.02),
        "g_norm_mix": 1.0 + nrm(ks[5], (DEPTH, D_MODEL), 0.02),
        "g_norm_ffn": 1.0 + nrm(ks[6], (DEPTH, D_MODEL), 0.02),
        "w_in": nrm(ks[7], (DEPTH, D_MODEL, IN_DIM), D_MODEL ** -0.5),
        "w_out": nrm(ks[8], (DEPTH, D_MIX, D_MODEL), D_MIX ** -0.5),
        "hgrn_lb_logits": nrm(ks[9], (DEPTH, B_HEADS * B_DK), 0.5),
        "hgrn_out_norm": 1.0 + nrm(ks[10], (DEPTH, B_DV), 0.02),
        "gmlp_vnorm_g": 1.0 + nrm(ks[11], (DEPTH, C_DIM), 0.02),
        "gmlp_vnorm_b": nrm(ks[12], (DEPTH, C_DIM), 0.02),
        "gmlp_w_s": nrm(ks[13], (DEPTH, C_GROUPS, C_CHUNK, C_CHUNK), C_CHUNK ** -0.5),
        "gmlp_b_s": 1.0 + nrm(ks[14], (DEPTH, C_GROUPS, C_CHUNK), 0.02),
        "ffn_w_gate": nrm(ks[15], (N_DENSE, D_MODEL, F_DENSE), D_MODEL ** -0.5),
        "ffn_w_up": nrm(ks[16], (N_DENSE, D_MODEL, F_DENSE), D_MODEL ** -0.5),
        "ffn_w_down": nrm(ks[17], (N_DENSE, F_DENSE, D_MODEL), F_DENSE ** -0.5),
        "moe_w_router": nrm(ks[18], (N_MOE, D_MODEL, N_EXPERTS), D_MODEL ** -0.5),
        "moe_w_gate": nrm(ks[19], (N_MOE, N_EXPERTS, D_MODEL, F_EXPERT), D_MODEL ** -0.5),
        "moe_w_up": nrm(ks[20], (N_MOE, N_EXPERTS, D_MODEL, F_EXPERT), D_MODEL ** -0.5),
        "moe_w_down": nrm(ks[21], (N_MOE, N_EXPERTS, F_EXPERT, D_MODEL), F_EXPERT ** -0.5),
        "g_final": 1.0 + nrm(ks[22], (D_MODEL,), 0.02),
    }

def first_block(x, c, positions, w_ada, b_ada, g_norm_mix, g_norm_ffn, w_in, w_out, hgrn_lb_logits, hgrn_out_norm, gmlp_vnorm_g, gmlp_vnorm_b, gmlp_w_s, gmlp_b_s, ffn_w_gate, ffn_w_up, ffn_w_down, moe_w_router, moe_w_gate, moe_w_up, moe_w_down, g_final):
    Bn, S = x.shape[0], x.shape[1]
    p_lb = jax.nn.softmax(hgrn_lb_logits.astype(jnp.float32), axis=0)
    cum = jnp.cumsum(p_lb, axis=0)
    lower_bounds = cum - cum[0:1]
    splits = [int(s) for s in np.cumsum(IN_WIDTHS)[:-1]]
    cond = jax.nn.silu(c)
    for l in range(DEPTH):
        mod = cond @ w_ada[l] + b_ada[l]
        sh1, sc1, g1, sh2, sc2, g2 = [m[:, None, :] for m in jnp.split(mod, 6, axis=-1)]
        h = rms_norm(x, g_norm_mix[l]) * (1 + sc1) + sh1
        z = h @ w_in[l]
        aq, ak, av, iq, ik, iw, bq, bf, bi, bg, cuv = jnp.split(z, splits, axis=-1)
        a_out = dsa_mixer(aq.reshape(Bn, S, A_HEADS, HEAD_DIM), ak, av, iq.reshape(Bn, S, IDX_HEADS, IDX_DIM), ik, iw, positions)
        b_out = hgrn2_mixer(bq.reshape(Bn, S, B_HEADS, B_DK), bf.reshape(Bn, S, B_HEADS, B_DK), bi.reshape(Bn, S, B_HEADS, B_DV), bg.reshape(Bn, S, B_HEADS, B_DV), lower_bounds[l], hgrn_out_norm[l])
        c_out = gmlp_mixer(cuv, gmlp_vnorm_g[l], gmlp_vnorm_b[l], gmlp_w_s[l], gmlp_b_s[l])
        mix = jnp.concatenate([a_out, b_out, c_out], axis=-1) @ w_out[l]
        x = x + g1 * mix
        h = rms_norm(x, g_norm_ffn[l]) * (1 + sc2) + sh2
        if l % 2 == 0:
            y = swiglu(h, ffn_w_gate[l // 2], ffn_w_up[l // 2], ffn_w_down[l // 2])
        else:
            y = moe_swiglu(h, moe_w_router[l // 2], moe_w_gate[l // 2], moe_w_up[l // 2], moe_w_down[l // 2])
        x = x + g2 * y
    return rms_norm(x, g_final)


NSA_HEADS = 6
NSA_KV_GROUPS = 2
NSA_REP = NSA_HEADS // NSA_KV_GROUPS
N_BRANCH = 3
CMP_LEN = 32
CMP_STRIDE = 16
CMP_HIDDEN = 2 * HEAD_DIM
SEL_BLOCK = 64
SEL_TOP_N = 16
WINDOW = 512
NSA_Q_BLOCK = 32
MLA_HEADS = 5
MLA_Q_RANK = 256
MLA_KV_RANK = 128
MLA_NOPE_DIM = 64
MLA_ROPE_DIM = 32
MLA_V_DIM = 64
ATTN_Q_BLOCK = 128
RET_HEADS = 5
RET_CHUNK = 128
ROPE_THETA_2 = 500000.0
PARTIAL_ROPE_DIM = HEAD_DIM // 4
RET_THETA = 10000.0
D_FF = 4 * D_MODEL
NORM_EPS = 1e-6
NEG_INF = -1e30
FORCE_SCORE = 1e9

NSA_Q_W = NSA_HEADS * HEAD_DIM
NSA_KV_W = NSA_KV_GROUPS * HEAD_DIM
NSA_GATE_W = NSA_HEADS * N_BRANCH
MLA_OUT_W = MLA_HEADS * MLA_V_DIM
RET_W = RET_HEADS * HEAD_DIM
MIX_WIDTH = NSA_Q_W + MLA_OUT_W + RET_W
IN_SIZES = (NSA_Q_W, NSA_KV_W, NSA_KV_W, NSA_KV_W, NSA_KV_W, NSA_KV_W, NSA_KV_W, NSA_GATE_W,
            MLA_Q_RANK, MLA_KV_RANK, MLA_ROPE_DIM, RET_W, RET_W, RET_W, RET_W)
N_IN = sum(IN_SIZES)


F32 = jnp.float32

def in_offsets():
    return [int(o) for o in np.cumsum(IN_SIZES)[:-1]]

def rms_norm_2(x, gain):
    xf = x.astype(F32)
    y = xf * lax.rsqrt(jnp.mean(xf * xf, axis=-1, keepdims=True) + NORM_EPS) * gain.astype(F32)
    return y.astype(x.dtype)

def masked_softmax(s, mask):
    s = jnp.where(mask, s.astype(F32), NEG_INF)
    m = jnp.max(s, axis=-1, keepdims=True)
    p = jnp.exp(s - m) * mask
    return p / jnp.maximum(jnp.sum(p, axis=-1, keepdims=True), 1e-30)

def rope_tables(positions, dim, theta):
    inv = 1.0 / (theta ** (jnp.arange(0, dim, 2, dtype=F32) / dim))
    ang = positions.astype(F32)[..., None] * inv
    return jnp.cos(ang), jnp.sin(ang)

def apply_rope(x, cos, sin):
    half = x.shape[-1] // 2
    x1 = x[..., :half].astype(F32)
    x2 = x[..., half:].astype(F32)
    c = cos[:, :, None, :]
    s = sin[:, :, None, :]
    return jnp.concatenate([x1 * c - x2 * s, x2 * c + x1 * s], axis=-1).astype(x.dtype)

def partial_rope(x, cos, sin):
    return jnp.concatenate([apply_rope(x[..., :PARTIAL_ROPE_DIM], cos, sin), x[..., PARTIAL_ROPE_DIM:]], axis=-1)

def selection_overlap(n_cmp, n_sel):
    cs = np.arange(n_cmp) * CMP_STRIDE
    ce = cs + CMP_LEN
    ss = np.arange(n_sel) * SEL_BLOCK
    se = ss + SEL_BLOCK
    ov = np.clip(np.minimum(ce[:, None], se[None, :]) - np.maximum(cs[:, None], ss[None, :]), 0, None) / CMP_LEN
    return jnp.asarray(ov.astype(np.float32))

def compress_blocks(tok, tok_idx, pos_emb, w1, w2):
    b, _, g, dh = tok.shape
    blk = tok[:, tok_idx] + pos_emb[None, None, :, None, :]
    flat = blk.transpose(0, 1, 3, 2, 4).reshape(b, tok_idx.shape[0], g, CMP_LEN * dh)
    return jax.nn.gelu(flat @ w1) @ w2

def nsa_mixer(q, k_cmp, v_cmp, k_slc, v_slc, k_win, v_win, gates, pos_k, w1_k, w2_k, pos_v, w1_v, w2_v):
    b, s, _, dh = q.shape
    g, r = NSA_KV_GROUPS, NSA_REP
    n_cmp = (s - CMP_LEN) // CMP_STRIDE + 1
    n_sel = s // SEL_BLOCK
    top_n = min(SEL_TOP_N, n_sel)
    scale = dh ** -0.5
    qb_len = NSA_Q_BLOCK

    tok_idx = np.arange(n_cmp)[:, None] * CMP_STRIDE + np.arange(CMP_LEN)[None, :]
    kc = compress_blocks(k_cmp, tok_idx, pos_k, w1_k, w2_k)
    vc = compress_blocks(v_cmp, tok_idx, pos_v, w1_v, w2_v)
    cmp_end = jnp.arange(n_cmp) * CMP_STRIDE + CMP_LEN - 1
    overlap = selection_overlap(n_cmp, n_sel)

    ks_blk = k_slc.reshape(b, n_sel, SEL_BLOCK, g, dh).transpose(0, 3, 1, 2, 4)
    vs_blk = v_slc.reshape(b, n_sel, SEL_BLOCK, g, dh).transpose(0, 3, 1, 2, 4)
    kw_pad = jnp.pad(k_win, ((0, 0), (WINDOW, 0), (0, 0), (0, 0)))
    vw_pad = jnp.pad(v_win, ((0, 0), (WINDOW, 0), (0, 0), (0, 0)))

    n_qb = s // qb_len
    q_blocks = q.reshape(b, n_qb, qb_len, g, r, dh).transpose(1, 0, 2, 3, 4, 5)
    gate_blocks = jax.nn.sigmoid(gates.astype(F32)).reshape(b, n_qb, qb_len, g, r, N_BRANCH).transpose(1, 0, 2, 3, 4, 5)
    b_idx = jnp.arange(b)[:, None, None, None]
    g_idx = jnp.arange(g)[None, :, None, None]
    sel_ids = jnp.arange(n_sel)[None, :]

    def block(args):
        qb, gb, i = args
        q0 = i * qb_len
        t = q0 + jnp.arange(qb_len)
        s_c = jnp.einsum('bqgrd,bngd->bgrqn', qb, kc) * scale
        p_c = masked_softmax(s_c, cmp_end[None, :] <= t[:, None])
        o_c = jnp.einsum('bgrqn,bngd->bqgrd', p_c, vc)
        imp = jnp.einsum('bgrqn,nm->bgqm', p_c, overlap)
        cur = (t // SEL_BLOCK)[:, None]
        valid = sel_ids <= cur
        forced = (sel_ids == 0) | (sel_ids == cur) | (sel_ids == cur - 1)
        imp = jnp.where(valid & forced, FORCE_SCORE, imp)
        imp = jnp.where(valid, imp, NEG_INF)
        _, idx = lax.top_k(imp, top_n)
        k_sel = ks_blk[b_idx, g_idx, idx]
        v_sel = vs_blk[b_idx, g_idx, idx]
        key_pos = idx[..., None] * SEL_BLOCK + jnp.arange(SEL_BLOCK)
        mask_s = (key_pos <= t[None, None, :, None, None]).reshape(b, g, 1, qb_len, top_n * SEL_BLOCK)
        s_s = jnp.einsum('bqgrd,bgqjsd->bgrqjs', qb, k_sel).reshape(b, g, r, qb_len, top_n * SEL_BLOCK) * scale
        p_s = masked_softmax(s_s, mask_s).reshape(b, g, r, qb_len, top_n, SEL_BLOCK)
        o_s = jnp.einsum('bgrqjs,bgqjsd->bqgrd', p_s, v_sel)
        kw = lax.dynamic_slice_in_dim(kw_pad, q0, qb_len + WINDOW, axis=1)
        vw = lax.dynamic_slice_in_dim(vw_pad, q0, qb_len + WINDOW, axis=1)
        kp = (q0 - WINDOW + jnp.arange(qb_len + WINDOW))[None, :]
        mask_w = (kp <= t[:, None]) & (kp > t[:, None] - WINDOW) & (kp >= 0)
        s_w = jnp.einsum('bqgrd,bkgd->bgrqk', qb, kw) * scale
        p_w = masked_softmax(s_w, mask_w)
        o_w = jnp.einsum('bgrqk,bkgd->bqgrd', p_w, vw)
        return gb[..., 0:1] * o_c + gb[..., 1:2] * o_s + gb[..., 2:3] * o_w

    out = lax.map(block, (q_blocks, gate_blocks, jnp.arange(n_qb)))
    return out.transpose(1, 0, 2, 3, 4, 5).reshape(b, s, NSA_HEADS * dh)

def causal_block_attention(q, k, v, scale):
    b, s, h, dq = q.shape
    n_qb = s // ATTN_Q_BLOCK
    q_blocks = q.reshape(b, n_qb, ATTN_Q_BLOCK, h, dq).transpose(1, 0, 2, 3, 4)
    kp = jnp.arange(s)[None, :]

    def block(args):
        qi, i = args
        t = (i * ATTN_Q_BLOCK + jnp.arange(ATTN_Q_BLOCK))[:, None]
        sc = jnp.einsum('bqhd,bkhd->bhqk', qi, k) * scale
        p = masked_softmax(sc, kp <= t)
        return jnp.einsum('bhqk,bkhd->bqhd', p, v)

    out = lax.map(block, (q_blocks, jnp.arange(n_qb)))
    return out.transpose(1, 0, 2, 3, 4).reshape(b, s, h, v.shape[-1])

def mla_mixer(c_q, c_kv, k_pe, q_norm, w_uq, kv_norm, w_ukv, cos, sin):
    b, s, _ = c_q.shape
    q = (rms_norm_2(c_q, q_norm) @ w_uq).reshape(b, s, MLA_HEADS, MLA_NOPE_DIM + MLA_ROPE_DIM)
    q_nope, q_pe = q[..., :MLA_NOPE_DIM], apply_rope(q[..., MLA_NOPE_DIM:], cos, sin)
    kv = (rms_norm_2(c_kv, kv_norm) @ w_ukv).reshape(b, s, MLA_HEADS, MLA_NOPE_DIM + MLA_V_DIM)
    k_nope, v = kv[..., :MLA_NOPE_DIM], kv[..., MLA_NOPE_DIM:]
    k_pe = apply_rope(k_pe[:, :, None, :], cos, sin)
    q_full = jnp.concatenate([q_nope, q_pe], axis=-1)
    k_full = jnp.concatenate([k_nope, jnp.broadcast_to(k_pe, (b, s, MLA_HEADS, MLA_ROPE_DIM)).astype(k_nope.dtype)], axis=-1)
    o = causal_block_attention(q_full, k_full, v, (MLA_NOPE_DIM + MLA_ROPE_DIM) ** -0.5)
    return o.reshape(b, s, MLA_OUT_W)

def chunkwise_retention(q, k, v):
    b, s, h, d = q.shape
    n = s // RET_CHUNK
    log_g = jnp.log(1.0 - 2.0 ** (-5.0 - jnp.arange(h, dtype=F32)))
    i = jnp.arange(RET_CHUNK, dtype=F32)
    diff = i[:, None] - i[None, :]
    intra = jnp.where(diff >= 0, jnp.exp(jnp.maximum(diff, 0.0)[None] * log_g[:, None, None]), 0.0)
    read_decay = jnp.exp((i + 1.0)[None, :] * log_g[:, None])[None, :, :, None]
    write_decay = jnp.exp((RET_CHUNK - 1.0 - i)[None, :] * log_g[:, None])[None, :, :, None]
    chunk_decay = jnp.exp(RET_CHUNK * log_g)[None, :, None, None]

    def to_chunks(a):
        return a.reshape(b, n, RET_CHUNK, h, d).transpose(1, 0, 3, 2, 4)

    def step(state, xs):
        qc, kc, vc = xs
        sc = jnp.einsum('bhid,bhjd->bhij', qc, kc) * intra
        o = jnp.einsum('bhij,bhjd->bhid', sc, vc) + jnp.einsum('bhid,bhde->bhie', qc, state) * read_decay
        state = state * chunk_decay + jnp.einsum('bhjd,bhje->bhde', kc * write_decay, vc)
        return state, o

    state0 = jnp.zeros((b, h, d, d), F32)
    _, outs = lax.scan(step, state0, (to_chunks(q), to_chunks(k), to_chunks(v)))
    return outs.transpose(1, 0, 3, 2, 4).reshape(b, s, h, d)

def retention_mixer(q, k, v, gate, gn_gain, cos, sin):
    b, s, _ = q.shape
    h, d = RET_HEADS, HEAD_DIM
    q = apply_rope(q.reshape(b, s, h, d), cos, sin).astype(F32)
    k = apply_rope(k.reshape(b, s, h, d), cos, sin).astype(F32) * (d ** -0.5)
    v = v.reshape(b, s, h, d).astype(F32)
    o = chunkwise_retention(q, k, v)
    mu = jnp.mean(o, axis=-1, keepdims=True)
    var = jnp.mean(jnp.square(o - mu), axis=-1, keepdims=True)
    o = (o - mu) * lax.rsqrt(var + NORM_EPS) * gn_gain.astype(F32)
    return jax.nn.silu(gate.astype(F32)) * o.reshape(b, s, h * d)

def second_inputs(seed: int = 0) -> dict:
    key = jax.random.key(seed)
    ks = jax.random.split(key, 24)

    def nrm(k, shape, scale):
        return scale * jax.random.normal(k, shape, F32)

    def gain(k, shape):
        return 1.0 + 0.02 * jax.random.normal(k, shape, F32)

    offs = jax.random.randint(ks[1], (BATCH, 1), 0, 4096)
    positions = (jnp.arange(SEQ, dtype=jnp.int32)[None, :] + offs).astype(jnp.int32)
    return {
        'x': nrm(ks[0], (BATCH, SEQ, D_MODEL), 1.0),
        'positions': positions,
        'ln1_gain': gain(ks[2], (DEPTH, D_MODEL)),
        'w_in': nrm(ks[3], (DEPTH, D_MODEL, N_IN), D_MODEL ** -0.5),
        'cmp_pos_k': nrm(ks[4], (DEPTH, CMP_LEN, HEAD_DIM), 0.1),
        'cmp_w1_k': nrm(ks[5], (DEPTH, CMP_LEN * HEAD_DIM, CMP_HIDDEN), (CMP_LEN * HEAD_DIM) ** -0.5),
        'cmp_w2_k': nrm(ks[6], (DEPTH, CMP_HIDDEN, HEAD_DIM), CMP_HIDDEN ** -0.5),
        'cmp_pos_v': nrm(ks[7], (DEPTH, CMP_LEN, HEAD_DIM), 0.1),
        'cmp_w1_v': nrm(ks[8], (DEPTH, CMP_LEN * HEAD_DIM, CMP_HIDDEN), (CMP_LEN * HEAD_DIM) ** -0.5),
        'cmp_w2_v': nrm(ks[9], (DEPTH, CMP_HIDDEN, HEAD_DIM), CMP_HIDDEN ** -0.5),
        'mla_q_norm': gain(ks[10], (DEPTH, MLA_Q_RANK)),
        'mla_w_uq': nrm(ks[11], (DEPTH, MLA_Q_RANK, MLA_HEADS * (MLA_NOPE_DIM + MLA_ROPE_DIM)), MLA_Q_RANK ** -0.5),
        'mla_kv_norm': gain(ks[12], (DEPTH, MLA_KV_RANK)),
        'mla_w_ukv': nrm(ks[13], (DEPTH, MLA_KV_RANK, MLA_HEADS * (MLA_NOPE_DIM + MLA_V_DIM)), MLA_KV_RANK ** -0.5),
        'ret_gn_gain': gain(ks[14], (DEPTH, RET_HEADS, HEAD_DIM)),
        'w_out': nrm(ks[15], (DEPTH, MIX_WIDTH, D_MODEL), MIX_WIDTH ** -0.5),
        'ln2_gain': gain(ks[16], (DEPTH, D_MODEL)),
        'w_up': nrm(ks[17], (DEPTH, D_MODEL, D_FF), D_MODEL ** -0.5),
        'w_down': nrm(ks[18], (DEPTH, D_FF, D_MODEL), D_FF ** -0.5),
        'final_gain': gain(ks[19], (D_MODEL,)),
    }

def second_block(x, positions, ln1_gain, w_in, cmp_pos_k, cmp_w1_k, cmp_w2_k, cmp_pos_v, cmp_w1_v, cmp_w2_v,
              mla_q_norm, mla_w_uq, mla_kv_norm, mla_w_ukv, ret_gn_gain, w_out, ln2_gain, w_up, w_down,
              final_gain):
    b, s, _ = x.shape
    cos_p, sin_p = rope_tables(positions, PARTIAL_ROPE_DIM, ROPE_THETA_2)
    cos_m, sin_m = rope_tables(positions, MLA_ROPE_DIM, ROPE_THETA_2)
    cos_r, sin_r = rope_tables(positions, HEAD_DIM, RET_THETA)
    offsets = in_offsets()
    for l in range(DEPTH):
        h = rms_norm_2(x, ln1_gain[l])
        proj = h @ w_in[l]
        (nsa_q, k_cmp, v_cmp, k_slc, v_slc, k_win, v_win, nsa_gate,
         mla_cq, mla_ckv, mla_kpe, ret_q, ret_k, ret_v, ret_gate) = jnp.split(proj, offsets, axis=-1)

        def kv_heads(a):
            return a.reshape(b, s, NSA_KV_GROUPS, HEAD_DIM)

        o_nsa = nsa_mixer(
            partial_rope(nsa_q.reshape(b, s, NSA_HEADS, HEAD_DIM), cos_p, sin_p),
            partial_rope(kv_heads(k_cmp), cos_p, sin_p), kv_heads(v_cmp),
            partial_rope(kv_heads(k_slc), cos_p, sin_p), kv_heads(v_slc),
            partial_rope(kv_heads(k_win), cos_p, sin_p), kv_heads(v_win),
            nsa_gate.reshape(b, s, NSA_HEADS, N_BRANCH),
            cmp_pos_k[l], cmp_w1_k[l], cmp_w2_k[l], cmp_pos_v[l], cmp_w1_v[l], cmp_w2_v[l])
        o_mla = mla_mixer(mla_cq, mla_ckv, mla_kpe, mla_q_norm[l], mla_w_uq[l], mla_kv_norm[l], mla_w_ukv[l],
                          cos_m, sin_m)
        o_ret = retention_mixer(ret_q, ret_k, ret_v, ret_gate, ret_gn_gain[l], cos_r, sin_r)
        mixed = jnp.concatenate([o_nsa.astype(x.dtype), o_mla.astype(x.dtype), o_ret.astype(x.dtype)], axis=-1)
        x = x + mixed @ w_out[l]
        h = rms_norm_2(x, ln2_gain[l])
        x = x + jnp.square(jax.nn.relu(h @ w_up[l])) @ w_down[l]
    return rms_norm_2(x, final_gain)


def setup_inputs(seed=0):
    out = dict(first_inputs(seed))
    for name, value in second_inputs(seed + 1).items():
        if name != "x":
            out[name + "_2"] = value
    return out


def reference(
    x, c, positions, w_ada, b_ada, g_norm_mix, g_norm_ffn, w_in, w_out, hgrn_lb_logits,
    hgrn_out_norm, gmlp_vnorm_g, gmlp_vnorm_b, gmlp_w_s, gmlp_b_s, ffn_w_gate, ffn_w_up,
    ffn_w_down, moe_w_router, moe_w_gate, moe_w_up, moe_w_down, g_final, positions_2,
    ln1_gain_2, w_in_2, cmp_pos_k_2, cmp_w1_k_2, cmp_w2_k_2, cmp_pos_v_2, cmp_w1_v_2,
    cmp_w2_v_2, mla_q_norm_2, mla_w_uq_2, mla_kv_norm_2, mla_w_ukv_2, ret_gn_gain_2, w_out_2,
    ln2_gain_2, w_up_2, w_down_2, final_gain_2,
):
    x = first_block(
        x, c, positions, w_ada, b_ada, g_norm_mix, g_norm_ffn, w_in, w_out, hgrn_lb_logits,
        hgrn_out_norm, gmlp_vnorm_g, gmlp_vnorm_b, gmlp_w_s, gmlp_b_s, ffn_w_gate, ffn_w_up,
        ffn_w_down, moe_w_router, moe_w_gate, moe_w_up, moe_w_down, g_final,
    )
    return second_block(
        x, positions_2, ln1_gain_2, w_in_2, cmp_pos_k_2, cmp_w1_k_2, cmp_w2_k_2, cmp_pos_v_2,
        cmp_w1_v_2, cmp_w2_v_2, mla_q_norm_2, mla_w_uq_2, mla_kv_norm_2, mla_w_ukv_2,
        ret_gn_gain_2, w_out_2, ln2_gain_2, w_up_2, w_down_2, final_gain_2,
    )


_drawn_inputs = setup_inputs


def setup_inputs(seed=0):
    import zlib

    import numpy as np

    out = dict(_drawn_inputs(seed))
    spreads = {}
    factors = {'hgrn_out_norm': 5.238,
     'gmlp_vnorm_g': 7.005,
     'gmlp_vnorm_b': 5.12,
     'gmlp_b_s': 7.888,
     'ln1_gain_2': 2.981,
     'cmp_pos_k_2': 8.0,
     'cmp_pos_v_2': 11.847,
     'mla_q_norm_2': 8.0,
     'mla_kv_norm_2': 8.0,
     'ret_gn_gain_2': 6.437,
     'ln2_gain_2': 4.414}
    for name, (base, spread) in spreads.items():
        noise = np.random.default_rng([zlib.crc32(name.encode()), seed]).standard_normal(out[name].shape)
        drawn = base * np.exp(spread * noise) if base else spread * noise
        out[name] = __import__('jax').numpy.asarray(drawn.astype(out[name].dtype))
    for name, factor in factors.items():
        out[name] = (out[name] * factor).astype(out[name].dtype)
    return out
```

```python
from contextlib import ExitStack

import numpy as np

import concourse.bass as bass
from concourse import mybir

F32 = mybir.dt.float32
I32 = mybir.dt.int32
ALU = mybir.AluOpType
ACT = mybir.ActivationFunctionType
AX = mybir.AxisListType.X

P = 128
S = 256
D = 1024
KD = D // P
DEPTH = 2
HD = 64
EPS = 1e-6
NEG = -1e30
TAKEN = -3e38
TOPK = 64
F_DENSE, F_EXPERT, D_FF, NE = 2816, 3584, 4096, 8
SLOTS, SLOT = 7, 4096
C = 16
NB = S // C
NCMP = 15


CONST = {}


def constants():
    parts = []
    eye = np.eye(P, dtype=np.float32)
    row = np.arange(P)[:, None]
    col = np.arange(P)[None, :]

    def add(name, a):
        a = np.asarray(a, np.float32)
        a = a.reshape(a.shape[0], -1)
        if a.shape[0] < P:
            a = np.concatenate([a, np.zeros((P - a.shape[0], a.shape[1]), np.float32)])
        CONST[name] = (sum(x.shape[1] for x in parts), a.shape[1])
        parts.append(a)

    add("ident", eye)
    add("ones", np.ones((P, P)))
    add("headsum", (row // HD) == (col // HD))
    tri = np.where(col <= row, 0.0, NEG)
    add("causal", np.concatenate([tri, np.zeros((P, P)), tri], 1))
    add("upper", row <= col)

    def turn(heads, at, half):
        m = np.zeros((P, P), np.float32)
        for h in heads:
            for d in range(half):
                a, b = h + at + d, h + at + half + d
                m[b, a] = -1.0
                m[a, b] = 1.0
        return m

    add("turn64", turn((0, 64), 0, 32))
    add("turn16", turn((0, 64), 0, 8))
    add("turn32", turn((0,), 64, 16))

    def rates(theta, dim, heads, at, width=P):
        v = np.zeros((P, 1), np.float32)
        inv = (np.float32(1.0) / (np.float32(theta) ** (np.arange(0, dim, 2, dtype=np.float32) / np.float32(dim)))).astype(np.float32)
        for h in heads:
            v[h + at:h + at + dim // 2, 0] = inv
            v[h + at + dim // 2:h + at + dim, 0] = inv
        return v

    add("rate64", rates(10000.0, 64, (0, 64), 0))
    add("rate16", rates(500000.0, 16, (0, 64), 0))
    add("rate32", rates(500000.0, 32, (0,), 64))
    t = np.arange(S).reshape(2, P).T[:, :, None]
    end = (np.arange(NCMP) * 16 + 31)[None, None, :]
    see = np.zeros((P, 2, 16), np.float32)
    see[:, :, :NCMP] = end <= t
    add("cmp_see", see)
    add("cmp_hide", np.where(see > 0, 0.0, NEG))
    decay = np.zeros((P, 5, 384), np.float64)
    for h in range(5):
        g = np.log(1.0 - 2.0 ** (-5.0 - h))
        j = np.arange(P)[:, None]
        i = np.arange(S)[None, :]
        decay[:, h, :S] = np.where(i >= j, np.exp(np.maximum(i - j, 0) * g), 0.0)
        decay[:, h, S:] = decay[:, h, :P]
    add("decay", decay)
    add("blocks", (np.arange(P)[:, None] // C) == np.arange(P // C)[None, :])
    add("slot_ids", np.broadcast_to(np.arange(S)[None, :], (P, S)))
    add("before", np.broadcast_to((np.arange(NE)[None, :] < np.arange(NE)[:, None]).reshape(1, -1), (P, NE * NE)))
    return np.concatenate(parts, 1).astype(np.float32)


CONSTS = constants()

VEC, VEC_LOADS = {}, []


def vector_rows():
    at = [0, 0, 0]
    for tile, name, rows in ((0, "c", 8), (0, "g_norm_mix", 16), (0, "g_norm_ffn", 16), (0, "g_final", 8),
                             (0, "ln1_gain_2", 16), (0, "ln2_gain_2", 16), (0, "final_gain_2", 8),
                             (0, "mla_q_norm_2", 4), (0, "mla_kv_norm_2", 2), (0, "hgrn_lb_logits", 6),
                             (1, "b_ada", 96), (2, "cmp_pos_k_2", 32), (2, "cmp_pos_v_2", 32)):
        VEC[name] = (tile, at[tile])
        VEC_LOADS.append((name, tile, at[tile], rows))
        at[tile] += rows
    for name, rows in (("onorm", 2), ("ret_gain", 6)):
        VEC[name] = (0, at[0])
        at[0] += rows
    assert max(at) <= P


vector_rows()


IN1 = [(0, 512), (512, 836), (836, 1220), (1220, 1604), (1604, 1988), (1988, 2372), (2372, 2884)]
IN2 = [(0, 512), (512, 1024), (1024, 1426), (1426, 1906), (1906, 2226), (2226, 2546), (2546, 2866)]


def ffn_groups(width):
    return [(f, min(512, width - f)) for f in range(0, width, 512)]


def stream_items():
    before = [("ada", 0, i) for i in range(12)]
    experts, after = [], []
    for layer in range(DEPTH):
        out = before
        out += [("in1", layer, i) for i in range(len(IN1))] + [("gmlp", layer)] + [("out1", layer, h) for h in range(2)]
        if layer == 0:
            groups = ffn_groups(F_DENSE)
            for g in range(len(groups)):
                out += [("gate", g), ("up", g)]
                if g:
                    out.append(("down", g - 1))
                out += [("ada", 1, 2 * g), ("ada", 1, 2 * g + 1)]
            out.append(("down", len(groups) - 1))
    before.append(("router",))
    n = len(ffn_groups(F_EXPERT))
    for g in range(n):
        experts += [("egate", g), ("eup", g)]
        if g:
            experts.append(("edown", g - 1))
    experts.append(("edown", n - 1))
    for layer in range(DEPTH):
        after += [("in2", layer, i) for i in range(len(IN2))]
        after += [("cmp", layer), ("mla", layer)] + [("out2", layer, h) for h in range(2)]
        n = len(ffn_groups(D_FF))
        for g in range(n):
            after.append(("mup", layer, g))
            if g:
                after.append(("mdown", layer, g - 1))
        after.append(("mdown", layer, n - 1))
    assert len(experts) % SLOTS == 0
    return before, experts, after


BEFORE, EXPERTS, AFTER = stream_items()
FIRST_EXPERT = len(BEFORE)
FIRST_AFTER = FIRST_EXPERT + NE * len(EXPERTS)
PLACE = {item: n for n, item in enumerate(BEFORE)}
PLACE.update({item: FIRST_EXPERT + n for n, item in enumerate(EXPERTS)})
PLACE.update({item: FIRST_AFTER + n for n, item in enumerate(AFTER)})


class Counts:

    def __init__(self, known):
        self.known, self.names, self.last = known, {}, {}

    def up(self, engine, *name):
        self.last[engine] = self.last.get(engine, 0) + 1
        if name:
            assert (engine, *name) not in self.names, name
            self.names[(engine, *name)] = self.last[engine]
        return 1

    def at(self, engine, *name):
        if self.known is None:
            return 1
        return self.known[(engine, *name)]

    def now(self, engine):
        return self.last[engine]


def program(nc, given, out, known, stop=None, dumps=None):
    count = Counts(known)
    up, at, now = count.up, count.at, count.now

    with ExitStack() as ctx:
        def sb(name, shape, dt=F32):
            return ctx.enter_context(nc.sbuf_tensor(name, shape, dt))

        def sem(name):
            return ctx.enter_context(nc.semaphore(name))

        ring = sb("ring", [P, SLOTS, SLOT])
        const = sb("const", list(CONSTS.shape))
        vec_rows = sb("vec_rows", [P, 3, P])
        vec = sb("vec", [P, 3, P])
        xT = sb("xT", [P, KD, S])
        hT = sb("hT", [P, KD, S])
        mixT = sb("mixT", [P, KD, S])
        cond = sb("cond", [P, KD])
        mods = sb("mods", [P, DEPTH, 48])
        gain = sb("gain", [P, 4, KD])
        lower = sb("lower", [P, DEPTH, 3])
        stat = sb("stat", [P, 128])
        table = sb("table", [P, 4, 2, S])
        SCR = sb("scratch", [P, 11264])
        acc = ctx.enter_context(nc.psum_tensor("acc", [P, 4, 512], F32))
        wrk = ctx.enter_context(nc.psum_tensor("wrk", [P, 4, 512], F32))

        def K(name):
            o, n = CONST[name]
            return const[:, o:o + n]

        def carve(tensor, offset, *shape):
            n = int(np.prod(shape))
            flat = tensor if tensor is not SCR else SCR[:, :]
            v = flat[:, offset:offset + n]
            if len(shape) == 2:
                v = v.rearrange("p (a b) -> p a b", a=shape[0])
            if len(shape) == 3:
                v = v.rearrange("p (a b c) -> p a b c", a=shape[0], b=shape[1])
            return v

        def column(name, i):
            t, r = VEC[name]
            return vec[:, t, r + i:r + i + 1]

        def columns(name, i, n):
            t, r = VEC[name]
            return vec[:, t, r + i:r + i + n]

        params_landed = sem("params_landed")
        landed = [sem(f"landed{i}") for i in range(SLOTS)]
        freed_by_pe = sem("freed_by_pe")
        freed_by_dve = sem("freed_by_dve")
        pe_done, act_done = sem("pe_done"), sem("act_done")
        dve_done, pool_done = sem("dve_done"), sem("pool_done")
        ffn_up = sem("ffn_up")
        ffn_silu = sem("ffn_silu")
        ffn_act = sem("ffn_act")
        ffn_read = sem("ffn_read")
        picked = sem("picked")
        pick_turned = sem("pick_turned")
        pick_ready = sem("pick_ready")
        gathered = sem("gathered")
        tokens_ready = sem("tokens_ready")
        rows_ready = sem("rows_ready")
        scattered = sem("scattered")
        share_added = sem("share_added")
        out_landed = sem("out_landed")

        free, counts = {}, {"pe": 0, "dve": 0, "up": 0}
        UP_TILES = sum(n // P for _, n in ffn_groups(F_EXPERT))
        FREED = sum(1 for i in EXPERTS if i[0] != "eup")

        def note(n, item):
            kind = item[0]
            if kind == "ada":
                counts["dve"] += 1
                free[n] = (freed_by_dve, counts["dve"], 0)
            elif kind in ("up", "eup", "mup"):
                width = {"up": F_DENSE, "eup": F_EXPERT, "mup": D_FF}[kind]
                counts["up"] += ffn_groups(width)[item[-1]][1] // P
                free[n] = (ffn_up, counts["up"], UP_TILES)
            else:
                counts["pe"] += 1
                free[n] = (freed_by_pe, counts["pe"], FREED)

        for n, item in enumerate(BEFORE):
            note(n, item)
        before_experts = dict(counts)
        for i, item in enumerate(EXPERTS):
            note(FIRST_EXPERT + i, item)
        assert counts["pe"] - before_experts["pe"] == FREED and counts["up"] - before_experts["up"] == UP_TILES
        counts["pe"] += FREED * (NE - 1)
        counts["up"] += UP_TILES * (NE - 1)
        for i in range(SLOTS):
            s_, v_, d_ = free[FIRST_EXPERT + len(EXPERTS) - SLOTS + i]
            free[FIRST_AFTER - SLOTS + i] = (s_, v_ + d_ * (NE - 1), 0)
        for i, item in enumerate(AFTER):
            note(FIRST_AFTER + i, item)

        def free_of(n):
            return free[n][0], free[n][1]

        def freeing(item):
            assert free[PLACE[item]][0] is freed_by_pe
            return free[PLACE[item]][1]

        def slot_of(item):
            return ring[:, PLACE[item] % SLOTS, :]

        def w_cols(item, width):
            return slot_of(item)[:, 0:KD * width].rearrange("p (k f) -> p k f", k=KD)

        def by_rows(w):
            return w.rearrange("(k p) f -> p k f", p=P)

        g = given

        def loads(item):
            kind = item[0]
            s = slot_of(item)
            if kind == "ada":
                return [(w_cols(item, 512), by_rows(g["w_ada"][item[1]])[:, :, item[2] * 512:item[2] * 512 + 512])]
            if item[0] == "in2" and item[2] == 0:
                w = by_rows(g["w_in_2"][item[1]])
                v = w_cols(item, 512)
                heads = v[:, :, 0:384].rearrange("p k (i g d) -> p k i g d", i=3, g=2)
                src = w[:, :, 0:384].rearrange("p k (g i d) -> p k i g d", i=3, g=2)
                return [(heads[:, :, i, q], src[:, :, i, q]) for i in range(3) for q in range(2)] + [(v[:, :, 384:512], w[:, :, 384:512])]
            if kind in ("in1", "in2"):
                a, b = (IN1 if kind == "in1" else IN2)[item[2]]
                w = g["w_in" if kind == "in1" else "w_in_2"][item[1]]
                return [(w_cols(item, b - a), by_rows(w)[:, :, a:b])]
            if kind in ("out1", "out2"):
                w = g["w_out" if kind == "out1" else "w_out_2"][item[1]]
                return [(w_cols(item, 512), by_rows(w)[:, :, item[2] * 512:item[2] * 512 + 512])]
            if kind in ("gate", "up"):
                f, n = ffn_groups(F_DENSE)[item[1]]
                return [(w_cols(item, n), by_rows(g["ffn_w_" + kind][0])[:, :, f:f + n])]
            if kind == "down":
                f, n = ffn_groups(F_DENSE)[item[1]]
                return [(s[:, 0:n * KD].rearrange("p (j d) -> p j d", d=D),
                         g["ffn_w_down"][0, f:f + n].rearrange("(j p) d -> p j d", p=P))]
            if kind == "mup":
                f, n = ffn_groups(D_FF)[item[2]]
                return [(w_cols(item, n), by_rows(g["w_up_2"][item[1]])[:, :, f:f + n])]
            if kind == "mdown":
                f, n = ffn_groups(D_FF)[item[2]]
                return [(s[:, 0:n * KD].rearrange("p (j d) -> p j d", d=D),
                         g["w_down_2"][item[1], f:f + n].rearrange("(j p) d -> p j d", p=P))]
            if kind == "gmlp":
                l = item[1]
                return [(s[:, 0:256], rows_of(g["gmlp_vnorm_g"], l)),
                        (s[:, 256:512], rows_of(g["gmlp_vnorm_b"], l)),
                        (s[:, 512:1024].rearrange("p (g s) -> p g s", g=4), g["gmlp_w_s"][l].rearrange("g t s -> t g s")),
                        (s[0:1, 1024:1536], g["gmlp_b_s"][l:l + 1].rearrange("a g t -> a (g t)"))]
            if kind == "router":
                return [(s[:, 0:64].rearrange("p (k e) -> p k e", k=KD), by_rows(g["moe_w_router"][0]))]
            if kind == "cmp":
                l = item[1]
                v = s.rearrange("p (a j h) -> p a j h", a=2, j=16)
                return [(v[:, 0], g["cmp_w1_k_2"][l].rearrange("(j p) h -> p j h", p=P)),
                        (v[:, 1], g["cmp_w1_v_2"][l].rearrange("(j p) h -> p j h", p=P))]
            if kind == "mla":
                l = item[1]
                return [(s[:, 0:960].rearrange("p (k f) -> p k f", k=2), by_rows(g["mla_w_uq_2"][l])),
                        (s[:, 960:1600], g["mla_w_ukv_2"][l]),
                        (s[:, 1600:1664], g["cmp_w2_k_2"][l]),
                        (s[:, 1664:1728], g["cmp_w2_v_2"][l])]
            raise KeyError(item)

        def rows_of(w, l):
            r = w[l:l + 1, :]
            return bass.AP(tensor=r.tensor, offset=r.offset, ap=[[0, P], [1, r.shape[1]]])

        land = {}
        total = [0] * SLOTS
        for n, item in enumerate(BEFORE):
            total[n % SLOTS] += 16 * len(loads(item))
            land[n] = total[n % SLOTS]
        at_experts = list(total)
        for i in range(SLOTS):
            total[i] += 16 * NE * (len(EXPERTS) // SLOTS)
        for i, item in enumerate(AFTER):
            n = FIRST_AFTER + i
            total[n % SLOTS] += 16 * len(loads(item))
            land[n] = total[n % SLOTS]

        def landing(item):
            n = PLACE[item]
            return landed[n % SLOTS], land[n]

        param_loads = []
        param_loads.append((const[:, :], g["consts"]))
        for name, t, r, rows in VEC_LOADS:
            src = g[name]
            letters = "abcd"[:len(src.shape)]
            flat = src.rearrange(f"{' '.join(letters)} -> ({' '.join(letters)})") if len(src.shape) > 1 else src
            param_loads.append((vec_rows[r:r + rows, t, :], flat.rearrange("(r p) -> r p", p=P)))
        t, r = VEC["onorm"]
        for half in range(2):
            param_loads.append((vec_rows[r:r + 2, t, half * HD:(half + 1) * HD], g["hgrn_out_norm"]))
        t, r = VEC["ret_gain"]
        for l in range(DEPTH):
            gl = g["ret_gn_gain_2"][l].rearrange("h d -> (h d)")
            param_loads.append((vec_rows[r + 3 * l:r + 3 * l + 1, t, HD:P], gl[0:HD].rearrange("(a d) -> a d", a=1)))
            param_loads.append((vec_rows[r + 3 * l + 1:r + 3 * l + 3, t, :], gl[HD:5 * HD].rearrange("(r p) -> r p", p=P)))
        xin = carve(hT[:, :, :].rearrange("p k t -> p (k t)"), 0, 2, D)
        param_loads.append((xin, g["x"][0].rearrange("(t p) d -> p t d", p=P)))
        pos = SCR[:, 0:2 * S].bitcast(I32).rearrange("p (b t) -> p b t", b=2)
        for b, name in enumerate(("positions", "positions_2")):
            r = g[name]
            param_loads.append((pos[:, b, :], bass.AP(tensor=r.tensor, offset=r.offset, ap=[[0, P], [1, S]])))
        PARAMS = 16 * len(param_loads)

        block = ctx.enter_context(nc.Block())
        stops = {}

        def body_sync(sp):
            for n, item in enumerate(BEFORE):
                if stop is not None and n >= stop[0]:
                    break
                if n >= SLOTS:
                    sp.wait_ge(*free_of(n - SLOTS))
                for place, src in loads(item):
                    sp.dma_start(place, src).then_inc(landed[n % SLOTS], 16)
            if stop is None:
                sources = {"egate": g["moe_w_gate"], "eup": g["moe_w_up"], "edown": g["moe_w_down"]}
                groups = ffn_groups(F_EXPERT)
                with sp.Fori(0, NE) as e:
                    for i, item in enumerate(EXPERTS):
                        n = FIRST_EXPERT + i
                        if i >= SLOTS:
                            s, v, d = free[n - SLOTS]
                            sp.wait_ge(s, e * d + v)
                        else:
                            s, v, d = free[n - SLOTS + len(EXPERTS)]
                            sp.wait_ge(*free_of(n - SLOTS))
                            sp.wait_ge(s, e * d + (v - d))
                        f, w = groups[item[1]]
                        src = sources[item[0]][0][e]
                        if item[0] == "edown":
                            sp.dma_start(ring[:, n % SLOTS, 0:w * KD].rearrange("p (j d) -> p j d", d=D),
                                         src[f:f + w].rearrange("(j p) d -> p j d", p=P)).then_inc(landed[n % SLOTS], 16)
                        else:
                            sp.dma_start(ring[:, n % SLOTS, 0:w * KD].rearrange("p (k f) -> p k f", k=KD),
                                         by_rows(src)[:, :, f:f + w]).then_inc(landed[n % SLOTS], 16)
                for i, item in enumerate(AFTER):
                    n = FIRST_AFTER + i
                    sp.wait_ge(*free_of(n - SLOTS))
                    for place, src in loads(item):
                        sp.dma_start(place, src).then_inc(landed[n % SLOTS], 16)

        accv = acc[:, :, :].rearrange("p b (h t) -> p (b h) t", t=S)
        T0, T1 = slice(0, P), slice(P, S)
        ident, ones, headsum = K("ident"), K("ones"), K("headsum")
        rstd = mixT[:, 0, :]

        def settle(eng, name, s):
            eng.wait_ge(s, now(name))

        ang = carve(SCR, 512, 4, S)
        turns = carve(SCR, 512 + 1024, 4, S)
        fpos = carve(SCR, 512 + 2048, 2, S)
        TWO_PI_PARTS = (6.28125, 0.0019340515136718750, 2 * np.pi - 6.28125 - 0.0019340515136718750)
        ROUND = 12582912.0

        def start_act(act):
            act.wait_ge(dve_done, at("dve", "rows cleared"))
            for place, src in param_loads:
                act.dma_start(place, src).then_inc(params_landed, 16)
            act.wait_ge(pe_done, at("pe", "x turned"))
            act.activation(xT[:, 0:4, :], accv[:, 0:4, :], ACT.Copy).then_inc(act_done, up("act"))
            act.activation(xT[:, 4:8, :], accv[:, 4:8, :], ACT.Copy).then_inc(act_done, up("act", "x"))
            act.wait_ge(dve_done, at("dve", "vec"))
            act.activation(cond[:, :], columns("c", 0, 8), ACT.Silu).then_inc(act_done, up("act", "cond"))
            act.wait_ge(dve_done, at("dve", "lower in"))
            act.activation(stat[:, 3:9], stat[:, 3:9], ACT.Exp).then_inc(act_done, up("act", "lower exp"))
            act.wait_ge(dve_done, at("dve", "angles"))
            act.activation(table[:, :, 1, :], ang, ACT.Sin).then_inc(act_done, up("act"))
            act.activation(table[:, :, 0, :], turns, ACT.Sin).then_inc(act_done, up("act", "tables"))

        def start_pe(pe):
            pe.wait_ge(params_landed, PARAMS)
            for t in range(3):
                mm = pe.transpose(wrk[:, 0, t * P:(t + 1) * P], vec_rows[:, t, :], ident)
            mm.then_inc(pe_done, up("pe", "vec"))
            for k in range(KD):
                for t in range(2):
                    mm = pe.transpose(accv[:, k, t * P:(t + 1) * P], xin[:, t, k * P:(k + 1) * P], ident)
            mm.then_inc(pe_done, up("pe", "x turned"))

        def start_dve(dve):
            dve.memset(vec_rows[:, :, :], 0.0).then_inc(dve_done, up("dve", "rows cleared"))
            dve.wait_ge(pe_done, at("pe", "vec"))
            dve.tensor_copy(vec[:, :, :].rearrange("p a b -> p (a b)"), wrk[:, 0, 0:3 * P]).then_inc(dve_done, up("dve", "vec"))
            settle(dve, "dve", dve_done)
            a0, a1 = columns("hgrn_lb_logits", 0, 3), columns("hgrn_lb_logits", 3, 3)
            dve.tensor_tensor(stat[:, 0:3], a0, a1, ALU.max).then_inc(dve_done, up("dve"))
            settle(dve, "dve", dve_done)
            dve.tensor_tensor(stat[:, 3:6], a0, stat[:, 0:3], ALU.subtract).then_inc(dve_done, up("dve"))
            dve.tensor_tensor(stat[:, 6:9], a1, stat[:, 0:3], ALU.subtract).then_inc(dve_done, up("dve", "lower in"))
            dve.wait_ge(act_done, at("act", "lower exp"))
            dve.tensor_tensor(stat[:, 9:12], stat[:, 3:6], stat[:, 6:9], ALU.add).then_inc(dve_done, up("dve"))
            settle(dve, "dve", dve_done)
            dve.reciprocal(stat[:, 12:15], stat[:, 9:12]).then_inc(dve_done, up("dve"))
            settle(dve, "dve", dve_done)
            dve.tensor_tensor(stat[:, 15:18], stat[:, 3:6], stat[:, 12:15], ALU.mult).then_inc(dve_done, up("dve"))
            dve.tensor_tensor(stat[:, 18:21], stat[:, 6:9], stat[:, 12:15], ALU.mult).then_inc(dve_done, up("dve"))
            settle(dve, "dve", dve_done)
            dve.tensor_tensor(stat[:, 21:24], stat[:, 15:18], stat[:, 18:21], ALU.add).then_inc(dve_done, up("dve"))
            dve.tensor_tensor(lower[:, 0, :], stat[:, 15:18], stat[:, 15:18], ALU.subtract).then_inc(dve_done, up("dve"))
            settle(dve, "dve", dve_done)
            dve.tensor_tensor(lower[:, 1, :], stat[:, 21:24], stat[:, 15:18], ALU.subtract).then_inc(dve_done, up("dve", "lower"))
            dve.tensor_copy(fpos, pos).then_inc(dve_done, up("dve"))
            settle(dve, "dve", dve_done)
            for i, (b, rate) in enumerate(((0, "rate64"), (1, "rate64"), (1, "rate16"), (1, "rate32"))):
                dve.tensor_scalar(ang[:, i, :], fpos[:, b, :], K(rate), None, ALU.mult).then_inc(dve_done, up("dve"))
            settle(dve, "dve", dve_done)
            dve.tensor_scalar(turns, ang, float(1 / (2 * np.pi)), ROUND, ALU.mult, ALU.add).then_inc(dve_done, up("dve"))
            settle(dve, "dve", dve_done)
            dve.tensor_scalar(turns, turns, ROUND, None, ALU.subtract).then_inc(dve_done, up("dve"))
            for part in TWO_PI_PARTS:
                settle(dve, "dve", dve_done)
                for i in range(4):
                    dve.scalar_tensor_tensor(ang[:, i, :], turns[:, i, :], -float(part), ang[:, i, :], ALU.mult, ALU.add)\
                       .then_inc(dve_done, up("dve"))
            settle(dve, "dve", dve_done)
            dve.tensor_scalar(ang, ang, 3.1415925, -3.1415925, ALU.min, ALU.max).then_inc(dve_done, up("dve"))
            settle(dve, "dve", dve_done)
            dve.scalar_tensor_tensor(turns, ang, -1.0, ang, ALU.mult, ALU.max).then_inc(dve_done, up("dve"))
            settle(dve, "dve", dve_done)
            dve.tensor_scalar(turns, turns, -1.0, float(np.pi / 2), ALU.mult, ALU.add).then_inc(dve_done, up("dve", "angles"))

        part_sum = [SCR[:, 10240 + 512 * i:10240 + 512 * (i + 1)] for i in range(2)]

        def ada_dve(dve, l, i):
            item = ("ada", l, i)
            w = w_cols(item, 512)
            dve.wait_ge(*landing(item))
            if l == 0 and i == 0:
                dve.wait_ge(act_done, at("act", "cond"))
                dve.wait_ge(act_done, at("act", "tables"))
            n = 12 * l + i
            if n >= 2:
                dve.wait_ge(pe_done, at("pe", "ada", n - 2))
            dst = part_sum[n % 2]
            for k in range(KD):
                if k == 0:
                    ins = dve.tensor_scalar(dst, w[:, k, :], cond[:, k:k + 1], None, ALU.mult)
                else:
                    settle(dve, "dve", dve_done)
                    ins = dve.scalar_tensor_tensor(dst, w[:, k, :], cond[:, k:k + 1], dst, ALU.mult, ALU.add)
                if k < KD - 1:
                    ins.then_inc(dve_done, up("dve"))
                else:
                    ins.then_inc(freed_by_dve, 1)

        def ada_pe(pe, l, i):
            n = 12 * l + i
            pe.wait_ge(freed_by_dve, n + 1)
            for j in range(4):
                mm = pe.matmul(wrk[:, 3, 4 * i + j:4 * i + j + 1], part_sum[n % 2][:, j * P:(j + 1) * P], ones[:, 0:1],
                               start=True, stop=True)
            mm.then_inc(pe_done, up("pe", "ada", n))

        def ada_end_dve(dve, l):
            dve.wait_ge(pe_done, at("pe", "ada", 12 * l + 11))
            dve.tensor_tensor(mods[:, l, :], wrk[:, 3, 0:48], columns("b_ada", 48 * l, 48), ALU.add)\
               .then_inc(dve_done, up("dve"))
            settle(dve, "dve", dve_done)
            for j, (sc, name) in enumerate(((8, "g_norm_mix"), (32, "g_norm_ffn"))):
                dve.scalar_tensor_tensor(gain[:, 2 * l + j, :], mods[:, l, sc:sc + 8], 1.0, columns(name, 8 * l, 8),
                                         ALU.add, ALU.mult).then_inc(dve_done, up("dve", "gain", l, j))

        def norm_act(act, tag, wait_x, scale_of, shift_of, place=None):
            place = hT if place is None else place
            for s, v in wait_x:
                act.wait_ge(s, v)
            act.activation(hT[:, :, :], xT[:, :, :], ACT.Square).then_inc(act_done, up("act", "squares", tag))
            root_act(act, at("dve", "mean square", tag), ("root", tag), rstd)
            act.wait_ge(dve_done, at("dve", "scaled", tag))
            for k in range(KD):
                act.activation(place[:, k, :], hT[:, k, :], ACT.Identity, scale=scale_of(k),
                               bias=shift_of(k) if shift_of else 0.0).then_inc(act_done, up("act", "h", tag, k))

        def norm_pe(pe, tag):
            pe.wait_ge(act_done, at("act", "squares", tag))
            for k in range(KD):
                mm = pe.matmul(wrk[:, 3, 0:S], ones, hT[:, k, :], start=(k == 0), stop=(k == KD - 1))
            mm.then_inc(pe_done, up("pe", "sum of squares", tag))

        def norm_dve(dve, tag):
            dve.wait_ge(pe_done, at("pe", "sum of squares", tag))
            dve.tensor_scalar(rstd, wrk[:, 3, 0:S], 1.0 / D, EPS, ALU.mult, ALU.add).then_inc(dve_done, up("dve", "mean square", tag))
            inverse_root_dve(dve, ("root", tag), rstd)
            settle(dve, "dve", dve_done)
            dve.tensor_tensor(hT[:, :, :], xT[:, :, :], rstd.unsqueeze(1).broadcast_to([P, KD, S]), ALU.mult)\
               .then_inc(dve_done, up("dve", "scaled", tag))

        def root_act(act, wait, name, place):
            act.wait_ge(dve_done, wait)
            act.activation(place, place, ACT.Sqrt).then_inc(act_done, up("act", *name))

        def inverse_root_dve(dve, name, place):
            dve.wait_ge(act_done, at("act", *name))
            dve.reciprocal(place, place).then_inc(dve_done, up("dve"))

        def project_pe(pe, tag, plan, wait_first):
            last_item = None
            for s, v in wait_first:
                pe.wait_ge(s, v)
            for i, (name, item, mode, cols, m, p0, places) in enumerate(plan):
                if item != last_item:
                    pe.wait_ge(*landing(item))
                    last_item = item
                if i >= 4:
                    pe.wait_ge(act_done, at("act", "proj", tag, plan[i - 4][0]))
                ends = i + 1 == len(plan) or plan[i + 1][1] != item
                for k in range(KD):
                    if mode == "f":
                        mm = pe.matmul(wrk[p0:p0 + m, i % 4, 0:S], cols(k), hT[:, k, :], start=(k == 0), stop=(k == KD - 1))
                    else:
                        t = T0 if mode == "t0" else T1
                        mm = pe.matmul(wrk[:, i % 4, 0:m], hT[:, k, t], cols(k), start=(k == 0), stop=(k == KD - 1))
                if ends:
                    mm.then_inc(freed_by_pe, 1)
                else:
                    mm.then_inc(pe_done, up("pe", "proj", tag, name))

        def project_act(act, tag, plan):
            for i, (name, item, mode, cols, m, p0, places) in enumerate(plan):
                if i + 1 == len(plan) or plan[i + 1][1] != item:
                    act.wait_ge(freed_by_pe, freeing(item))
                else:
                    act.wait_ge(pe_done, at("pe", "proj", tag, name))
                n = S if mode == "f" else m
                lo, hi = (p0, p0 + m) if mode == "f" else (0, P)
                for j, (place, func, scale) in enumerate(places):
                    src = wrk[lo:hi, i % 4, 0:n]
                    ins = act.activation(place, src, func, scale=scale)
                    ins.then_inc(act_done, up("act", "proj", tag, name) if j == len(places) - 1 else up("act"))

        rope_tmp = [SCR[:, 10240 + 256 * i:10240 + 256 * (i + 1)] for i in range(4)]

        def rope_pe(pe, tag, plan, wait_names):
            for i, (name, tile, turn, tab, p0, rows) in enumerate(plan):
                pe.wait_ge(act_done, wait_names(name))
                if i >= 4:
                    pe.wait_ge(dve_done, at("dve", "rope", tag, plan[i - 4][0]))
                pe.matmul(acc[p0:p0 + rows, i % 4, 0:S], K(turn)[p0:p0 + rows, p0:p0 + rows], tile, start=True, stop=True)\
                  .then_inc(pe_done, up("pe", "rope", tag, name))

        def rope_dve(dve, tag, plan, wait_names):
            for i, (name, tile, turn, tab, p0, rows) in enumerate(plan):
                a, b = rope_tmp[2 * (i % 2)][p0:p0 + rows], rope_tmp[2 * (i % 2) + 1][p0:p0 + rows]
                dve.wait_ge(act_done, wait_names(name))
                if i >= 2:
                    dve.wait_ge(dve_done, at("dve", "rope", tag, plan[i - 2][0]))
                dve.tensor_tensor(a, tile, table[p0:p0 + rows, tab, 0, :], ALU.mult).then_inc(dve_done, up("dve"))
                dve.wait_ge(pe_done, at("pe", "rope", tag, name))
                dve.tensor_tensor(b, acc[p0:p0 + rows, i % 4, 0:S], table[p0:p0 + rows, tab, 1, :], ALU.mult)\
                   .then_inc(dve_done, up("dve"))
                settle(dve, "dve", dve_done)
                dve.tensor_tensor(tile, a, b, ALU.add).then_inc(dve_done, up("dve", "rope", tag, name))

        def outproj_pe(pe, tag, items, waits):
            for s, v in waits:
                pe.wait_ge(s, v)
            for h, item in enumerate(items):
                w = w_cols(item, 512)
                pe.wait_ge(*landing(item))
                for m in range(4):
                    for k in range(KD):
                        mm = pe.matmul(accv[:, 4 * h + m, :], w[:, k, m * P:(m + 1) * P], mixT[:, k, :],
                                       start=(k == 0), stop=(k == KD - 1))
                    if m < 3:
                        mm.then_inc(pe_done, up("pe", "out", tag, 4 * h + m))
                mm.then_inc(freed_by_pe, 1)

        def residual_dve(dve, tag, gate_of, waits):
            for m in range(KD):
                dve.wait_ge(*waits[m])
                if gate_of is None:
                    ins = dve.tensor_tensor(xT[:, m, :], accv[:, m, :], xT[:, m, :], ALU.add)
                else:
                    ins = dve.scalar_tensor_tensor(xT[:, m, :], accv[:, m, :], gate_of(m), xT[:, m, :], ALU.mult, ALU.add)
                ins.then_inc(dve_done, up("dve", "residual", tag, m))

        def out_waits(tag, items):
            return [(freed_by_pe, freeing(items[m // 4])) if m % 4 >= 2 else (pe_done, at("pe", "out", tag, m | 1))
                    for m in range(KD)]

        AT = 8448
        a_score = [carve(SCR, AT + 384 * i, 384) for i in range(2)]
        a_prob = [carve(SCR, AT + 768 + 384 * i, 384) for i in range(2)]
        a_probT = [carve(SCR, AT + 1536 + 384 * i, 384) for i in range(2)]

        def a_stat(u, what):
            return stat[:, 32 + 8 * (u % 4) + 2 * what:32 + 8 * (u % 4) + 2 * what + 2]

        def spans(kind):
            return ((0, 15), (16, 31)) if kind == "cmp" else ((0, P), (P, 384))

        def att_scores_pe(pe, tag, u, b):
            for s, v in b["ready"]:
                pe.wait_ge(s, v)
            if u >= 2:
                pe.wait_ge(dve_done, at("dve", "masked", tag, u - 2))
            for t, (lo, hi) in enumerate(spans(b["kind"])):
                mm = pe.matmul(wrk[:, u % 2, lo:hi], b["q"][:, t * P:(t + 1) * P], b["k"][:, 0:hi - lo], start=True, stop=True)
            mm.then_inc(pe_done, up("pe", "scores", tag, u))

        def att_turn_pe(pe, tag, u, b):
            pe.wait_ge(dve_done, at("dve", "probs", tag, u))
            if u >= 2:
                pe.wait_ge(act_done, at("act", "probT", tag, u - 2))
            if b["kind"] == "cmp":
                for t, (lo, hi) in enumerate(spans("cmp")):
                    mm = pe.transpose(wrk[0:15, 2 + u % 2, t * P:(t + 1) * P], a_prob[u % 2][:, lo:hi], ident)
            else:
                for j in range(3):
                    mm = pe.transpose(wrk[:, 2 + u % 2, j * P:(j + 1) * P], a_prob[u % 2][:, j * P:(j + 1) * P], ident)
            mm.then_inc(pe_done, up("pe", "turned", tag, u))

        def att_value_pe(pe, tag, u, b, head):
            pe.wait_ge(act_done, at("act", "probT", tag, u))
            if b["first"] and head >= 4:
                pe.wait_ge(dve_done, at("dve", "head out", tag, head - 4))
            p0 = b["p0"]
            o = acc[p0:p0 + HD, head % 4, 0:S]
            if b["kind"] == "cmp":
                mm = pe.matmul(o, b["v"](0), a_probT[u % 2][0:15, 0:S], start=b["first"], stop=b["last"], skip_group_check=True)
            else:
                pe.matmul(o, b["v"](0), a_probT[u % 2][:, 0:S], start=b["first"], stop=False, skip_group_check=True)
                mm = pe.matmul(acc[p0:p0 + HD, head % 4, P:S], b["v"](1), a_probT[u % 2][:, S:S + P],
                               start=False, stop=b["last"], skip_group_check=True)
            mm.then_inc(pe_done, up("pe", "value", tag, u))

        def att_pe(pe, tag, branches):
            att_scores_pe(pe, tag, 0, branches[0])
            heads = head_numbers(branches)
            for u in range(len(branches) + 1):
                if u + 1 < len(branches):
                    att_scores_pe(pe, tag, u + 1, branches[u + 1])
                if u < len(branches):
                    att_turn_pe(pe, tag, u, branches[u])
                if u >= 1:
                    att_value_pe(pe, tag, u - 1, branches[u - 1], heads[u - 1])

        def head_numbers(branches):
            n, outs = -1, []
            for b in branches:
                n += b["first"]
                outs.append(n)
            return outs

        def att_dve(dve, tag, branches):
            heads = head_numbers(branches)

            def masked(u, b):
                dve.wait_ge(pe_done, at("pe", "scores", tag, u))
                for s, v in b["mask_ready"]:
                    dve.wait_ge(s, v)
                if u >= 2:
                    dve.wait_ge(act_done, at("act", "exp", tag, u - 2))
                for t, (lo, hi) in enumerate(spans(b["kind"])):
                    dve.tensor_tensor_reduce(out=a_score[u % 2][:, lo:hi], in0=wrk[:, u % 2, lo:hi], in1=b["mask"][:, lo:hi],
                                             scale=b["scale"], scalar=3 * NEG, op0=ALU.add, op1=ALU.max,
                                             accum_out=a_stat(u, 0)[:, t:t + 1]).then_inc(dve_done, up("dve"))
                settle(dve, "dve", dve_done)
                dve.tensor_scalar(a_stat(u, 1), a_stat(u, 0), -1.0, None, ALU.mult).then_inc(dve_done, up("dve", "masked", tag, u))

            def probs(u, b):
                dve.wait_ge(act_done, at("act", "exp", tag, u))
                if b["kind"] == "cmp":
                    for t, (lo, hi) in enumerate(spans("cmp")):
                        dve.tensor_tensor_reduce(out=a_prob[u % 2][:, lo:hi], in0=a_prob[u % 2][:, lo:hi],
                                                 in1=K("cmp_see")[:, lo:hi], scale=1.0, scalar=0.0, op0=ALU.mult, op1=ALU.add,
                                                 accum_out=a_stat(u, 2)[:, t:t + 1]).then_inc(dve_done, up("dve"))
                    settle(dve, "dve", dve_done)
                    dve.tensor_scalar(a_stat(u, 2), a_stat(u, 2), 1e-30, None, ALU.max).then_inc(dve_done, up("dve"))
                    settle(dve, "dve", dve_done)
                dve.reciprocal(a_stat(u, 3), a_stat(u, 2)).then_inc(dve_done, up("dve"))
                settle(dve, "dve", dve_done)
                for t, (lo, hi) in enumerate(spans(b["kind"])):
                    if b["gate"] is None:
                        ins = dve.tensor_scalar(a_prob[u % 2][:, lo:hi], a_prob[u % 2][:, lo:hi], a_stat(u, 3)[:, t:t + 1],
                                                None, ALU.mult)
                    else:
                        ins = dve.tensor_scalar(a_prob[u % 2][:, lo:hi], a_prob[u % 2][:, lo:hi], a_stat(u, 3)[:, t:t + 1],
                                                b["gate"](t), ALU.mult, ALU.mult)
                    ins.then_inc(dve_done, up("dve", "probs", tag, u) if t else up("dve"))

            masked(0, branches[0])
            for u, b in enumerate(branches):
                if u + 1 < len(branches):
                    masked(u + 1, branches[u + 1])
                probs(u, b)
                if u >= 1 and branches[u - 1]["last"]:
                    head_out(dve, tag, u - 1, branches[u - 1], heads[u - 1])
            head_out(dve, tag, len(branches) - 1, branches[-1], heads[-1])

        def head_out(dve, tag, u, b, head):
            dve.wait_ge(pe_done, at("pe", "value", tag, u))
            dve.tensor_copy(b["place"], acc[b["p0"]:b["p0"] + HD, head % 4, 0:S]).then_inc(dve_done, up("dve", "head out", tag, head))

        def att_act(act, tag, branches):
            def exps(u, b):
                act.wait_ge(dve_done, at("dve", "masked", tag, u))
                if u >= 2:
                    act.wait_ge(pe_done, at("pe", "turned", tag, u - 2))
                for t, (lo, hi) in enumerate(spans(b["kind"])):
                    act.activation(a_prob[u % 2][:, lo:hi], a_score[u % 2][:, lo:hi], ACT.Exp, bias=a_stat(u, 1)[:, t:t + 1],
                                   accum_out=a_stat(u, 2)[:, t:t + 1])\
                       .then_inc(act_done, up("act", "exp", tag, u) if t else up("act"))

            exps(0, branches[0])
            for u, b in enumerate(branches):
                if u + 1 < len(branches):
                    exps(u + 1, branches[u + 1])
                act.wait_ge(pe_done, at("pe", "turned", tag, u))
                if u >= 2:
                    act.wait_ge(pe_done, at("pe", "value", tag, u - 2))
                if b["kind"] == "cmp":
                    ins = act.activation(a_probT[u % 2][0:15, 0:S], wrk[0:15, 2 + u % 2, 0:S], ACT.Copy)
                else:
                    ins = act.activation(a_probT[u % 2], wrk[:, 2 + u % 2, 0:384], ACT.Copy)
                ins.then_inc(act_done, up("act", "probT", tag, u))

        Z = lambda o, *shape: carve(SCR, o, *shape)
        b_q, b_kk, b_f, b_g = Z(0, 3, S), Z(768, 3, S), Z(1536, 3, S), Z(2304, 3, S)
        b_i, c_u, c_v = Z(3072, 2, 384), Z(3840, 2, S), Z(4352, 2, S)
        s_q, s_k, s_iq, s_ik = Z(4864, 3, S), Z(5632, 1, S), Z(5888, 2, S), Z(6400, 1, S)
        s_v, s_iw = Z(6656, 2, HD), Z(6784, 2, 4)
        s_mask, s_work = Z(6800, 384), Z(7184, 384)
        s_relu = [Z(7568, 384), Z(7952, 384)]

        def plan1(l):
            items = [("in1", l, i) for i in range(len(IN1))]
            w = [w_cols(items[i], b - a) for i, (a, b) in enumerate(IN1)]

            def cols(i, c, n):
                return lambda k: w[i][:, k, c:c + n]

            def both(tile, scale=1.0):
                return [(tile[HD * p:HD * p + HD, 0, :], ACT.Copy, scale) for p in range(2)]

            plan = [(f"aq{j}", items[0], "f", cols(0, P * j, P), P, 0, [(s_q[:, j, :], ACT.Copy, 1.0)]) for j in range(3)]
            plan += [("ak", items[0], "f", cols(0, 384, HD), HD, 0, both(s_k))]
            plan += [(f"av{t}", items[0], f"t{t}", cols(0, 448, HD), HD, 0, [(s_v[:, t, :], ACT.Copy, 1.0)]) for t in range(2)]
            plan += [(f"iq{j}", items[1], "f", cols(1, P * j, P), P, 0, [(s_iq[:, j, :], ACT.Copy, 1.0)]) for j in range(2)]
            plan += [("ik", items[1], "f", cols(1, 256, HD), HD, 0, both(s_ik))]
            plan += [(f"iw{t}", items[1], f"t{t}", cols(1, 320, 4), 4, 0, [(s_iw[:, t, :], ACT.Copy, 0.5)]) for t in range(2)]
            plan += [(f"bq{j}", items[2], "f", cols(2, P * j, P), P, 0, [(b_q[:, j, :], ACT.Copy, 1.0)]) for j in range(3)]
            plan += [(f"bf{j}", items[3], "f", cols(3, P * j, P), P, 0,
                      [(b_f[:, j, :], ACT.Sigmoid, 1.0), (b_kk[:, j, :], ACT.Sigmoid, -1.0)]) for j in range(3)]
            plan += [(f"bi{t}", items[4], f"t{t}", cols(4, 0, 384), 384, 0, [(b_i[:, t, :], ACT.Copy, 1.0)]) for t in range(2)]
            plan += [(f"bg{j}", items[5], "f", cols(5, P * j, P), P, 0, [(b_g[:, j, :], ACT.Silu, 1.0)]) for j in range(3)]
            plan += [(f"cu{j}", items[6], "f", cols(6, P * j, P), P, 0, [(c_u[:, j, :], ACT.Gelu, 1.0)]) for j in range(2)]
            plan += [(f"cv{t}", items[6], f"t{t}", cols(6, 256, 256), 256, 0, [(c_v[:, t, :], ACT.Gelu, 1.0)]) for t in range(2)]
            return plan

        def rope1(l):
            tiles = [("iq0", s_iq[:, 0, :]), ("iq1", s_iq[:, 1, :]), ("ik", s_ik[:, 0, :])]
            tiles += [(f"aq{j}", s_q[:, j, :]) for j in range(3)] + [("ak", s_k[:, 0, :])]
            return [(name, tile, "turn64", 0, 0, P) for name, tile in tiles]

        def index_pe(pe, l):
            pe.wait_ge(act_done, at("act", "proj", ("1", l), "cv1"))
            for h in range(4):
                pe.wait_ge(dve_done, at("dve", "rope", ("1", l), "ik"))
                p0 = HD * (h % 2)
                q, k = s_iq[p0:p0 + HD, h // 2, :], s_ik[p0:p0 + HD, 0, :]
                pe.matmul(wrk[:, h, 0:P], q[:, T0], k[:, T0], start=True, stop=True)
                pe.matmul(wrk[:, h, P:384], q[:, T1], k[:, 0:S], start=True, stop=True)\
                  .then_inc(pe_done, up("pe", "index", l, h))

        def index_act(act, l):
            for h in range(4):
                act.wait_ge(pe_done, at("pe", "index", l, h))
                if h >= 2:
                    act.wait_ge(dve_done, at("dve", "index", l, h - 2))
                act.activation(s_relu[h % 2], wrk[:, h, 0:384], ACT.Relu, scale=IDX_SCALE).then_inc(act_done, up("act", "index", l, h))

        IDX_SCALE = float(HD) ** -0.5
        QT = ((0, P), (P, 384))

        def index_dve(dve, l):
            for h in range(4):
                dve.wait_ge(act_done, at("act", "index", l, h))
                for t, (lo, hi) in enumerate(QT):
                    if h == 0:
                        ins = dve.tensor_scalar(s_work[:, lo:hi], s_relu[0][:, lo:hi], s_iw[:, t, 0:1], None, ALU.mult)
                    else:
                        ins = dve.scalar_tensor_tensor(s_work[:, lo:hi], s_relu[h % 2][:, lo:hi], s_iw[:, t, h:h + 1],
                                                       s_work[:, lo:hi], ALU.mult, ALU.add)
                    ins.then_inc(dve_done, up("dve", "index", l, h) if t else up("dve"))
                settle(dve, "dve", dve_done)
            dve.tensor_tensor(s_work, s_work, K("causal"), ALU.add).then_inc(dve_done, up("dve"))
            for _ in range(TOPK // 8):
                settle(dve, "dve", dve_done)
                for t, (lo, hi) in enumerate(QT):
                    dve.max(stat[:, 8 * t:8 * t + 8], s_work[:, lo:hi]).then_inc(dve_done, up("dve"))
                settle(dve, "dve", dve_done)
                for t, (lo, hi) in enumerate(QT):
                    dve.match_replace(s_work[:, lo:hi], stat[:, 8 * t:8 * t + 8], s_work[:, lo:hi], TAKEN)\
                       .then_inc(dve_done, up("dve"))
            settle(dve, "dve", dve_done)
            dve.tensor_scalar(s_mask, s_work, TAKEN / 2, NEG, ALU.is_gt, ALU.mult).then_inc(dve_done, up("dve"))
            settle(dve, "dve", dve_done)
            dve.tensor_tensor(s_mask, s_mask, K("causal"), ALU.add).then_inc(dve_done, up("dve", "mask", l))

        def branches1(l):
            out = []
            for h in range(6):
                p0, j = HD * (h % 2), h // 2
                out.append(dict(q=s_q[p0:p0 + HD, j, :], k=s_k[p0:p0 + HD, 0, :], v=lambda t: s_v[:, t, :], mask=s_mask,
                                kind="causal", scale=float(HD) ** -0.5, gate=None, first=True, last=True, p0=p0,
                                place=mixT[p0:p0 + HD, j, :],
                                ready=[(dve_done, at("dve", "rope", ("1", l), "ak")), (act_done, at("act", "index", l, 3))] if h == 0 else [],
                                mask_ready=[(dve_done, at("dve", "mask", l))] if h == 0 else []))
            return out

        def gmlp_parts(l):
            s = slot_of(("gmlp", l))
            return (s[:, 0:256], s[:, 256:512], s[:, 512:1024].rearrange("p (g s) -> p g s", g=4), s[0:1, 1024:1536],
                    s[:, 1536:2048].rearrange("p (g t) -> p g t", g=4))

        def gmlp_pe(pe, l):
            g_row, b_row, ws, bs, wsT = gmlp_parts(l)
            pe.wait_ge(*landing(("gmlp", l)))
            pe.wait_ge(act_done, now_act_read(l))
            for i in range(4):
                mm = pe.transpose(wrk[:, 0, i * P:(i + 1) * P], ws[:, i, :], ident)
            mm.then_inc(pe_done, up("pe", "ws turned", l))
            pe.wait_ge(dve_done, at("dve", "wsT", l))
            pe.wait_ge(dve_done, at("dve", "cv", l))
            for j in range(2):
                for p in range(2):
                    i, p0 = 2 * j + p, HD * p
                    for n in range(2):
                        o = acc[p0:p0 + HD, j, n * P:(n + 1) * P]
                        pe.matmul(o, c_v[:, n, i * HD:(i + 1) * HD], wsT[:, i, :], start=True, stop=False, skip_group_check=True)
                        mm = pe.matmul(o, ones[0:1, 0:HD], bs[:, i * P:(i + 1) * P], start=False, stop=True, skip_group_check=True)
                if j == 0:
                    mm.then_inc(pe_done, up("pe", "mixed", l, j))
                else:
                    mm.then_inc(freed_by_pe, 1)

        def now_act_read(l):
            return at("act", "probT", ("1", l), 5)

        def gmlp_dve(dve, l):
            g_row, b_row, ws, bs, wsT = gmlp_parts(l)
            dve.wait_ge(act_done, at("act", "proj", ("1", l), "cv1"))
            for t in range(2):
                dve.bn_stats(stat[:, 8 * t:8 * t + 6], c_v[:, t, :]).then_inc(dve_done, up("dve"))
            settle(dve, "dve", dve_done)
            for t in range(2):
                dve.bn_aggr(stat[:, 16 + 2 * t:18 + 2 * t], stat[:, 8 * t:8 * t + 6]).then_inc(dve_done, up("dve"))
            settle(dve, "dve", dve_done)
            for t in range(2):
                dve.tensor_scalar(stat[:, 20 + t:21 + t], stat[:, 17 + 2 * t:18 + 2 * t], EPS, None, ALU.add)\
                   .then_inc(dve_done, up("dve", "cv variance", l) if t else up("dve"))
            inverse_root_dve(dve, ("cv root", l), stat[:, 20:22])
            settle(dve, "dve", dve_done)
            for t in range(2):
                dve.tensor_scalar(c_v[:, t, :], c_v[:, t, :], stat[:, 16 + 2 * t:17 + 2 * t], stat[:, 20 + t:21 + t],
                                  ALU.subtract, ALU.mult).then_inc(dve_done, up("dve"))
            dve.wait_ge(*landing(("gmlp", l)))
            settle(dve, "dve", dve_done)
            dve.tensor_tensor(c_v, c_v, g_row.unsqueeze(1).broadcast_to([P, 2, S]), ALU.mult).then_inc(dve_done, up("dve"))
            settle(dve, "dve", dve_done)
            dve.tensor_tensor(c_v, c_v, b_row.unsqueeze(1).broadcast_to([P, 2, S]), ALU.add).then_inc(dve_done, up("dve", "cv", l))
            dve.wait_ge(pe_done, at("pe", "ws turned", l))
            dve.tensor_tensor(wsT, wrk[:, 0, :].rearrange("p (g t) -> p g t", g=4),
                              K("upper").unsqueeze(1).broadcast_to([P, 4, P]), ALU.mult).then_inc(dve_done, up("dve", "wsT", l))
            for j in range(2):
                if j == 0:
                    dve.wait_ge(pe_done, at("pe", "mixed", l, 0))
                else:
                    dve.wait_ge(freed_by_pe, freeing(("gmlp", l)))
                dve.tensor_tensor(mixT[:, 6 + j, :], acc[:, j, 0:S], c_u[:, j, :], ALU.mult).then_inc(dve_done, up("dve", "c out", l, j))

        def grid(v):
            return v.rearrange("p a (b c) -> p (a b) c", c=C)

        NP3 = 3 * NB
        r_w = [b_kk, Z(4864, 3, S)]
        r_kdec, r_v = Z(5632, 3, S), Z(6400, 3, S)
        r_qw = [Z(7168, 768), Z(10240, 768)]
        r_t, r_p, r_o = Z(7936, 3, S), Z(8704, 3, S), Z(9472, 3, S)
        r_state = Z(4864, 3, NB * HD).rearrange("p a (b v) -> p a b v", v=HD)
        r_kT = Z(7936, 6, P)
        r_pick = [Z(512 * i, P // C, HD) for i in range(3)]
        r_whole = stat[:, 64:64 + NP3]

        def band(j):
            n = C - j
            return n, r_qw[j % 2][:, 0:NP3 * n].rearrange("p (a c) -> p a c", c=n)

        def band_psum(j, half):
            n = C - j
            return wrk[:, 2 * (j % 2) + half, 0:24 * n]

        def hgrn_pe(pe, l):
            pe.wait_ge(act_done, at("act", "proj", ("1", l), "bi1"))
            pe.wait_ge(dve_done, at("dve", "c out", l, 1))
            for a in range(3):
                for t in range(2):
                    mm = pe.transpose(accv[:, a, t * P:(t + 1) * P], b_i[:, t, a * P:(a + 1) * P], ident)
            mm.then_inc(pe_done, up("pe", "v turned", l))
            for j in range(C):
                n, qw = band(j)
                pe.wait_ge(dve_done, at("dve", "qw", l, j))
                if j >= 2:
                    pe.wait_ge(dve_done, at("dve", "band", l, j - 2))
                for half in range(2):
                    mm = pe.matmul(band_psum(j, half), headsum, r_qw[j % 2][:, 24 * n * half:24 * n * (half + 1)],
                                   start=True, stop=True)
                mm.then_inc(pe_done, up("pe", "band", l, j))
            pe.wait_ge(act_done, at("act", "v", l))
            pe.wait_ge(act_done, at("act", "kdec", l))
            for a in range(3):
                for t in range(2):
                    mm = pe.transpose(accv[:, a, t * P:(t + 1) * P], r_kdec[:, a, t * P:(t + 1) * P], ident)
            mm.then_inc(pe_done, up("pe", "k turned", l))
            pe.wait_ge(act_done, at("act", "kT", l))
            pe.wait_ge(dve_done, at("dve", "band", l, C - 1))
            n = 0
            for a in range(3):
                for h in range(2):
                    for t in range(2):
                        o = wrk[HD * h:HD * h + HD, 2 * a + t, :] if a < 2 else acc[HD * h:HD * h + HD, 2 + t, :]
                        pe.wait_ge(dve_done, at("dve", "pick", l, n))
                        pe.matmul(o, r_kT[:, 2 * a + t, HD * h:HD * h + HD], r_pick[n % 3].rearrange("p b v -> p (b v)"),
                                  start=True, stop=True).then_inc(pe_done, up("pe", "kv", l, n))
                        n += 1
            for a in range(3):
                pe.wait_ge(dve_done, at("dve", "states", l, a))
                for b in range(NB):
                    for h in range(2):
                        rows = slice(HD * h, HD * h + HD)
                        mm = pe.matmul(acc[rows, a // 2, S * (a % 2) + b * C:S * (a % 2) + (b + 1) * C], r_state[rows, a, b, :],
                                       r_p[rows, a, b * C:(b + 1) * C], start=True, stop=True, skip_group_check=True)
                mm.then_inc(pe_done, up("pe", "inter", l, a))
            pe.wait_ge(act_done, at("act", "o squares", l))
            for half in range(2):
                mm = pe.matmul(wrk[:, half, 0:384], headsum, r_qw[1][:, 384 * half:384 * (half + 1)], start=True, stop=True)
            mm.then_inc(pe_done, up("pe", "o sums", l))

        def hgrn_act(act, l):
            act.wait_ge(pe_done, at("pe", "v turned", l))
            act.activation(r_v, accv[:, 0:3, :], ACT.Copy).then_inc(act_done, up("act", "v", l))
            for j in range(C):
                act.wait_ge(dve_done, at("dve", "w", l, j))
                act.activation(grid(r_kdec)[:, :, C - 1 - j:C - j], grid(r_w[j % 2])[:, :, C - 1:C], ACT.Copy)\
                   .then_inc(act_done, up("act", "kdec", l) if j == C - 1 else up("act", "kdec part", l, j))
            act.wait_ge(pe_done, at("pe", "k turned", l))
            act.wait_ge(dve_done, at("dve", "band end", l))
            act.activation(r_kT.rearrange("p (a t) d -> p a (t d)", t=2), accv[:, 0:3, :], ACT.Copy).then_inc(act_done, up("act", "kT", l))
            act.wait_ge(dve_done, at("dve", "o", l))
            act.activation(r_qw[1], r_o.rearrange("p a t -> p (a t)"), ACT.Square).then_inc(act_done, up("act", "o squares", l))
            root_act(act, at("dve", "o mean square", l), ("o root", l), r_t)

        def hgrn_dve(dve, l):
            dve.tensor_scalar(stat[:, 24:27], lower[:, l, :], -1.0, 1.0, ALU.mult, ALU.add).then_inc(dve_done, up("dve"))
            settle(dve, "dve", dve_done)
            for a in range(3):
                dve.wait_ge(act_done, at("act", "proj", ("1", l), f"bf{a}"))
                dve.tensor_scalar(b_f[:, a, :], b_f[:, a, :], stat[:, 24 + a:25 + a], lower[:, l, a:a + 1], ALU.mult, ALU.add)\
                   .then_inc(dve_done, up("dve"))
                dve.tensor_scalar(b_kk[:, a, :], b_kk[:, a, :], stat[:, 24 + a:25 + a], None, ALU.mult)\
                   .then_inc(dve_done, up("dve", "w", l, 0) if a == 2 else up("dve"))
            settle(dve, "dve", dve_done)
            f, q, p, v = grid(b_f), grid(b_q), grid(r_p), grid(r_v)
            dve.tensor_copy(p[:, :, 0:1], f[:, :, 0:1]).then_inc(dve_done, up("dve"))

            def weigh(j):
                n, qw = band(j)
                if j:
                    settle(dve, "dve", dve_done)
                    if j >= 2:
                        dve.wait_ge(act_done, at("act", "kdec part", l, j - 2))
                    dve.tensor_tensor(grid(r_w[j % 2])[:, :, j:C], grid(r_w[(j - 1) % 2])[:, :, j - 1:C - 1], f[:, :, j:C], ALU.mult)\
                       .then_inc(dve_done, up("dve", "w", l, j))
                    dve.tensor_tensor(p[:, :, j:j + 1], p[:, :, j - 1:j], f[:, :, j:j + 1], ALU.mult).then_inc(dve_done, up("dve"))
                    settle(dve, "dve", dve_done)
                if j >= 2:
                    dve.wait_ge(pe_done, at("pe", "band", l, j - 2))
                dve.tensor_tensor(qw, q[:, :, j:C], grid(r_w[j % 2])[:, :, j:C], ALU.mult).then_inc(dve_done, up("dve", "qw", l, j))

            weigh(0)
            dve.wait_ge(act_done, at("act", "v", l))
            for j in range(C):
                if j + 1 < C:
                    weigh(j + 1)
                dve.wait_ge(pe_done, at("pe", "band", l, j))
                n = C - j
                o = grid(r_o if j == 0 else r_t)[:, :, j:C]
                for half in range(2):
                    dve.tensor_tensor(o[:, 24 * half:24 * half + 24, :], band_psum(j, half).rearrange("p (a c) -> p a c", c=n),
                                      v[:, 24 * half:24 * half + 24, 0:n], ALU.mult)\
                       .then_inc(dve_done, up("dve", "band", l, j) if half else up("dve"))
                if j:
                    settle(dve, "dve", dve_done)
                    dve.tensor_tensor(grid(r_o)[:, :, j:C], grid(r_o)[:, :, j:C], o, ALU.add)\
                       .then_inc(dve_done, up("dve", "band end", l) if j == C - 1 else up("dve"))
                settle(dve, "dve", dve_done)
            dve.tensor_copy(r_whole, p[:, :, C - 1:C].rearrange("p a c -> p (a c)")).then_inc(dve_done, up("dve"))
            settle(dve, "dve", dve_done)
            dve.tensor_tensor(r_p, r_p, b_q, ALU.mult).then_inc(dve_done, up("dve"))
            settle(dve, "dve", dve_done)
            dve.wait_ge(act_done, at("act", "kdec", l))
            n = 0
            for a in range(3):
                for h in range(2):
                    for t in range(2):
                        if n >= 3:
                            dve.wait_ge(pe_done, at("pe", "kv", l, n - 3))
                        dve.tensor_tensor(r_pick[n % 3], K("blocks").unsqueeze(2).broadcast_to([P, P // C, HD]),
                                          b_i[:, t, (2 * a + h) * HD:(2 * a + h + 1) * HD].unsqueeze(1).broadcast_to([P, P // C, HD]),
                                          ALU.mult).then_inc(dve_done, up("dve", "pick", l, n))
                        n += 1
            dve.wait_ge(pe_done, at("pe", "k turned", l))
            dve.memset(r_state[:, :, 0, :], 0.0).then_inc(dve_done, up("dve"))
            dve.wait_ge(pe_done, at("pe", "kv", l, 11))
            for a in range(3):
                for b in range(1, NB):
                    bank = wrk[:, 2 * a + (b - 1) // 8, :] if a < 2 else acc[:, 2 + (b - 1) // 8, :]
                    c = (b - 1) % 8
                    settle(dve, "dve", dve_done)
                    dve.scalar_tensor_tensor(r_state[:, a, b, :], r_state[:, a, b - 1, :], r_whole[:, a * NB + b - 1:a * NB + b],
                                             bank[:, c * HD:(c + 1) * HD], ALU.mult, ALU.add)\
                       .then_inc(dve_done, up("dve", "states", l, a) if b == NB - 1 else up("dve"))
            for a in range(3):
                dve.wait_ge(pe_done, at("pe", "inter", l, max(a, 1)))
                dve.tensor_tensor(r_o[:, a, :], r_o[:, a, :], accv[:, a, :], ALU.add)\
                   .then_inc(dve_done, up("dve", "o", l) if a == 2 else up("dve"))
            dve.wait_ge(pe_done, at("pe", "o sums", l))
            rt = r_t.rearrange("p a t -> p (a t)").rearrange("p (h n) -> p h n", h=2)
            dve.tensor_scalar(rt, wrk[:, 0:2, 0:384], 1.0 / HD, EPS, ALU.mult, ALU.add).then_inc(dve_done, up("dve", "o mean square", l))
            inverse_root_dve(dve, ("o root", l), r_t)
            settle(dve, "dve", dve_done)
            dve.tensor_tensor(r_o, r_o, r_t, ALU.mult).then_inc(dve_done, up("dve"))
            settle(dve, "dve", dve_done)
            dve.scalar_tensor_tensor(mixT[:, 3:6, :], r_o, column("onorm", l), b_g, ALU.mult, ALU.mult)\
               .then_inc(dve_done, up("dve", "b out", l))

        F_ACT = Z(0, 8, S)
        F_SIL = Z(2048, 4, S)
        def tile_base(kind, l):
            return {"dense": 0, "moe": F_DENSE // P, "mlp": F_DENSE // P + NE * UP_TILES + l * (D_FF // P)}[kind]

        def group_base(kind, l):
            n_d, n_e, n_m = (len(ffn_groups(w)) for w in (F_DENSE, F_EXPERT, D_FF))
            return {"dense": 0, "moe": n_d, "mlp": n_d + NE * n_e + l * n_m}[kind]

        def dense_items(g):
            return ("gate", g), ("up", g), ("down", g)

        def ffn_up_pe(pe, g, width, items, base, gbase):
            f, n = ffn_groups(width)[g]
            gate, up_ = items
            for j in range(n // P):
                i = base + 4 * g + j
                if i >= 3:
                    pe.wait_ge(ffn_act, i - 2)
                for item, lo in ((gate, 0), (up_, S)):
                    if item is None:
                        continue
                    if j == 0:
                        pe.wait_ge(*landing(item))
                    w = w_cols(item, n)
                    for k in range(KD):
                        mm = pe.matmul(wrk[:, i % 3, lo:lo + S], w[:, k, j * P:(j + 1) * P], hT[:, k, :],
                                       start=(k == 0), stop=(k == KD - 1))
                    if item is gate and j == n // P - 1:
                        mm.then_inc(freed_by_pe, 1)
                mm.then_inc(ffn_up, 1)

        def ffn_down_pe(pe, g, width, item, base, gbase, tag):
            groups = ffn_groups(width)
            f, n = groups[g]
            w = slot_of(item)[:, 0:n * KD].rearrange("p (j d) -> p j d", d=D)
            pe.wait_ge(*landing(item))
            pe.wait_ge(ffn_act, base + 4 * g + n // P)
            for m in range(KD):
                for j in range(n // P):
                    mm = pe.matmul(accv[:, m, :], w[:, j, m * P:(m + 1) * P], F_ACT[:, 4 * (g % 2) + j, :],
                                   start=(g == 0 and j == 0 and m % 2 == 0), stop=(g == len(groups) - 1 and j == n // P - 1),
                                   skip_group_check=True)
            mm.then_inc(freed_by_pe, 1)

        def dense_pe(pe):
            n = len(ffn_groups(F_DENSE))
            pe.wait_ge(act_done, at("act", "h", ("ffn", 0), KD - 1))
            for g in range(n + 1):
                if g < n:
                    ffn_up_pe(pe, g, F_DENSE, dense_items(g)[:2], 0, 0)
                if g >= 1:
                    ffn_down_pe(pe, g - 1, F_DENSE, dense_items(g - 1)[2], 0, 0, "dense")
                if g < n:
                    for i in (2 * g, 2 * g + 1):
                        ada_pe(pe, 1, i)

        def dense_act(act):
            for i in range(F_DENSE // P):
                act.wait_ge(ffn_up, i + 1)
                if i >= 4:
                    act.wait_ge(ffn_act, i - 3)
                act.activation(F_SIL[:, i % 4, :], wrk[:, i % 3, 0:S], ACT.Silu).then_inc(ffn_silu, 1)

        def dense_dve(dve):
            groups = ffn_groups(F_DENSE)
            for g, (f, n) in enumerate(groups):
                if g >= 2:
                    dve.wait_ge(freed_by_pe, freeing(("down", g - 2)))
                for j in range(n // P):
                    i = 4 * g + j
                    dve.wait_ge(ffn_silu, i + 1)
                    dve.tensor_tensor(F_ACT[:, 4 * (g % 2) + j, :], F_SIL[:, i % 4, :], wrk[:, i % 3, S:2 * S], ALU.mult)\
                       .then_inc(ffn_act, 1)
                for i in (2 * g, 2 * g + 1):
                    ada_dve(dve, 1, i)
            ada_end_dve(dve, 1)
            dve.wait_ge(freed_by_pe, freeing(("down", len(groups) - 1)))
            for m in range(KD):
                dve.scalar_tensor_tensor(xT[:, m, :], accv[:, m, :], mods[:, 0, 40 + m:41 + m], xT[:, m, :], ALU.mult, ALU.add)\
                   .then_inc(dve_done, up("dve", "residual", ("ffn", 0), m))

        def out_items(kind, l):
            return [(kind, l, 0), (kind, l, 1)]

        def mod_col(l, o):
            return lambda k: mods[:, l, o + k:o + k + 1]

        def gain_col(i):
            return lambda k: gain[:, i, k:k + 1]

        def x_ready(l):
            if l == 0:
                return [(act_done, at("act", "x")), (dve_done, at("dve", "gain", 0, 1))]
            return [(dve_done, at("dve", "residual", ("ffn", 0), KD - 1)), (dve_done, at("dve", "gain", 1, 1))]

        def act_from(wait_names):
            return lambda name: at("act", "proj", wait_names, name)

        def block1_pe(pe, l):
            tag = ("1", l)
            norm_pe(pe, ("mix", l))
            project_pe(pe, tag, plan1(l), [(act_done, at("act", "h", ("mix", l), KD - 1))])
            rope_pe(pe, tag, rope1(l), act_from(tag))
            index_pe(pe, l)
            att_pe(pe, tag, branches1(l))
            gmlp_pe(pe, l)
            hgrn_pe(pe, l)
            outproj_pe(pe, tag, out_items("out1", l), [(dve_done, at("dve", "b out", l))])
            norm_pe(pe, ("ffn", l))

        def block1_act(act, l):
            tag = ("1", l)
            norm_act(act, ("mix", l), x_ready(l), gain_col(2 * l), mod_col(l, 0))
            project_act(act, tag, plan1(l))
            index_act(act, l)
            att_act(act, tag, branches1(l))
            root_act(act, at("dve", "cv variance", l), ("cv root", l), stat[:, 20:22])
            hgrn_act(act, l)
            norm_act(act, ("ffn", l), [(dve_done, at("dve", "residual", ("mix", l), KD - 1))], gain_col(2 * l + 1), mod_col(l, 24))

        def block1_dve(dve, l):
            tag = ("1", l)
            norm_dve(dve, ("mix", l))
            rope_dve(dve, tag, rope1(l), act_from(tag))
            index_dve(dve, l)
            att_dve(dve, tag, branches1(l))
            gmlp_dve(dve, l)
            hgrn_dve(dve, l)
            residual_dve(dve, ("mix", l), mod_col(l, 16), out_waits(tag, out_items("out1", l)))
            norm_dve(dve, ("ffn", l))


        m_h = Z(3072, 2, D)
        m_rows = Z(5120, 2, D)
        m_pick, m_wpick, m_wpickT = Z(7168, 2, S), Z(7680, 2, S), Z(8192, 2, S)
        m_logit, m_gate, m_pos, m_sel = (Z(8704 + 16 * i, 2, NE) for i in range(4))
        m_cmp = [Z(8800 + 64 * i, NE, NE) for i in range(4)]
        m_part = Z(9072, 2, 4)
        m_many = sb("m_many", [1, NE], I32)
        y_sum = mixT
        MOE = tile_base("moe", 0)
        flat_mix = mixT[:, :, :].rearrange("p k t -> p (k t)")
        flat_acc = acc[:, :, :].rearrange("p b n -> p (b n)")

        def route_pe(pe):
            pe.wait_ge(act_done, at("act", "h", ("ffn", 1), KD - 1))
            pe.wait_ge(*landing(("router",)))
            wr = slot_of(("router",))[:, 0:64].rearrange("p (k e) -> p k e", k=KD)
            for t in range(2):
                for k in range(KD):
                    mm = pe.matmul(wrk[:, 3, t * NE:(t + 1) * NE], hT[:, k, t * P:(t + 1) * P], wr[:, k, :],
                                   start=(k == 0), stop=(k == KD - 1))
            mm.then_inc(freed_by_pe, 1)
            for t in range(2):
                for k in range(KD):
                    mm = pe.transpose(flat_acc[:, t * D + k * P:t * D + (k + 1) * P], hT[:, k, t * P:(t + 1) * P], ident)
            mm.then_inc(pe_done, up("pe", "h turned"))
            pe.wait_ge(dve_done, at("dve", "selected"))
            pe.matmul(wrk[:, 2, 0:NE], K("upper"), m_sel[:, 0, :], start=True, stop=True)
            pe.matmul(wrk[:, 2, NE:2 * NE], ones, m_sel[:, 0, :], start=True, stop=False)
            pe.matmul(wrk[:, 2, NE:2 * NE], K("upper"), m_sel[:, 1, :], start=False, stop=True)
            pe.matmul(wrk[0:1, 2, 2 * NE:3 * NE], ones[:, 0:1], m_sel[:, 0, :], start=True, stop=False)
            pe.matmul(wrk[0:1, 2, 2 * NE:3 * NE], ones[:, 0:1], m_sel[:, 1, :], start=False, stop=True).then_inc(pe_done, up("pe", "counted"))

        def route_act(act):
            act.wait_ge(pe_done, at("pe", "h turned"))
            act.activation(m_h.rearrange("p t d -> p (t d)"), flat_acc, ACT.Copy).then_inc(act_done, up("act", "h tokens"))
            act.wait_ge(dve_done, at("dve", "logits less max"))
            act.activation(m_gate, m_gate, ACT.Exp).then_inc(act_done, up("act", "router exp"))

        def route_dve(dve):
            dve.wait_ge(freed_by_pe, freeing(("router",)))
            dve.tensor_copy(m_logit, wrk[:, 3, 0:2 * NE].rearrange("p (t e) -> p t e", t=2)).then_inc(dve_done, up("dve"))
            settle(dve, "dve", dve_done)
            for t in range(2):
                own = m_logit[:, t, :].unsqueeze(2).broadcast_to([P, NE, NE])
                other = m_logit[:, t, :].unsqueeze(1).broadcast_to([P, NE, NE])
                dve.tensor_tensor(m_cmp[t], other, own, ALU.is_gt).then_inc(dve_done, up("dve"))
                dve.tensor_tensor(m_cmp[2 + t], other, own, ALU.is_equal).then_inc(dve_done, up("dve"))
            settle(dve, "dve", dve_done)
            for t in range(2):
                dve.tensor_tensor(m_cmp[2 + t], m_cmp[2 + t], K("before").rearrange("p (a b) -> p a b", a=NE), ALU.mult)\
                   .then_inc(dve_done, up("dve"))
            settle(dve, "dve", dve_done)
            for t in range(2):
                dve.tensor_tensor(m_cmp[t], m_cmp[t], m_cmp[2 + t], ALU.add).then_inc(dve_done, up("dve"))
                dve.tensor_reduce(m_part[:, t, 0:1], m_logit[:, t, :], AX, ALU.max).then_inc(dve_done, up("dve"))
            settle(dve, "dve", dve_done)
            for t in range(2):
                dve.tensor_reduce(m_sel[:, t, :], m_cmp[t], AX, ALU.add).then_inc(dve_done, up("dve"))
                dve.tensor_scalar(m_gate[:, t, :], m_logit[:, t, :], m_part[:, t, 0:1], None, ALU.subtract)\
                   .then_inc(dve_done, up("dve", "logits less max") if t else up("dve"))
            settle(dve, "dve", dve_done)
            dve.tensor_scalar(m_sel, m_sel, 1.5, None, ALU.is_lt).then_inc(dve_done, up("dve", "selected"))
            dve.wait_ge(act_done, at("act", "router exp"))
            settle(dve, "dve", dve_done)
            dve.tensor_tensor(m_gate, m_gate, m_sel, ALU.mult).then_inc(dve_done, up("dve"))
            settle(dve, "dve", dve_done)
            dve.tensor_reduce(m_part[:, :, 1:2].rearrange("p a b -> p (a b)"), m_gate, AX, ALU.add).then_inc(dve_done, up("dve"))
            settle(dve, "dve", dve_done)
            dve.reciprocal(m_part[:, :, 2:3], m_part[:, :, 1:2]).then_inc(dve_done, up("dve"))
            settle(dve, "dve", dve_done)
            for t in range(2):
                dve.tensor_scalar(m_gate[:, t, :], m_gate[:, t, :], m_part[:, t, 2:3], None, ALU.mult).then_inc(dve_done, up("dve"))
            dve.wait_ge(pe_done, at("pe", "counted"))
            dve.tensor_tensor(m_pos, wrk[:, 2, 0:2 * NE].rearrange("p (t e) -> p t e", t=2), m_sel, ALU.mult).then_inc(dve_done, up("dve"))
            dve.tensor_scalar(m_many[:, :], wrk[0:1, 2, 2 * NE:3 * NE], P + 0.5, None, ALU.is_gt).then_inc(dve_done, up("dve"))
            settle(dve, "dve", dve_done)
            dve.tensor_scalar(m_pos, m_pos, -1.0, None, ALU.add).then_inc(dve_done, up("dve", "routed"))
            dve.memset(mixT[:, :, :], 0.0).then_inc(share_added, 1)

        def by_count(eng, e, body):
            many = eng.value_load(m_many[0:1, bass.ds(e, 1)], min_val=0, max_val=1)
            with eng.If(many == 0):
                body(e, 1)
            with eng.Else():
                body(e, 2)

        def experts_pe(pe):
            groups = ffn_groups(F_EXPERT)
            base = MOE

            def arrive(e, item):
                n = PLACE[item]
                mine = (n - FIRST_EXPERT) // SLOTS + 1
                pe.wait_ge(landed[n % SLOTS], e * (16 * (len(EXPERTS) // SLOTS)) + (at_experts[n % SLOTS] + 16 * mine))

            def rise(e, g, width):
                for j in range(4):
                    i = base + 4 * g + j
                    pe.wait_ge(ffn_act, e * UP_TILES + (i - 3))
                    for item, lo in ((("egate", g), 0), (("eup", g), S)):
                        if j == 0:
                            arrive(e, item)
                        w = w_cols(item, 512)
                        for k in range(KD):
                            mm = pe.matmul(wrk[:, j, lo:lo + width], w[:, k, j * P:(j + 1) * P], hT[:, k, 0:width],
                                           start=(k == 0), stop=(k == KD - 1))
                        if lo == 0 and j == 3:
                            mm.then_inc(freed_by_pe, 1)
                    mm.then_inc(ffn_up, 1)

            def fall(e, g, blocks):
                arrive(e, ("edown", g))
                w = slot_of(("edown", g)).rearrange("p (j d) -> p j d", d=D)
                pe.wait_ge(ffn_act, e * UP_TILES + (base + 4 * g + 4))
                for b in range(blocks):
                    for n in range(2):
                        for j in range(4):
                            mm = pe.matmul(acc[:, 2 * b + n, :], F_ACT[:, 4 * (g % 2) + j, b * P:(b + 1) * P],
                                           w[:, j, n * 512:(n + 1) * 512], start=(g == 0 and j == 0),
                                           stop=(g == len(groups) - 1 and j == 3), skip_group_check=True)
                mm.then_inc(freed_by_pe, 1)

            def expert(e, blocks):
                width = blocks * P
                pe.wait_ge(picked, e * 4 + 4)
                for b in range(blocks):
                    for t in range(2):
                        mm = pe.transpose(wrk[:, 3, b * S + t * P:b * S + (t + 1) * P], m_wpick[:, t, b * P:(b + 1) * P], ident)
                mm.then_inc(pick_turned, 1)
                pe.wait_ge(share_added, e + 1)
                for k in range(KD):
                    for t in range(2):
                        mm = pe.matmul(accv[:, k, 0:width], m_h[:, t, k * P:(k + 1) * P], m_pick[:, t, 0:width],
                                       start=(t == 0), stop=(t == 1))
                mm.then_inc(gathered, 1)
                pe.wait_ge(tokens_ready, e + 1)
                pe.wait_ge(pick_ready, e + 1)
                for g in range(len(groups) + 1):
                    if g < len(groups):
                        rise(e, g, width)
                    if g >= 1:
                        fall(e, g - 1, blocks)
                pe.wait_ge(rows_ready, e + 1)
                for k in range(KD):
                    for b in range(blocks):
                        mm = pe.matmul(accv[:, k, :], m_rows[:, b, k * P:(k + 1) * P], m_wpickT[:, b, :],
                                       start=(b == 0), stop=(b == blocks - 1))
                mm.then_inc(scattered, 1)

            pe.wait_ge(act_done, at("act", "h tokens"))
            pe.wait_ge(dve_done, at("dve", "routed"))
            with pe.Fori(0, NE) as e:
                by_count(pe, e, expert)

        def experts_act(act):
            n = len(ffn_groups(F_EXPERT))

            def expert(e, blocks):
                width = blocks * P
                act.wait_ge(pick_turned, e + 1)
                act.activation(m_wpickT[:, 0:blocks, :].rearrange("p b t -> p (b t)"), wrk[:, 3, 0:blocks * S], ACT.Copy)\
                   .then_inc(pick_ready, 1)
                act.wait_ge(gathered, e + 1)
                act.activation(hT[:, :, 0:width], accv[:, :, 0:width], ACT.Copy).then_inc(tokens_ready, 1)
                for i in range(UP_TILES):
                    act.wait_ge(ffn_up, e * UP_TILES + (MOE + i + 1))
                    act.wait_ge(ffn_act, e * UP_TILES + (MOE + i - 3))
                    act.activation(F_SIL[:, i % 4, 0:width], wrk[:, i % 4, 0:width], ACT.Silu).then_inc(ffn_silu, 1)
                act.wait_ge(freed_by_pe, e * FREED + freeing(("edown", n - 1)))
                act.activation(m_rows[:, 0:blocks, :].rearrange("p b d -> p (b d)"), flat_acc[:, 0:blocks * D], ACT.Copy)\
                   .then_inc(rows_ready, 1)

            act.wait_ge(dve_done, at("dve", "routed"))
            with act.Fori(0, NE) as e:
                by_count(act, e, expert)

        def experts_dve(dve):
            def expert(e, blocks):
                width = blocks * P
                for t in range(2):
                    dve.tensor_scalar(m_pick[:, t, 0:width], K("slot_ids")[:, 0:width], m_pos[:, t, bass.ds(e, 1)], None, ALU.is_equal)\
                       .then_inc(picked, 1)
                    dve.tensor_scalar(m_wpick[:, t, 0:width], K("slot_ids")[:, 0:width], m_pos[:, t, bass.ds(e, 1)],
                                      m_gate[:, t, bass.ds(e, 1)], ALU.is_equal, ALU.mult).then_inc(picked, 1)
                for i in range(UP_TILES):
                    g, j = i // 4, i % 4
                    if j == 0 and g >= 2:
                        dve.wait_ge(freed_by_pe, e * FREED + freeing(("edown", g - 2)))
                    dve.wait_ge(ffn_silu, e * UP_TILES + (MOE + i + 1))
                    dve.tensor_tensor(F_ACT[:, 4 * (g % 2) + j, 0:width], F_SIL[:, j, 0:width], wrk[:, j, S:S + width], ALU.mult)\
                       .then_inc(ffn_act, 1)
                dve.wait_ge(scattered, e + 1)
                dve.tensor_tensor(y_sum[:, :, :], accv, y_sum[:, :, :], ALU.add).then_inc(share_added, 1)

            settle(dve, "dve", dve_done)
            dve.wait_ge(share_added, 1)
            with dve.Fori(0, NE) as e:
                by_count(dve, e, expert)

        def experts_end_dve(dve):
            dve.wait_ge(share_added, NE + 1)
            for m in range(KD):
                dve.scalar_tensor_tensor(xT[:, m, :], y_sum[:, m, :], mods[:, 1, 40 + m:41 + m], xT[:, m, :], ALU.mult, ALU.add)\
                   .then_inc(dve_done, up("dve", "residual", ("ffn", 1), m))

        n_q, n_ks, n_kw, n_kc, n_vc = Z(0, 3, S), Z(768, 1, S), Z(1024, 1, S), Z(1280, 1, S), Z(1536, 1, S)
        n_vs, n_vw, n_gate = Z(1792, 2, P), Z(2048, 2, P), Z(2304, 2, 18)
        l_cq, l_ckv, l_kpe = Z(2344, 2, S), Z(2856, 1, S), Z(3112, 1, S)
        l_q = Z(3368, 5, S)
        t_q, t_k, t_g, t_v = Z(4648, 3, S), Z(5416, 3, S), Z(6184, 3, S), Z(6952, 2, 320)
        n_hid, n_kcT, n_vcT = Z(7592, 2, 32), Z(7656, 16), Z(7672, P)
        l_tmp = Z(7800, 640)
        n_blk = Z(8448, 2, 16, 30)
        flat_h = hT[:, :, :].rearrange("p k t -> p (k t)")
        l_k = flat_h[:, 0:1280].rearrange("p (h t) -> p h t", h=5)
        l_v = flat_h[:, 1280:1920].rearrange("p (t n) -> p t n", t=2)

        def plan2(l):
            items = [("in2", l, i) for i in range(len(IN2))]
            w = [w_cols(items[i], b - a) for i, (a, b) in enumerate(IN2)]

            def cols(i, c, n):
                return lambda k: w[i][:, k, c:c + n]

            def tile(name, i, c, place, func=ACT.Copy, scale=1.0, m=P, p0=0):
                return (name, items[i], "f", cols(i, c, m), m, p0, [(place[p0:p0 + m], func, scale)])

            def rows(name, i, c, n, place, func=ACT.Copy):
                return [(f"{name}{t}", items[i], f"t{t}", cols(i, c, n), n, 0, [(place[:, t, 0:n], func, 1.0)]) for t in range(2)]

            def heads5(name, i, c, place, func=ACT.Copy, scale=1.0):
                return [tile(name + "0", i, c, place[:, 0, :], func, scale, HD, HD),
                        tile(name + "1", i, c + HD, place[:, 1, :], func, scale),
                        tile(name + "2", i, c + HD + P, place[:, 2, :], func, scale)]

            plan = [tile(f"nq{j}", 0, P * j, n_q[:, j, :]) for j in range(3)] + [tile("nkc", 0, 384, n_kc[:, 0, :])]
            plan += [tile("nvc", 1, 0, n_vc[:, 0, :]), tile("nks", 1, 128, n_ks[:, 0, :])]
            plan += rows("nvs", 1, 256, P, n_vs) + [tile("nkw", 1, 384, n_kw[:, 0, :])]
            plan += rows("nvw", 2, 0, P, n_vw) + rows("ng", 2, 128, 18, n_gate, ACT.Sigmoid)
            plan += [tile(f"cq{j}", 2, 146 + P * j, l_cq[:, j, :]) for j in range(2)]
            plan += [tile("ckv", 3, 0, l_ckv[:, 0, :]), tile("kpe", 3, 128, l_kpe[:, 0, :], m=32, p0=64)]
            plan += heads5("rq", 3, 160, t_q) + heads5("rk", 4, 0, t_k, ACT.Copy, float(HD) ** -0.5)
            plan += rows("rv", 5, 0, 320, t_v) + heads5("rg", 6, 0, t_g, ACT.Silu)
            return plan

        def rope2(l):
            plan = [("nkc", n_kc[:, 0, :], "turn16", 2, 0, P), ("nks", n_ks[:, 0, :], "turn16", 2, 0, P),
                    ("nkw", n_kw[:, 0, :], "turn16", 2, 0, P)]
            plan += [(f"nq{j}", n_q[:, j, :], "turn16", 2, 0, P) for j in range(3)]
            plan += [("kpe", l_kpe[64:96, 0, :], "turn32", 3, 64, 32)]
            for n, z in (("rq", t_q), ("rk", t_k)):
                plan += [(n + "0", z[HD:P, 0, :], "turn64", 1, HD, HD)]
                plan += [(f"{n}{j}", z[:, j, :], "turn64", 1, 0, P) for j in (1, 2)]
            return plan

        def rope_mla(l):
            return [(f"mq{h}", l_q[0:96, h, :], "turn32", 3, 0, 96) for h in range(5)]

        def cmp_act(act, l):
            act.wait_ge(dve_done, at("dve", "rope", ("2", l), "nkc"))
            for a, src in enumerate((n_kc, n_vc)):
                for g_ in range(2):
                    v = src[HD * g_:HD * g_ + HD, 0, :].rearrange("p (c b) -> p b c", b=16)
                    for par in range(2):
                        for later in range(2):
                            act.activation(n_blk[HD * par:HD * par + HD, a, 8 * later:8 * later + 8, 15 * g_:15 * g_ + 15],
                                           v[:, par:16:2, later:later + 15], ACT.Copy)\
                               .then_inc(act_done, up("act", "blocks", l) if (a, g_, par, later) == (1, 1, 1, 1) else up("act"))
            act.wait_ge(pe_done, at("pe", "hidden", l))
            act.activation(n_hid[:, :, 0:30], wrk[:, 0, 0:64].rearrange("p (a n) -> p a n", a=2)[:, :, 0:30], ACT.Gelu_apprx_tanh)\
               .then_inc(act_done, up("act", "hidden", l))
            act.wait_ge(freed_by_pe, freeing(("cmp", l)))
            act.activation(n_kcT[:, 0:15], wrk[:, 1, 0:15], ACT.Copy).then_inc(act_done, up("act"))
            act.activation(n_vcT[0:15, :], wrk[0:15, 2, 0:P], ACT.Copy).then_inc(act_done, up("act", "compressed", l))

        def cmp_dve(dve, l):
            dve.wait_ge(act_done, at("act", "blocks", l))
            for a, name in enumerate(("cmp_pos_k_2", "cmp_pos_v_2")):
                dve.tensor_tensor(n_blk[:, a], n_blk[:, a], columns(name, 16 * l, 16).unsqueeze(2).broadcast_to([P, 16, 30]), ALU.add)\
                   .then_inc(dve_done, up("dve", "blocks", l) if a else up("dve"))

        def cmp_pe(pe, l):
            w1 = slot_of(("cmp", l)).rearrange("p (a j h) -> p a j h", a=2, j=16)
            w2 = slot_of(("mla", l))[:, 1600:1728]
            pe.wait_ge(*landing(("cmp", l)))
            pe.wait_ge(dve_done, at("dve", "blocks", l))
            for a in range(2):
                for j in range(16):
                    mm = pe.matmul(wrk[:, 0, 32 * a:32 * a + 30], w1[:, a, j, :], n_blk[:, a, j, :], start=(j == 0), stop=(j == 15))
            mm.then_inc(pe_done, up("pe", "hidden", l))
            pe.wait_ge(*landing(("mla", l)))
            pe.wait_ge(act_done, at("act", "hidden", l))
            for g_ in range(2):
                mm = pe.matmul(wrk[HD * g_:HD * g_ + HD, 1, 0:15], w2[:, 0:HD], n_hid[:, 0, 15 * g_:15 * g_ + 15], start=True, stop=True)
            for g_ in range(2):
                mm = pe.matmul(wrk[0:15, 2, HD * g_:HD * g_ + HD], n_hid[:, 1, 15 * g_:15 * g_ + 15], w2[:, HD:P], start=True, stop=True)
            mm.then_inc(freed_by_pe, 1)

        def mla_entries(l):
            s = slot_of(("mla", l))
            uq = s[:, 0:960].rearrange("p (k f) -> p k f", k=2)
            ukv = s[:, 960:1600]
            out = []
            for h in range(5):
                out.append((f"mq{h}", 96, S, [(uq[:, k, 96 * h:96 * h + 96], l_cq[:, k, :]) for k in range(2)], l_q[0:96, h, :]))
            for h in range(5):
                out.append((f"mk{h}", HD, S, [(ukv[:, P * h:P * h + HD], l_ckv[:, 0, :])], l_k[0:HD, h, :]))
            v_cols = ukv.rearrange("p (h c) -> p h c", c=P)[:, :, HD:P]
            for t in range(2):
                out.append((f"mv{t}", P, 320, [(l_ckv[:, 0, t * P:(t + 1) * P], v_cols)], l_v[:, t, :]))
            return out

        def mla_pe(pe, l):
            pe.wait_ge(act_done, at("act", "latent squares", l))
            pe.matmul(wrk[:, 3, 0:S], ones, l_tmp3[:, 0, :], start=True, stop=False)
            pe.matmul(wrk[:, 3, 0:S], ones, l_tmp3[:, 1, :], start=False, stop=True)
            pe.matmul(wrk[:, 3, S:2 * S], ones, l_tmp3[:, 2, :], start=True, stop=True).then_inc(pe_done, up("pe", "latent sums", l))
            pe.wait_ge(dve_done, at("dve", "latents", l))
            entries = mla_entries(l)
            for i, (name, m, n, parts, place) in enumerate(entries):
                if i >= 4:
                    pe.wait_ge(act_done, at("act", "mla", l, entries[i - 4][0]))
                elif i < 3:
                    pe.wait_ge(act_done, at("act", "compressed", l))
                for k, (lhsT, rhs) in enumerate(parts):
                    mm = pe.matmul(wrk[0:m, i % 4, 0:n], lhsT, rhs, start=(k == 0), stop=(k == len(parts) - 1))
                if i == len(entries) - 1:
                    mm.then_inc(freed_by_pe, 1)
                else:
                    mm.then_inc(pe_done, up("pe", "mla", l, name))

        l_tmp3 = Z(9408, 3, S)

        def mla_act(act, l):
            act.wait_ge(act_done, at("act", "proj", ("2", l), "ckv"))
            act.activation(l_tmp3[:, 0:2, :], l_cq, ACT.Square).then_inc(act_done, up("act"))
            act.activation(l_tmp3[:, 2:3, :], l_ckv, ACT.Square).then_inc(act_done, up("act", "latent squares", l))
            root_act(act, at("dve", "latent mean squares", l), ("latent root", l), l_tmp[:, 0:512])
            act.wait_ge(dve_done, at("dve", "rope", ("2", l), "kpe"))
            act.wait_ge(pe_done, at("pe", "mla", l, "mq0"))
            for h in range(5):
                act.activation(l_k[64:96, h, :], l_kpe[64:96, 0, :], ACT.Copy).then_inc(act_done, up("act", "kpe", l) if h == 4 else up("act"))
            for i, (name, m, n, parts, place) in enumerate(mla_entries(l)):
                if name == "mv1":
                    act.wait_ge(freed_by_pe, freeing(("mla", l)))
                else:
                    act.wait_ge(pe_done, at("pe", "mla", l, name))
                act.activation(place, wrk[0:m, i % 4, 0:n], ACT.Copy).then_inc(act_done, up("act", "mla", l, name))

        def mla_dve(dve, l):
            dve.wait_ge(pe_done, at("pe", "latent sums", l))
            dve.tensor_scalar(l_tmp[:, 0:S], wrk[:, 3, 0:S], 1.0 / 256, EPS, ALU.mult, ALU.add).then_inc(dve_done, up("dve"))
            dve.tensor_scalar(l_tmp[:, S:2 * S], wrk[:, 3, S:2 * S], 1.0 / 128, EPS, ALU.mult, ALU.add)\
               .then_inc(dve_done, up("dve", "latent mean squares", l))
            inverse_root_dve(dve, ("latent root", l), l_tmp[:, 0:512])
            settle(dve, "dve", dve_done)
            for k in range(2):
                dve.scalar_tensor_tensor(l_cq[:, k, :], l_cq[:, k, :], column("mla_q_norm_2", 2 * l + k), l_tmp[:, 0:S],
                                         ALU.mult, ALU.mult).then_inc(dve_done, up("dve"))
            dve.scalar_tensor_tensor(l_ckv[:, 0, :], l_ckv[:, 0, :], column("mla_kv_norm_2", l), l_tmp[:, S:2 * S],
                                     ALU.mult, ALU.mult).then_inc(dve_done, up("dve", "latents", l))

        def branches2(l):
            out = []
            for h in range(6):
                g_, i = h // 3, h % 3
                rows = slice(HD * g_, HD * g_ + HD)
                q = n_q[rows, i, :]
                for br, kind in enumerate(("cmp", "slc", "win")):
                    k = (n_kcT[rows, :], n_ks[rows, 0, :], n_kw[rows, 0, :])[br]
                    if br == 0:
                        v = lambda t, g_=g_: n_vcT[0:15, HD * g_:HD * g_ + HD]
                    else:
                        z = (None, n_vs, n_vw)[br]
                        v = lambda t, z=z, g_=g_: z[:, t, HD * g_:HD * g_ + HD]
                    out.append(dict(q=q, k=k, v=v, mask=K("cmp_hide") if br == 0 else K("causal"), kind="cmp" if br == 0 else "causal",
                                    scale=float(HD) ** -0.5, gate=lambda t, c=3 * h + br: n_gate[:, t, c:c + 1], first=br == 0,
                                    last=br == 2, p0=HD * (h % 2), place=mixT[HD * (h % 2):HD * (h % 2) + HD, h // 2, :],
                                    ready=[(act_done, at("act", "mla", l, "mv1")),
                                           (dve_done, at("dve", "rope", ("mla", l), "mq4"))] if (h, br) == (0, 0) else [],
                                    mask_ready=[]))
            for h in range(5):
                p0 = HD * (h % 2)
                out.append(dict(q=l_q[0:96, h, :], k=l_k[0:96, h, :], v=lambda t, h=h: l_v[:, t, HD * h:HD * h + HD],
                                mask=K("causal"), kind="causal", scale=96.0 ** -0.5, gate=None, first=True, last=True, p0=p0,
                                place=mixT[p0:p0 + HD, 3 + h // 2, :], ready=[(act_done, at("act", "kpe", l))] if h == 0 else [],
                                mask_ready=[]))
            return out

        t_a = [a_prob[0], a_prob[1]]
        UPPER = slice(HD, P)

        def ret_at(h):
            return (h + 1) // 2, HD * ((h + 1) % 2)

        def ret_pe(pe, l):
            units = len(branches2(l))
            pe.wait_ge(act_done, at("act", "probT", ("2", l), units - 1))
            pe.wait_ge(dve_done, at("dve", "head out", ("2", l), 10))
            for h in range(6):
                if h < 5:
                    j, p0 = ret_at(h)
                    q, k = t_q[p0:p0 + HD, j, :], t_k[p0:p0 + HD, j, :]
                    if h >= 2:
                        pe.wait_ge(dve_done, at("dve", "decayed", l, h - 2))
                    pe.matmul(wrk[:, h % 2, 0:S], k[:, T0], q, start=True, stop=True)
                    pe.matmul(wrk[:, h % 2, S:384], k[:, T1], q[:, T1], start=True, stop=True).then_inc(pe_done, up("pe", "ret scores", l, h))
                if h >= 1:
                    j, p0 = ret_at(h - 1)
                    pe.wait_ge(dve_done, at("dve", "decayed", l, h - 1))
                    a = t_a[(h - 1) % 2]
                    pe.matmul(acc[p0:p0 + HD, j, 0:S], t_v[:, 0, HD * (h - 1):HD * h], a[:, 0:S], start=True, stop=False, skip_group_check=True)
                    pe.matmul(acc[p0:p0 + HD, j, P:S], t_v[:, 1, HD * (h - 1):HD * h], a[:, S:384], start=False, stop=True,
                              skip_group_check=True).then_inc(pe_done, up("pe", "ret out", l, h - 1))

            def head_sums(src, name):
                pe.matmul(wrk[UPPER, 2, 0:S], headsum[UPPER, UPPER], src[UPPER, 0, :], start=True, stop=True)
                pe.matmul(wrk[:, 3, :], headsum, src[:, 1:3, :].rearrange("p a t -> p (a t)"), start=True, stop=True)\
                  .then_inc(pe_done, up("pe", name, l))

            pe.wait_ge(act_done, at("act", "ret o", l))
            head_sums(t_q, "ret means")
            pe.wait_ge(act_done, at("act", "ret squares", l))
            head_sums(t_k, "ret variances")

        def ret_act(act, l):
            act.wait_ge(pe_done, at("pe", "ret out", l, 4))
            act.activation(t_q[UPPER, 0, :], acc[UPPER, 0, 0:S], ACT.Copy).then_inc(act_done, up("act"))
            act.activation(t_q[:, 1:3, :], acc[:, 1:3, 0:S], ACT.Copy).then_inc(act_done, up("act", "ret o", l))
            act.wait_ge(dve_done, at("dve", "ret centred", l))
            act.activation(t_k[UPPER, 0, :], t_q[UPPER, 0, :], ACT.Square).then_inc(act_done, up("act"))
            act.activation(t_k[:, 1:3, :], t_q[:, 1:3, :], ACT.Square).then_inc(act_done, up("act", "ret squares", l))
            act.wait_ge(dve_done, at("dve", "ret spreads", l))
            act.activation(t_k[UPPER, 0, :], t_k[UPPER, 0, :], ACT.Sqrt).then_inc(act_done, up("act"))
            act.activation(t_k[:, 1:3, :], t_k[:, 1:3, :], ACT.Sqrt).then_inc(act_done, up("act", "ret roots", l))

        def ret_dve(dve, l):
            decay = K("decay").rearrange("p (h n) -> p h n", h=5)
            for h in range(5):
                dve.wait_ge(pe_done, at("pe", "ret scores", l, h))
                if h >= 2:
                    dve.wait_ge(pe_done, at("pe", "ret out", l, h - 2))
                dve.tensor_tensor(t_a[h % 2], wrk[:, h % 2, 0:384], decay[:, h, :], ALU.mult).then_inc(dve_done, up("dve", "decayed", l, h))
            parts = ((UPPER, slice(0, 1), wrk[UPPER, 2:3, 0:S]),
                     (slice(0, P), slice(1, 3), wrk[:, 3, :].rearrange("p (a t) -> p a t", a=2)))
            dve.wait_ge(pe_done, at("pe", "ret means", l))
            for i, (rows, tiles, sums) in enumerate(parts):
                dve.scalar_tensor_tensor(t_q[rows, tiles, :], sums, -1.0 / HD, t_q[rows, tiles, :], ALU.mult, ALU.add)\
                   .then_inc(dve_done, up("dve", "ret centred", l) if i else up("dve"))
            dve.wait_ge(pe_done, at("pe", "ret variances", l))
            for i, (rows, tiles, sums) in enumerate(parts):
                dve.tensor_scalar(t_k[rows, tiles, :], sums, 1.0 / HD, EPS, ALU.mult, ALU.add)\
                   .then_inc(dve_done, up("dve", "ret spreads", l) if i else up("dve"))
            dve.wait_ge(act_done, at("act", "ret roots", l))
            for rows, tiles, sums in parts:
                dve.reciprocal(t_k[rows, tiles, :], t_k[rows, tiles, :]).then_inc(dve_done, up("dve"))
            settle(dve, "dve", dve_done)
            for rows, tiles, sums in parts:
                dve.tensor_tensor(t_q[rows, tiles, :], t_q[rows, tiles, :], t_k[rows, tiles, :], ALU.mult).then_inc(dve_done, up("dve"))
            settle(dve, "dve", dve_done)
            for j in range(3):
                rows = UPPER if j == 0 else slice(0, P)
                col = column("ret_gain", 3 * l + j)[rows]
                dve.scalar_tensor_tensor(mixT[rows, 5 + j, :], t_q[rows, j, :], col, t_g[rows, j, :], ALU.mult, ALU.mult)\
                   .then_inc(dve_done, up("dve", "r out", l) if j == 2 else up("dve"))

        def mlp_pe(pe, l):
            n = len(ffn_groups(D_FF))
            base = tile_base("mlp", l)
            pe.wait_ge(act_done, at("act", "h", ("mlp", l), KD - 1))
            for g_ in range(n + 1):
                if g_ < n:
                    item = ("mup", l, g_)
                    pe.wait_ge(*landing(item))
                    w = w_cols(item, 512)
                    for j in range(4):
                        i = base + 4 * g_ + j
                        pe.wait_ge(ffn_act, i - 3)
                        for k in range(KD):
                            mm = pe.matmul(wrk[:, j, 0:S], w[:, k, j * P:(j + 1) * P], hT[:, k, :], start=(k == 0), stop=(k == KD - 1))
                        mm.then_inc(ffn_up, 1)
                if g_ >= 1:
                    ffn_down_pe(pe, g_ - 1, D_FF, ("mdown", l, g_ - 1), base, 0, "mlp")

        def mlp_dve(dve, l):
            base = tile_base("mlp", l)
            groups = ffn_groups(D_FF)
            for g_ in range(len(groups)):
                if g_ >= 2:
                    dve.wait_ge(freed_by_pe, freeing(("mdown", l, g_ - 2)))
                for j in range(4):
                    i = base + 4 * g_ + j
                    dve.wait_ge(ffn_up, i + 1)
                    dve.tensor_scalar(F_SIL[:, j, :], wrk[:, j, 0:S], 0.0, None, ALU.max).then_inc(dve_done, up("dve"))
                    settle(dve, "dve", dve_done)
                    dve.tensor_tensor(F_ACT[:, 4 * (g_ % 2) + j, :], F_SIL[:, j, :], F_SIL[:, j, :], ALU.mult).then_inc(ffn_act, 1)
            dve.wait_ge(freed_by_pe, freeing(("mdown", l, len(groups) - 1)))
            for m in range(KD):
                dve.tensor_tensor(xT[:, m, :], accv[:, m, :], xT[:, m, :], ALU.add).then_inc(dve_done, up("dve", "residual", ("mlp", l), m))

        def vec_cols(name, l):
            return lambda k: column(name, 8 * l + k)

        def x_ready2(l):
            if l == 0:
                return [(act_done, at("act", "h", ("between",), KD - 1))]
            return [(dve_done, at("dve", "residual", ("mlp", 0), KD - 1))]

        def block2_pe(pe, l):
            tag = ("2", l)
            norm_pe(pe, ("ln1", l))
            project_pe(pe, tag, plan2(l), [(act_done, at("act", "h", ("ln1", l), KD - 1))])
            rope_pe(pe, tag, rope2(l), act_from(tag))
            pe.wait_ge(act_done, at("act", "proj", tag, "rg2"))
            cmp_pe(pe, l)
            mla_pe(pe, l)
            rope_pe(pe, ("mla", l), rope_mla(l), lambda name: at("act", "mla", l, name))
            att_pe(pe, tag, branches2(l))
            ret_pe(pe, l)
            outproj_pe(pe, tag, out_items("out2", l), [(dve_done, at("dve", "r out", l))])
            norm_pe(pe, ("mlp", l))
            mlp_pe(pe, l)

        def block2_act(act, l):
            tag = ("2", l)
            norm_act(act, ("ln1", l), x_ready2(l), vec_cols("ln1_gain_2", l), None)
            project_act(act, tag, plan2(l))
            cmp_act(act, l)
            mla_act(act, l)
            att_act(act, tag, branches2(l))
            ret_act(act, l)
            norm_act(act, ("mlp", l), [(dve_done, at("dve", "residual", ("out2", l), KD - 1))], vec_cols("ln2_gain_2", l), None)

        def block2_dve(dve, l):
            tag = ("2", l)
            norm_dve(dve, ("ln1", l))
            rope_dve(dve, tag, rope2(l), act_from(tag))
            cmp_dve(dve, l)
            mla_dve(dve, l)
            rope_dve(dve, ("mla", l), rope_mla(l), lambda name: at("act", "mla", l, name))
            att_dve(dve, tag, branches2(l))
            ret_dve(dve, l)
            residual_dve(dve, ("out2", l), None, out_waits(tag, out_items("out2", l)))
            norm_dve(dve, ("mlp", l))
            mlp_dve(dve, l)

        y_tok = flat_mix.rearrange("p (t d) -> p t d", t=2)

        def end_pe(pe):
            pe.wait_ge(act_done, at("act", "h", ("end",), KD - 1))
            for t in range(2):
                for k in range(KD):
                    mm = pe.transpose(flat_acc[:, t * D + k * P:t * D + (k + 1) * P], hT[:, k, t * P:(t + 1) * P], ident)
                mm.then_inc(pe_done, up("pe", "result", t))

        def end_act(act):
            for t in range(2):
                act.wait_ge(pe_done, at("pe", "result", t))
                act.activation(y_tok[:, t, :], flat_acc[:, t * D:(t + 1) * D], ACT.Copy).then_inc(act_done, up("act", "result", t))

        @block.sync
        def _(sp):
            body_sync(sp)
            for t in range(2):
                sp.wait_ge(act_done, at("act", "result", t))
                sp.dma_start(out[0, t * P:(t + 1) * P, :], y_tok[:, t, :]).then_inc(out_landed, 16)
            sp.wait_ge(out_landed, 32)

        @block.scalar
        def _(act):
            start_act(act)
            block1_act(act, 0)
            dense_act(act)
            block1_act(act, 1)
            route_act(act)
            experts_act(act)
            norm_act(act, ("between",), [(dve_done, at("dve", "residual", ("ffn", 1), KD - 1))], vec_cols("g_final", 0), None, xT)
            for l in range(DEPTH):
                block2_act(act, l)
            norm_act(act, ("end",), [(dve_done, at("dve", "residual", ("mlp", 1), KD - 1))], vec_cols("final_gain_2", 0), None)
            end_act(act)

        @block.tensor
        def _(pe):
            start_pe(pe)
            for i in range(12):
                ada_pe(pe, 0, i)
            block1_pe(pe, 0)
            dense_pe(pe)
            block1_pe(pe, 1)
            route_pe(pe)
            experts_pe(pe)
            norm_pe(pe, ("between",))
            for l in range(DEPTH):
                block2_pe(pe, l)
            norm_pe(pe, ("end",))
            end_pe(pe)

        @block.vector
        def _(dve):
            start_dve(dve)
            for i in range(12):
                ada_dve(dve, 0, i)
            ada_end_dve(dve, 0)
            block1_dve(dve, 0)
            dense_dve(dve)
            block1_dve(dve, 1)
            route_dve(dve)
            experts_dve(dve)
            experts_end_dve(dve)
            norm_dve(dve, ("between",))
            for l in range(DEPTH):
                block2_dve(dve, l)
            norm_dve(dve, ("end",))

    return count


_INS = ["x", "c", "positions", "w_ada", "b_ada", "g_norm_mix", "g_norm_ffn", "w_in", "w_out", "hgrn_lb_logits",
        "hgrn_out_norm", "gmlp_vnorm_g", "gmlp_vnorm_b", "gmlp_w_s", "gmlp_b_s", "ffn_w_gate", "ffn_w_up", "ffn_w_down",
        "moe_w_router", "moe_w_gate", "moe_w_up", "moe_w_down", "g_final", "positions_2", "ln1_gain_2", "w_in_2",
        "cmp_pos_k_2", "cmp_w1_k_2", "cmp_w2_k_2", "cmp_pos_v_2", "cmp_w1_v_2", "cmp_w2_v_2", "mla_q_norm_2", "mla_w_uq_2",
        "mla_kv_norm_2", "mla_w_ukv_2", "ret_gn_gain_2", "w_out_2", "ln2_gain_2", "w_up_2", "w_down_2", "final_gain_2"]


def written(known, arrays, bacc):
    nc = bacc.Bacc("TRN2", target_bir_lowering=False, num_devices=1)
    given = {}
    for name, a in arrays.items():
        given[name] = nc.dram_tensor(f"in_{name}_dram", a.shape, mybir.dt.from_np(a.dtype), kind="ExternalInput").ap()
    out = nc.dram_tensor("out_0_dram", (1, S, D), F32, kind="ExternalOutput").ap()
    return nc, program(nc, given, out, known)


def kernel(**inputs):
    import concourse.bacc as _bacc
    from concourse.bass_utils import run_bass_kernel_spmd as _run

    arrays = {name: np.ascontiguousarray(inputs[name]) for name in _INS}
    arrays["consts"] = CONSTS
    _, count = written(None, arrays, _bacc)
    nc, _ = written(count.names, arrays, _bacc)
    r = _run(nc, [{f"in_{name}_dram": a for name, a in arrays.items()}], core_ids=[0])
    return r.results[0]["out_0_dram"]
```

```python
from contextlib import ExitStack

import numpy as np

import concourse.bass as bass
from concourse import mybir

F32 = mybir.dt.float32
I32 = mybir.dt.int32
ALU = mybir.AluOpType
ACT = mybir.ActivationFunctionType
AX = mybir.AxisListType.X

P = 128
S = 256
D = 1024
KD = D // P
DEPTH = 2
HD = 64
EPS = 1e-6
NEG = -1e30
TAKEN = -3e38
TOPK = 64
F_DENSE, F_EXPERT, D_FF, NE = 2816, 3584, 4096, 8
SLOTS, SLOT = 7, 4096
C = 16
NB = S // C
NCMP = 15


CONST = {}


def constants():
    parts = []
    eye = np.eye(P, dtype=np.float32)
    row = np.arange(P)[:, None]
    col = np.arange(P)[None, :]

    def add(name, a):
        a = np.asarray(a, np.float32)
        a = a.reshape(a.shape[0], -1)
        if a.shape[0] < P:
            a = np.concatenate([a, np.zeros((P - a.shape[0], a.shape[1]), np.float32)])
        CONST[name] = (sum(x.shape[1] for x in parts), a.shape[1])
        parts.append(a)

    add("ident", eye)
    add("ones", np.ones((P, P)))
    add("headsum", (row // HD) == (col // HD))
    tri = np.where(col <= row, 0.0, NEG)
    add("causal", np.concatenate([tri, np.zeros((P, P)), tri], 1))
    add("upper", row <= col)

    def turn(heads, at, half):
        m = np.zeros((P, P), np.float32)
        for h in heads:
            for d in range(half):
                a, b = h + at + d, h + at + half + d
                m[b, a] = -1.0
                m[a, b] = 1.0
        return m

    add("turn64", turn((0, 64), 0, 32))
    add("turn16", turn((0, 64), 0, 8))
    add("turn32", turn((0,), 64, 16))

    def rates(theta, dim, heads, at, width=P):
        v = np.zeros((P, 1), np.float32)
        inv = (np.float32(1.0) / (np.float32(theta) ** (np.arange(0, dim, 2, dtype=np.float32) / np.float32(dim)))).astype(np.float32)
        for h in heads:
            v[h + at:h + at + dim // 2, 0] = inv
            v[h + at + dim // 2:h + at + dim, 0] = inv
        return v

    add("rate64", rates(10000.0, 64, (0, 64), 0))
    add("rate16", rates(500000.0, 16, (0, 64), 0))
    add("rate32", rates(500000.0, 32, (0,), 64))
    t = np.arange(S).reshape(2, P).T[:, :, None]
    end = (np.arange(NCMP) * 16 + 31)[None, None, :]
    see = np.zeros((P, 2, 16), np.float32)
    see[:, :, :NCMP] = end <= t
    add("cmp_see", see)
    add("cmp_hide", np.where(see > 0, 0.0, NEG))
    decay = np.zeros((P, 5, 384), np.float64)
    for h in range(5):
        g = np.log(1.0 - 2.0 ** (-5.0 - h))
        j = np.arange(P)[:, None]
        i = np.arange(S)[None, :]
        decay[:, h, :S] = np.where(i >= j, np.exp(np.maximum(i - j, 0) * g), 0.0)
        decay[:, h, S:] = decay[:, h, :P]
    CONST["decay"] = decay.reshape(P, -1).astype(np.float32)
    add("blocks", (np.arange(P)[:, None] // C) == np.arange(P // C)[None, :])
    add("slot_ids", np.broadcast_to(np.arange(S)[None, :], (P, S)))
    add("before", np.broadcast_to((np.arange(NE)[None, :] < np.arange(NE)[:, None]).reshape(1, -1), (P, NE * NE)))
    return np.concatenate(parts, 1).astype(np.float32)


CONSTS = constants()
DECAY = CONST.pop("decay")

VEC, VEC_LOADS = {}, []


def vector_rows():
    at = [0, 0, 0]
    for tile, name, rows in ((0, "c", 8), (0, "g_norm_mix", 16), (0, "g_norm_ffn", 16), (0, "g_final", 8),
                             (0, "ln1_gain_2", 16), (0, "ln2_gain_2", 16), (0, "final_gain_2", 8),
                             (0, "mla_q_norm_2", 4), (0, "mla_kv_norm_2", 2), (0, "hgrn_lb_logits", 6),
                             (1, "b_ada", 96), (2, "cmp_pos_k_2", 32), (2, "cmp_pos_v_2", 32)):
        VEC[name] = (tile, at[tile])
        VEC_LOADS.append((name, tile, at[tile], rows))
        at[tile] += rows
    for name, rows in (("onorm", 2), ("ret_gain", 6)):
        VEC[name] = (0, at[0])
        at[0] += rows
    assert max(at) <= P


vector_rows()


IN1 = [(0, 512), (512, 836), (836, 1220), (1220, 1604), (1604, 1988), (1988, 2372), (2372, 2884)]
IN2 = [(0, 512), (512, 1024), (1024, 1426), (1426, 1906), (1906, 2226), (2226, 2546), (2546, 2866)]


IN1_ORDER = (4, 2, 3, 0, 1, 5, 6)
DENSE_ADA = [(0, 10), (0, 11)] + [(1, i) for i in range(12)]


def dense_ada(g):
    return range(3 * g, 3 * g + 3) if g < 2 else range(6 + 2 * (g - 2), 8 + 2 * (g - 2))


def ffn_groups(width):
    return [(f, min(512, width - f)) for f in range(0, width, 512)]


def stream_items():
    before = [("ada", 0, i) for i in range(4)]
    experts, after = [], []
    for layer in range(DEPTH):
        out = before
        for n, i in enumerate(IN1_ORDER):
            out.append(("in1", layer, i))
            if layer == 0 and n >= 1:
                out.append(("ada", 0, 3 + n))
        out += [("gmlp", layer)] + [("out1", layer, h) for h in range(2)]
        if layer == 0:
            groups = ffn_groups(F_DENSE)
            for g in range(len(groups)):
                out += [("gate", g), ("up", g)]
                if g:
                    out.append(("down", g - 1))
                out += [("ada", *DENSE_ADA[n]) for n in dense_ada(g)]
            out.append(("down", len(groups) - 1))
    before.append(("router",))
    n = len(ffn_groups(F_EXPERT))
    for g in range(n):
        experts += [("egate", g), ("eup", g)]
        if g:
            experts.append(("edown", g - 1))
    experts.append(("edown", n - 1))
    for layer in range(DEPTH):
        after += [("in2", layer, i) for i in range(len(IN2))]
        after += [("cmp", layer), ("mla", layer), ("decay", layer)] + [("out2", layer, h) for h in range(2)]
        n = len(ffn_groups(D_FF))
        for g in range(n):
            after.append(("mup", layer, g))
            if g:
                after.append(("mdown", layer, g - 1))
        after.append(("mdown", layer, n - 1))
    assert len(experts) % SLOTS == 0
    return before, experts, after


BEFORE, EXPERTS, AFTER = stream_items()
FIRST_EXPERT = len(BEFORE)
FIRST_AFTER = FIRST_EXPERT + NE * len(EXPERTS)
PLACE = {item: n for n, item in enumerate(BEFORE)}
PLACE.update({item: FIRST_EXPERT + n for n, item in enumerate(EXPERTS)})
PLACE.update({item: FIRST_AFTER + n for n, item in enumerate(AFTER)})


class Counts:

    def __init__(self, known):
        self.known, self.names, self.last = known, {}, {}

    def up(self, engine, *name):
        self.last[engine] = self.last.get(engine, 0) + 1
        if name:
            assert (engine, *name) not in self.names, name
            self.names[(engine, *name)] = self.last[engine]
        return 1

    def at(self, engine, *name):
        if self.known is None:
            return 1
        return self.known[(engine, *name)]

    def now(self, engine):
        return self.last[engine]


def program(nc, given, out, known, stop=None, dumps=None):
    count = Counts(known)
    up, at, now = count.up, count.at, count.now

    with ExitStack() as ctx:
        def sb(name, shape, dt=F32):
            return ctx.enter_context(nc.sbuf_tensor(name, shape, dt))

        def sem(name):
            return ctx.enter_context(nc.semaphore(name))

        ring = sb("ring", [P, SLOTS, SLOT])
        const = sb("const", list(CONSTS.shape))
        vec_rows = sb("vec_rows", [P, 3, P])
        vec = sb("vec", [P, 3, P])
        xT = sb("xT", [P, KD, S])
        hT = sb("hT", [P, KD, S])
        mixT = sb("mixT", [P, KD, S])
        cond = sb("cond", [P, KD])
        mods = sb("mods", [P, DEPTH, 48])
        gain = sb("gain", [P, 4, KD])
        lower = sb("lower", [P, DEPTH, 3])
        stat = sb("stat", [P, 128])
        table = sb("table", [P, 4, 2, S])
        SCR = sb("scratch", [P, 13200])
        acc = ctx.enter_context(nc.psum_tensor("acc", [P, 4, 512], F32))
        wrk = ctx.enter_context(nc.psum_tensor("wrk", [P, 4, 512], F32))

        def K(name):
            o, n = CONST[name]
            return const[:, o:o + n]

        def carve(tensor, offset, *shape):
            n = int(np.prod(shape))
            flat = tensor if tensor is not SCR else SCR[:, :]
            v = flat[:, offset:offset + n]
            if len(shape) == 2:
                v = v.rearrange("p (a b) -> p a b", a=shape[0])
            if len(shape) == 3:
                v = v.rearrange("p (a b c) -> p a b c", a=shape[0], b=shape[1])
            return v

        def column(name, i):
            t, r = VEC[name]
            return vec[:, t, r + i:r + i + 1]

        def columns(name, i, n):
            t, r = VEC[name]
            return vec[:, t, r + i:r + i + n]

        params_landed = sem("params_landed")
        landed = [sem(f"landed{i}") for i in range(SLOTS)]
        freed_by_pe = sem("freed_by_pe")
        freed_by_dve = sem("freed_by_dve")
        pe_done, act_done = sem("pe_done"), sem("act_done")
        dve_done, pool_done = sem("dve_done"), sem("pool_done")
        ffn_up = sem("ffn_up")
        ffn_silu = sem("ffn_silu")
        ffn_act = sem("ffn_act")
        ffn_read = sem("ffn_read")
        picked = sem("picked")
        pick_turned = sem("pick_turned")
        pick_ready = sem("pick_ready")
        gathered = sem("gathered")
        tokens_ready = sem("tokens_ready")
        rows_ready = sem("rows_ready")
        scattered = sem("scattered")
        share_added = sem("share_added")
        out_landed = sem("out_landed")

        free, counts = {}, {"pe": 0, "dve": 0, "up": 0}
        UP_TILES = sum(n // P for _, n in ffn_groups(F_EXPERT))
        FREED = sum(1 for i in EXPERTS if i[0] != "eup")

        def note(n, item):
            kind = item[0]
            if kind in ("ada", "decay"):
                counts["dve"] += 1
                free[n] = (freed_by_dve, counts["dve"], 0)
            elif kind in ("up", "eup", "mup"):
                width = {"up": F_DENSE, "eup": F_EXPERT, "mup": D_FF}[kind]
                counts["up"] += ffn_groups(width)[item[-1]][1] // P
                free[n] = (ffn_up, counts["up"], UP_TILES)
            else:
                counts["pe"] += 1
                free[n] = (freed_by_pe, counts["pe"], FREED)

        for n, item in enumerate(BEFORE):
            note(n, item)
        before_experts = dict(counts)
        for i, item in enumerate(EXPERTS):
            note(FIRST_EXPERT + i, item)
        assert counts["pe"] - before_experts["pe"] == FREED and counts["up"] - before_experts["up"] == UP_TILES
        counts["pe"] += FREED * (NE - 1)
        counts["up"] += UP_TILES * (NE - 1)
        for i in range(SLOTS):
            s_, v_, d_ = free[FIRST_EXPERT + len(EXPERTS) - SLOTS + i]
            free[FIRST_AFTER - SLOTS + i] = (s_, v_ + d_ * (NE - 1), 0)
        for i, item in enumerate(AFTER):
            note(FIRST_AFTER + i, item)

        def free_of(n):
            return free[n][0], free[n][1]

        def freeing(item):
            assert free[PLACE[item]][0] is freed_by_pe
            return free[PLACE[item]][1]

        def slot_of(item):
            return ring[:, PLACE[item] % SLOTS, :]

        def w_cols(item, width):
            return slot_of(item)[:, 0:KD * width].rearrange("p (k f) -> p k f", k=KD)

        def by_rows(w):
            return w.rearrange("(k p) f -> p k f", p=P)

        g = given

        def loads(item):
            kind = item[0]
            s = slot_of(item)
            if kind == "ada":
                return [(w_cols(item, 512), by_rows(g["w_ada"][item[1]])[:, :, item[2] * 512:item[2] * 512 + 512])]
            if item[0] == "in2" and item[2] == 0:
                w = by_rows(g["w_in_2"][item[1]])
                v = w_cols(item, 512)
                heads = v[:, :, 0:384].rearrange("p k (i g d) -> p k i g d", i=3, g=2)
                src = w[:, :, 0:384].rearrange("p k (g i d) -> p k i g d", i=3, g=2)
                return [(heads[:, :, i, q], src[:, :, i, q]) for i in range(3) for q in range(2)] + [(v[:, :, 384:512], w[:, :, 384:512])]
            if kind in ("in1", "in2"):
                a, b = (IN1 if kind == "in1" else IN2)[item[2]]
                w = g["w_in" if kind == "in1" else "w_in_2"][item[1]]
                return [(w_cols(item, b - a), by_rows(w)[:, :, a:b])]
            if kind in ("out1", "out2"):
                w = g["w_out" if kind == "out1" else "w_out_2"][item[1]]
                return [(w_cols(item, 512), by_rows(w)[:, :, item[2] * 512:item[2] * 512 + 512])]
            if kind in ("gate", "up"):
                f, n = ffn_groups(F_DENSE)[item[1]]
                return [(w_cols(item, n), by_rows(g["ffn_w_" + kind][0])[:, :, f:f + n])]
            if kind == "down":
                f, n = ffn_groups(F_DENSE)[item[1]]
                return [(s[:, 0:n * KD].rearrange("p (j d) -> p j d", d=D),
                         g["ffn_w_down"][0, f:f + n].rearrange("(j p) d -> p j d", p=P))]
            if kind == "mup":
                f, n = ffn_groups(D_FF)[item[2]]
                return [(w_cols(item, n), by_rows(g["w_up_2"][item[1]])[:, :, f:f + n])]
            if kind == "mdown":
                f, n = ffn_groups(D_FF)[item[2]]
                return [(s[:, 0:n * KD].rearrange("p (j d) -> p j d", d=D),
                         g["w_down_2"][item[1], f:f + n].rearrange("(j p) d -> p j d", p=P))]
            if kind == "gmlp":
                l = item[1]
                return [(s[:, 0:256], rows_of(g["gmlp_vnorm_g"], l)),
                        (s[:, 256:512], rows_of(g["gmlp_vnorm_b"], l)),
                        (s[:, 512:1024].rearrange("p (g s) -> p g s", g=4), g["gmlp_w_s"][l].rearrange("g t s -> t g s")),
                        (s[0:1, 1024:1536], g["gmlp_b_s"][l:l + 1].rearrange("a g t -> a (g t)"))]
            if kind == "decay":
                return [(s[:, 0:5 * 384], g["decay"])]
            if kind == "router":
                return [(s[:, 0:64].rearrange("p (k e) -> p k e", k=KD), by_rows(g["moe_w_router"][0]))]
            if kind == "cmp":
                l = item[1]
                v = s.rearrange("p (a j h) -> p a j h", a=2, j=16)
                return [(v[:, 0], g["cmp_w1_k_2"][l].rearrange("(j p) h -> p j h", p=P)),
                        (v[:, 1], g["cmp_w1_v_2"][l].rearrange("(j p) h -> p j h", p=P))]
            if kind == "mla":
                l = item[1]
                return [(s[:, 0:960].rearrange("p (k f) -> p k f", k=2), by_rows(g["mla_w_uq_2"][l])),
                        (s[:, 960:1600], g["mla_w_ukv_2"][l]),
                        (s[:, 1600:1664], g["cmp_w2_k_2"][l]),
                        (s[:, 1664:1728], g["cmp_w2_v_2"][l])]
            raise KeyError(item)

        def rows_of(w, l):
            r = w[l:l + 1, :]
            return bass.AP(tensor=r.tensor, offset=r.offset, ap=[[0, P], [1, r.shape[1]]])

        land = {}
        total = [0] * SLOTS
        for n, item in enumerate(BEFORE):
            total[n % SLOTS] += 16 * len(loads(item))
            land[n] = total[n % SLOTS]
        at_experts = list(total)
        for i in range(SLOTS):
            total[i] += 16 * NE * (len(EXPERTS) // SLOTS)
        for i, item in enumerate(AFTER):
            n = FIRST_AFTER + i
            total[n % SLOTS] += 16 * len(loads(item))
            land[n] = total[n % SLOTS]

        def landing(item):
            n = PLACE[item]
            return landed[n % SLOTS], land[n]

        xin = carve(hT[:, :, :].rearrange("p k t -> p (k t)"), 0, 2, D)
        pos = SCR[:, 6800:6800 + 2 * S].bitcast(I32).rearrange("p (b t) -> p b t", b=2)
        c_rows = sb("c_rows", [KD, P])

        def flat_rows(src):
            letters = "abcd"[:len(src.shape)]
            flat = src.rearrange(f"{' '.join(letters)} -> ({' '.join(letters)})") if len(src.shape) > 1 else src
            return flat.rearrange("(r p) -> r p", p=P)

        IDENT = slice(CONST["ident"][0], CONST["ident"][0] + P)
        REST = slice(P, CONSTS.shape[1])
        x_landed, c_landed, rest_landed = sem("x_landed"), sem("c_landed"), sem("rest_landed")
        vec_loads = [(vec_rows[r:r + rows, t, :], flat_rows(g[name])) for name, t, r, rows in VEC_LOADS if name != "c"]
        t, r = VEC["onorm"]
        for half in range(2):
            vec_loads.append((vec_rows[r:r + 2, t, half * HD:(half + 1) * HD], g["hgrn_out_norm"]))
        t, r = VEC["ret_gain"]
        for l in range(DEPTH):
            gl = g["ret_gn_gain_2"][l].rearrange("h d -> (h d)")
            vec_loads.append((vec_rows[r + 3 * l:r + 3 * l + 1, t, HD:P], gl[0:HD].rearrange("(a d) -> a d", a=1)))
            vec_loads.append((vec_rows[r + 3 * l + 1:r + 3 * l + 3, t, :], gl[HD:5 * HD].rearrange("(r p) -> r p", p=P)))
        PARAMS = 16 * len(vec_loads)

        block = ctx.enter_context(nc.Block())
        stops = {}

        def body_sync(sp):
            sp.dma_start(const[:, IDENT], g["consts"][:, IDENT]).then_inc(c_landed, 16)
            sp.dma_start(c_rows[:, :], flat_rows(g["c"])).then_inc(c_landed, 16)
            sp.dma_start(xin, g["x"][0].rearrange("(t p) d -> p t d", p=P)).then_inc(x_landed, 16)
            sp.dma_start(const[:, REST], g["consts"][:, REST]).then_inc(rest_landed, 16)
            for n, item in enumerate(BEFORE):
                if stop is not None and n >= stop[0]:
                    break
                if n >= SLOTS:
                    sp.wait_ge(*free_of(n - SLOTS))
                for place, src in loads(item):
                    sp.dma_start(place, src).then_inc(landed[n % SLOTS], 16)
            if stop is None:
                sources = {"egate": g["moe_w_gate"], "eup": g["moe_w_up"], "edown": g["moe_w_down"]}
                groups = ffn_groups(F_EXPERT)
                with sp.Fori(0, NE) as e:
                    for i, item in enumerate(EXPERTS):
                        n = FIRST_EXPERT + i
                        if i >= SLOTS:
                            s, v, d = free[n - SLOTS]
                            sp.wait_ge(s, e * d + v)
                        else:
                            s, v, d = free[n - SLOTS + len(EXPERTS)]
                            sp.wait_ge(*free_of(n - SLOTS))
                            sp.wait_ge(s, e * d + (v - d))
                        f, w = groups[item[1]]
                        src = sources[item[0]][0][e]
                        if item[0] == "edown":
                            sp.dma_start(ring[:, n % SLOTS, 0:w * KD].rearrange("p (j d) -> p j d", d=D),
                                         src[f:f + w].rearrange("(j p) d -> p j d", p=P)).then_inc(landed[n % SLOTS], 16)
                        else:
                            sp.dma_start(ring[:, n % SLOTS, 0:w * KD].rearrange("p (k f) -> p k f", k=KD),
                                         by_rows(src)[:, :, f:f + w]).then_inc(landed[n % SLOTS], 16)
                for i, item in enumerate(AFTER):
                    n = FIRST_AFTER + i
                    sp.wait_ge(*free_of(n - SLOTS))
                    for place, src in loads(item):
                        sp.dma_start(place, src).then_inc(landed[n % SLOTS], 16)

        accv = acc[:, :, :].rearrange("p b (h t) -> p (b h) t", t=S)
        T0, T1 = slice(0, P), slice(P, S)
        ident, ones, headsum = K("ident"), K("ones"), K("headsum")
        rstd = mixT[:, 0, :]

        def settle(eng, name, s):
            eng.wait_ge(s, now(name))

        ang = carve(SCR, 7312, 4, S)
        turns = carve(SCR, 8336, 4, S)
        fpos = carve(SCR, 9360, 2, S)
        TWO_PI_PARTS = (6.28125, 0.0019340515136718750, 2 * np.pi - 6.28125 - 0.0019340515136718750)
        ROUND = 12582912.0

        def start_act(act):
            act.wait_ge(dve_done, at("dve", "rows cleared"))
            for place, src in vec_loads:
                act.dma_start(place, src).then_inc(params_landed, 16)
            for b, name in enumerate(("positions", "positions_2")):
                r = g[name]
                act.dma_start(pos[:, b, :], bass.AP(tensor=r.tensor, offset=r.offset, ap=[[0, P], [1, S]])).then_inc(rest_landed, 16)
            act.wait_ge(pe_done, at("pe", "c turned"))
            act.activation(cond[:, :], wrk[:, 0, 0:KD], ACT.Silu).then_inc(act_done, up("act", "cond"))
            act.wait_ge(pe_done, at("pe", "x turned"))
            act.activation(xT[:, 0:4, :], accv[:, 0:4, :], ACT.Copy).then_inc(act_done, up("act"))
            act.activation(xT[:, 4:8, :], accv[:, 4:8, :], ACT.Copy).then_inc(act_done, up("act", "x"))

        def tables_act(act):
            act.wait_ge(dve_done, at("dve", "lower in"))
            act.activation(stat[:, 3:9], stat[:, 3:9], ACT.Exp).then_inc(act_done, up("act", "lower exp"))
            act.wait_ge(dve_done, at("dve", "angles"))
            act.activation(table[:, :, 1, :], ang, ACT.Sin).then_inc(act_done, up("act"))
            act.activation(table[:, :, 0, :], turns, ACT.Sin).then_inc(act_done, up("act", "tables"))

        def start_pe(pe):
            pe.wait_ge(c_landed, 32)
            pe.transpose(wrk[:, 0, 0:KD], c_rows[:, :], ident[0:KD, 0:KD]).then_inc(pe_done, up("pe", "c turned"))
            pe.wait_ge(x_landed, 16)
            for k in range(KD):
                for t in range(2):
                    mm = pe.transpose(accv[:, k, t * P:(t + 1) * P], xin[:, t, k * P:(k + 1) * P], ident)
            mm.then_inc(pe_done, up("pe", "x turned"))
            pe.wait_ge(params_landed, PARAMS)
            for t in range(3):
                mm = pe.transpose(wrk[:, 1, t * P:(t + 1) * P], vec_rows[:, t, :], ident)
            mm.then_inc(pe_done, up("pe", "vec"))
            pe.wait_ge(rest_landed, 48)

        def start_dve(dve):
            dve.memset(vec_rows[:, :, :], 0.0).then_inc(dve_done, up("dve", "rows cleared"))

        def vec_dve(dve):
            dve.wait_ge(pe_done, at("pe", "vec"))
            dve.tensor_copy(vec[:, :, :].rearrange("p a b -> p (a b)"), wrk[:, 1, 0:3 * P]).then_inc(dve_done, up("dve", "vec"))

        def tables_dve(dve):
            a0, a1 = columns("hgrn_lb_logits", 0, 3), columns("hgrn_lb_logits", 3, 3)
            dve.tensor_tensor(stat[:, 0:3], a0, a1, ALU.max).then_inc(dve_done, up("dve"))
            settle(dve, "dve", dve_done)
            dve.tensor_tensor(stat[:, 3:6], a0, stat[:, 0:3], ALU.subtract).then_inc(dve_done, up("dve"))
            dve.tensor_tensor(stat[:, 6:9], a1, stat[:, 0:3], ALU.subtract).then_inc(dve_done, up("dve", "lower in"))
            dve.wait_ge(act_done, at("act", "lower exp"))
            dve.tensor_tensor(stat[:, 9:12], stat[:, 3:6], stat[:, 6:9], ALU.add).then_inc(dve_done, up("dve"))
            settle(dve, "dve", dve_done)
            dve.reciprocal(stat[:, 12:15], stat[:, 9:12]).then_inc(dve_done, up("dve"))
            settle(dve, "dve", dve_done)
            dve.tensor_tensor(stat[:, 15:18], stat[:, 3:6], stat[:, 12:15], ALU.mult).then_inc(dve_done, up("dve"))
            dve.tensor_tensor(stat[:, 18:21], stat[:, 6:9], stat[:, 12:15], ALU.mult).then_inc(dve_done, up("dve"))
            settle(dve, "dve", dve_done)
            dve.tensor_tensor(stat[:, 21:24], stat[:, 15:18], stat[:, 18:21], ALU.add).then_inc(dve_done, up("dve"))
            dve.tensor_tensor(lower[:, 0, :], stat[:, 15:18], stat[:, 15:18], ALU.subtract).then_inc(dve_done, up("dve"))
            settle(dve, "dve", dve_done)
            dve.tensor_tensor(lower[:, 1, :], stat[:, 21:24], stat[:, 15:18], ALU.subtract).then_inc(dve_done, up("dve", "lower"))
            dve.wait_ge(rest_landed, 48)
            dve.tensor_copy(fpos, pos).then_inc(dve_done, up("dve"))
            settle(dve, "dve", dve_done)
            for i, (b, rate) in enumerate(((0, "rate64"), (1, "rate64"), (1, "rate16"), (1, "rate32"))):
                dve.tensor_scalar(ang[:, i, :], fpos[:, b, :], K(rate), None, ALU.mult).then_inc(dve_done, up("dve"))
            settle(dve, "dve", dve_done)
            dve.tensor_scalar(turns, ang, float(1 / (2 * np.pi)), ROUND, ALU.mult, ALU.add).then_inc(dve_done, up("dve"))
            settle(dve, "dve", dve_done)
            dve.tensor_scalar(turns, turns, ROUND, None, ALU.subtract).then_inc(dve_done, up("dve"))
            for part in TWO_PI_PARTS:
                settle(dve, "dve", dve_done)
                for i in range(4):
                    dve.scalar_tensor_tensor(ang[:, i, :], turns[:, i, :], -float(part), ang[:, i, :], ALU.mult, ALU.add)\
                       .then_inc(dve_done, up("dve"))
            settle(dve, "dve", dve_done)
            dve.tensor_scalar(ang, ang, 3.1415925, -3.1415925, ALU.min, ALU.max).then_inc(dve_done, up("dve"))
            settle(dve, "dve", dve_done)
            dve.scalar_tensor_tensor(turns, ang, -1.0, ang, ALU.mult, ALU.max).then_inc(dve_done, up("dve"))
            settle(dve, "dve", dve_done)
            dve.tensor_scalar(turns, turns, -1.0, float(np.pi / 2), ALU.mult, ALU.add).then_inc(dve_done, up("dve", "angles"))

        part_sum = [SCR[:, 12176 + 512 * i:12176 + 512 * (i + 1)] for i in range(2)]

        def ada_dve(dve, l, i):
            item = ("ada", l, i)
            w = w_cols(item, 512)
            dve.wait_ge(*landing(item))
            n = 12 * l + i
            if n == 0:
                dve.wait_ge(act_done, at("act", "cond"))
            if n >= 2:
                dve.wait_ge(pe_done, at("pe", "ada", n - 2))
            dst = part_sum[n % 2]
            for k in range(KD):
                if k == 0:
                    ins = dve.tensor_scalar(dst, w[:, k, :], cond[:, k:k + 1], None, ALU.mult)
                else:
                    settle(dve, "dve", dve_done)
                    ins = dve.scalar_tensor_tensor(dst, w[:, k, :], cond[:, k:k + 1], dst, ALU.mult, ALU.add)
                if k < KD - 1:
                    ins.then_inc(dve_done, up("dve"))
                else:
                    ins.then_inc(freed_by_dve, 1)

        def ada_bank(l, i):
            return acc[:, 1, :] if (l, i) < (0, 10) else wrk[:, 3, 64 * l:64 * l + 48]

        def ada_pe(pe, l, i):
            n = 12 * l + i
            if n == 0:
                pe.wait_ge(act_done, at("act", "x"))
            pe.wait_ge(freed_by_dve, n + 1)
            for j in range(4):
                mm = pe.matmul(ada_bank(l, i)[:, 4 * i + j:4 * i + j + 1], part_sum[n % 2][:, j * P:(j + 1) * P], ones[:, 0:1],
                               start=True, stop=True)
            mm.then_inc(pe_done, up("pe", "ada", n))

        def ada_end_dve(dve, l, first, last):
            dve.wait_ge(pe_done, at("pe", "ada", 12 * l + last))
            a, b = 4 * first, 4 * last + 4
            dve.tensor_tensor(mods[:, l, a:b], ada_bank(l, last)[:, a:b], columns("b_ada", 48 * l + a, b - a), ALU.add)\
               .then_inc(dve_done, up("dve", "mods", l, last))
            settle(dve, "dve", dve_done)
            for j, (sc, name) in enumerate(((8, "g_norm_mix"), (32, "g_norm_ffn"))):
                if a <= sc < b:
                    dve.scalar_tensor_tensor(gain[:, 2 * l + j, :], mods[:, l, sc:sc + 8], 1.0, columns(name, 8 * l, 8),
                                             ALU.add, ALU.mult).then_inc(dve_done, up("dve", "gain", l, j))

        def norm_act(act, tag, wait_x, scale_of, shift_of, place=None, wait_scale=()):
            place = hT if place is None else place
            for s, v in wait_x:
                act.wait_ge(s, v)
            act.activation(hT[:, :, :], xT[:, :, :], ACT.Square).then_inc(act_done, up("act", "squares", tag))
            root_act(act, at("dve", "mean square", tag), ("root", tag), rstd)
            act.wait_ge(dve_done, at("dve", "scaled", tag))
            for s, v in wait_scale:
                act.wait_ge(s, v)
            for k in range(KD):
                act.activation(place[:, k, :], hT[:, k, :], ACT.Identity, scale=scale_of(k),
                               bias=shift_of(k) if shift_of else 0.0).then_inc(act_done, up("act", "h", tag, k))

        def norm_pe(pe, tag):
            pe.wait_ge(act_done, at("act", "squares", tag))
            for k in range(KD):
                mm = pe.matmul(wrk[:, 3, 0:S], ones, hT[:, k, :], start=(k == 0), stop=(k == KD - 1))
            mm.then_inc(pe_done, up("pe", "sum of squares", tag))

        def norm_dve(dve, tag):
            dve.wait_ge(pe_done, at("pe", "sum of squares", tag))
            dve.tensor_scalar(rstd, wrk[:, 3, 0:S], 1.0 / D, EPS, ALU.mult, ALU.add).then_inc(dve_done, up("dve", "mean square", tag))
            inverse_root_dve(dve, ("root", tag), rstd)
            settle(dve, "dve", dve_done)
            dve.tensor_tensor(hT[:, :, :], xT[:, :, :], rstd.unsqueeze(1).broadcast_to([P, KD, S]), ALU.mult)\
               .then_inc(dve_done, up("dve", "scaled", tag))

        def root_act(act, wait, name, place):
            act.wait_ge(dve_done, wait)
            act.activation(place, place, ACT.Sqrt).then_inc(act_done, up("act", *name))

        def inverse_root_dve(dve, name, place):
            dve.wait_ge(act_done, at("act", *name))
            dve.reciprocal(place, place).then_inc(dve_done, up("dve"))

        def project_pe(pe, tag, plan, i):
            name, item, mode, cols, m, p0, places = plan[i]
            bank = 2 + i % 2
            if i == 0 or plan[i - 1][1] != item:
                pe.wait_ge(*landing(item))
            if i >= 2:
                pe.wait_ge(act_done, at("act", "proj", tag, plan[i - 2][0]))
            for k in range(KD):
                if mode == "f":
                    mm = pe.matmul(acc[p0:p0 + m, bank, 0:S], cols(k), hT[:, k, :], start=(k == 0), stop=(k == KD - 1))
                else:
                    t = T0 if mode == "t0" else T1
                    mm = pe.matmul(acc[:, bank, 0:m], hT[:, k, t], cols(k), start=(k == 0), stop=(k == KD - 1))
            if i + 1 == len(plan) or plan[i + 1][1] != item:
                mm.then_inc(freed_by_pe, 1)
            else:
                mm.then_inc(pe_done, up("pe", "proj", tag, name))

        def project_act(act, tag, plan, i):
            name, item, mode, cols, m, p0, places = plan[i]
            if i + 1 == len(plan) or plan[i + 1][1] != item:
                act.wait_ge(freed_by_pe, freeing(item))
            else:
                act.wait_ge(pe_done, at("pe", "proj", tag, name))
            n = S if mode == "f" else m
            lo, hi = (p0, p0 + m) if mode == "f" else (0, P)
            for j, (place, func, scale) in enumerate(places):
                act.activation(place, acc[lo:hi, 2 + i % 2, 0:n], func, scale=scale)\
                   .then_inc(act_done, up("act", "proj", tag, name) if j == len(places) - 1 else up("act"))

        rope_tmp = [SCR[:, 12176 + 256 * i:12176 + 256 * (i + 1)] for i in range(4)]

        def rope_pe(pe, tag, plan, wait_names):
            for i, (name, tile, turn, tab, p0, rows) in enumerate(plan):
                pe.wait_ge(act_done, wait_names(name))
                if i >= 2:
                    pe.wait_ge(dve_done, at("dve", "rope", tag, plan[i - 2][0]))
                pe.matmul(acc[p0:p0 + rows, i % 2, 0:S], K(turn)[p0:p0 + rows, p0:p0 + rows], tile, start=True, stop=True)\
                  .then_inc(pe_done, up("pe", "rope", tag, name))

        def rope_dve(dve, tag, plan, wait_names):
            for i, (name, tile, turn, tab, p0, rows) in enumerate(plan):
                a, b = rope_tmp[2 * (i % 2)][p0:p0 + rows], rope_tmp[2 * (i % 2) + 1][p0:p0 + rows]
                dve.wait_ge(act_done, wait_names(name))
                if i >= 2:
                    dve.wait_ge(dve_done, at("dve", "rope", tag, plan[i - 2][0]))
                dve.tensor_tensor(a, tile, table[p0:p0 + rows, tab, 0, :], ALU.mult).then_inc(dve_done, up("dve"))
                dve.wait_ge(pe_done, at("pe", "rope", tag, name))
                dve.tensor_tensor(b, acc[p0:p0 + rows, i % 2, 0:S], table[p0:p0 + rows, tab, 1, :], ALU.mult)\
                   .then_inc(dve_done, up("dve"))
                settle(dve, "dve", dve_done)
                dve.tensor_tensor(tile, a, b, ALU.add).then_inc(dve_done, up("dve", "rope", tag, name))

        def outproj_pe(pe, tag, items, waits):
            for s, v in waits:
                pe.wait_ge(s, v)
            for h, item in enumerate(items):
                w = w_cols(item, 512)
                pe.wait_ge(*landing(item))
                for m in range(4):
                    for k in range(KD):
                        mm = pe.matmul(accv[:, 4 * h + m, :], w[:, k, m * P:(m + 1) * P], mixT[:, k, :],
                                       start=(k == 0), stop=(k == KD - 1))
                    if m < 3:
                        mm.then_inc(pe_done, up("pe", "out", tag, 4 * h + m))
                mm.then_inc(freed_by_pe, 1)

        def residual_dve(dve, tag, gate_of, waits):
            for m in range(KD):
                dve.wait_ge(*waits[m])
                if gate_of is None:
                    ins = dve.tensor_tensor(xT[:, m, :], accv[:, m, :], xT[:, m, :], ALU.add)
                else:
                    ins = dve.scalar_tensor_tensor(xT[:, m, :], accv[:, m, :], gate_of(m), xT[:, m, :], ALU.mult, ALU.add)
                ins.then_inc(dve_done, up("dve", "residual", tag, m))

        def out_waits(tag, items):
            return [(freed_by_pe, freeing(items[m // 4])) if m % 4 >= 2 else (pe_done, at("pe", "out", tag, m | 1))
                    for m in range(KD)]

        Z = lambda o, *shape: carve(SCR, o, *shape)
        AT2 = 8448

        a_score = {"1": [Z(10640 + 384 * i, 384) for i in range(2)], "2": [Z(AT2 + 384 * i, 384) for i in range(2)]}
        a_prob = {"1": [Z(384 * i, 384) for i in range(2)], "2": [Z(AT2 + 768 + 384 * i, 384) for i in range(2)]}
        a_probT = {"1": [Z(768 + 384 * i, 384) for i in range(2)], "2": [Z(AT2 + 1536 + 384 * i, 384) for i in range(2)]}

        def a_stat(u, what):
            return stat[:, 32 + 8 * (u % 4) + 2 * what:32 + 8 * (u % 4) + 2 * what + 2]

        def spans(kind):
            return ((0, 15), (16, 31)) if kind == "cmp" else ((0, P), (P, 384))

        def att_scores_pe(pe, tag, u, b):
            for s, v in b["ready"]:
                pe.wait_ge(s, v)
            if u >= 2:
                pe.wait_ge(dve_done, at("dve", "masked", tag, u - 2))
            for t, (lo, hi) in enumerate(spans(b["kind"])):
                mm = pe.matmul(wrk[:, u % 2, lo:hi], b["q"][:, t * P:(t + 1) * P], b["k"][:, 0:hi - lo], start=True, stop=True)
            mm.then_inc(pe_done, up("pe", "scores", tag, u))

        def att_turn_pe(pe, tag, u, b):
            pe.wait_ge(dve_done, at("dve", "probs", tag, u))
            if u >= 2:
                pe.wait_ge(act_done, at("act", "probT", tag, u - 2))
            if b["kind"] == "cmp":
                for t, (lo, hi) in enumerate(spans("cmp")):
                    mm = pe.transpose(wrk[0:15, 2 + u % 2, t * P:(t + 1) * P], a_prob[tag[0]][u % 2][:, lo:hi], ident)
            else:
                for j in range(3):
                    mm = pe.transpose(wrk[:, 2 + u % 2, j * P:(j + 1) * P], a_prob[tag[0]][u % 2][:, j * P:(j + 1) * P], ident)
            mm.then_inc(pe_done, up("pe", "turned", tag, u))

        def att_value_pe(pe, tag, u, b, head):
            pe.wait_ge(act_done, at("act", "probT", tag, u))
            if b["first"] and head >= 2:
                pe.wait_ge(dve_done, at("dve", "head out", tag, head - 2))
            p0 = b["p0"]
            o = acc[p0:p0 + HD, head % 2, 0:S]
            if b["kind"] == "cmp":
                mm = pe.matmul(o, b["v"](0), a_probT[tag[0]][u % 2][0:15, 0:S], start=b["first"], stop=b["last"], skip_group_check=True)
            else:
                pe.matmul(o, b["v"](0), a_probT[tag[0]][u % 2][:, 0:S], start=b["first"], stop=False, skip_group_check=True)
                mm = pe.matmul(acc[p0:p0 + HD, head % 2, P:S], b["v"](1), a_probT[tag[0]][u % 2][:, S:S + P],
                               start=False, stop=b["last"], skip_group_check=True)
            mm.then_inc(pe_done, up("pe", "value", tag, u))

        def att_pe(pe, tag, branches):
            att_scores_pe(pe, tag, 0, branches[0])
            heads = head_numbers(branches)
            for u in range(len(branches) + 1):
                if u + 1 < len(branches):
                    att_scores_pe(pe, tag, u + 1, branches[u + 1])
                if u < len(branches):
                    att_turn_pe(pe, tag, u, branches[u])
                if u >= 1:
                    att_value_pe(pe, tag, u - 1, branches[u - 1], heads[u - 1])

        def head_numbers(branches):
            n, outs = -1, []
            for b in branches:
                n += b["first"]
                outs.append(n)
            return outs

        def att_dve(dve, tag, branches):
            heads = head_numbers(branches)

            def masked(u, b):
                dve.wait_ge(pe_done, at("pe", "scores", tag, u))
                for s, v in b["mask_ready"]:
                    dve.wait_ge(s, v)
                if u >= 2:
                    dve.wait_ge(act_done, at("act", "exp", tag, u - 2))
                for t, (lo, hi) in enumerate(spans(b["kind"])):
                    dve.tensor_tensor_reduce(out=a_score[tag[0]][u % 2][:, lo:hi], in0=wrk[:, u % 2, lo:hi], in1=b["mask"][:, lo:hi],
                                             scale=b["scale"], scalar=3 * NEG, op0=ALU.add, op1=ALU.max,
                                             accum_out=a_stat(u, 0)[:, t:t + 1]).then_inc(dve_done, up("dve"))
                settle(dve, "dve", dve_done)
                dve.tensor_scalar(a_stat(u, 1), a_stat(u, 0), -1.0, None, ALU.mult).then_inc(dve_done, up("dve", "masked", tag, u))

            def probs(u, b):
                dve.wait_ge(act_done, at("act", "exp", tag, u))
                if b["kind"] == "cmp":
                    for t, (lo, hi) in enumerate(spans("cmp")):
                        dve.tensor_tensor_reduce(out=a_prob[tag[0]][u % 2][:, lo:hi], in0=a_prob[tag[0]][u % 2][:, lo:hi],
                                                 in1=K("cmp_see")[:, lo:hi], scale=1.0, scalar=0.0, op0=ALU.mult, op1=ALU.add,
                                                 accum_out=a_stat(u, 2)[:, t:t + 1]).then_inc(dve_done, up("dve"))
                    settle(dve, "dve", dve_done)
                    dve.tensor_scalar(a_stat(u, 2), a_stat(u, 2), 1e-30, None, ALU.max).then_inc(dve_done, up("dve"))
                    settle(dve, "dve", dve_done)
                dve.reciprocal(a_stat(u, 3), a_stat(u, 2)).then_inc(dve_done, up("dve"))
                settle(dve, "dve", dve_done)
                for t, (lo, hi) in enumerate(spans(b["kind"])):
                    if b["gate"] is None:
                        ins = dve.tensor_scalar(a_prob[tag[0]][u % 2][:, lo:hi], a_prob[tag[0]][u % 2][:, lo:hi], a_stat(u, 3)[:, t:t + 1],
                                                None, ALU.mult)
                    else:
                        ins = dve.tensor_scalar(a_prob[tag[0]][u % 2][:, lo:hi], a_prob[tag[0]][u % 2][:, lo:hi], a_stat(u, 3)[:, t:t + 1],
                                                b["gate"](t), ALU.mult, ALU.mult)
                    ins.then_inc(dve_done, up("dve", "probs", tag, u) if t else up("dve"))

            masked(0, branches[0])
            for u, b in enumerate(branches):
                if u + 1 < len(branches):
                    masked(u + 1, branches[u + 1])
                probs(u, b)
                if u >= 1 and branches[u - 1]["last"]:
                    head_out(dve, tag, u - 1, branches[u - 1], heads[u - 1])
            head_out(dve, tag, len(branches) - 1, branches[-1], heads[-1])

        def head_out(dve, tag, u, b, head):
            dve.wait_ge(pe_done, at("pe", "value", tag, u))
            dve.tensor_copy(b["place"], acc[b["p0"]:b["p0"] + HD, head % 2, 0:S]).then_inc(dve_done, up("dve", "head out", tag, head))

        def att_act(act, tag, branches):
            def exps(u, b):
                act.wait_ge(dve_done, at("dve", "masked", tag, u))
                if u >= 2:
                    act.wait_ge(pe_done, at("pe", "turned", tag, u - 2))
                for t, (lo, hi) in enumerate(spans(b["kind"])):
                    act.activation(a_prob[tag[0]][u % 2][:, lo:hi], a_score[tag[0]][u % 2][:, lo:hi], ACT.Exp, bias=a_stat(u, 1)[:, t:t + 1],
                                   accum_out=a_stat(u, 2)[:, t:t + 1])\
                       .then_inc(act_done, up("act", "exp", tag, u) if t else up("act"))

            exps(0, branches[0])
            for u, b in enumerate(branches):
                if u + 1 < len(branches):
                    exps(u + 1, branches[u + 1])
                act.wait_ge(pe_done, at("pe", "turned", tag, u))
                if u >= 2:
                    act.wait_ge(pe_done, at("pe", "value", tag, u - 2))
                if b["kind"] == "cmp":
                    ins = act.activation(a_probT[tag[0]][u % 2][0:15, 0:S], wrk[0:15, 2 + u % 2, 0:S], ACT.Copy)
                else:
                    ins = act.activation(a_probT[tag[0]][u % 2], wrk[:, 2 + u % 2, 0:384], ACT.Copy)
                ins.then_inc(act_done, up("act", "probT", tag, u))

        b_q, b_kk, b_f, b_g = Z(0, 3, S), Z(768, 3, S), Z(1536, 3, S), Z(2304, 3, S)
        b_i, c_u, c_v = Z(3072, 2, 384), Z(3840, 2, S), Z(4352, 2, S)
        s_q, s_k, s_iq, s_ik = Z(4864, 3, S), Z(5632, 1, S), Z(5888, 2, S), Z(6400, 1, S)
        s_v, s_iw = Z(6656, 2, HD), Z(6784, 2, 4)
        flat_h = hT[:, :, :].rearrange("p k t -> p (k t)")
        s_mask, s_work = flat_h[:, 0:384], flat_h[:, 384:768]
        s_relu = [flat_h[:, 768:1152], flat_h[:, 1152:1536]]

        def plan1(l):
            items = [("in1", l, i) for i in range(len(IN1))]
            w = [w_cols(items[i], b - a) for i, (a, b) in enumerate(IN1)]

            def cols(i, c, n):
                return lambda k: w[i][:, k, c:c + n]

            def both(tile, scale=1.0):
                return [(tile[HD * p:HD * p + HD, 0, :], ACT.Copy, scale) for p in range(2)]

            plan = []
            plan += [(f"bi{t}", items[4], f"t{t}", cols(4, 0, 384), 384, 0, [(b_i[:, t, :], ACT.Copy, 1.0)]) for t in range(2)]
            plan += [(f"bq{j}", items[2], "f", cols(2, P * j, P), P, 0, [(b_q[:, j, :], ACT.Copy, 1.0)]) for j in range(3)]
            plan += [(f"bf{j}", items[3], "f", cols(3, P * j, P), P, 0,
                      [(b_f[:, j, :], ACT.Sigmoid, 1.0), (b_kk[:, j, :], ACT.Sigmoid, -1.0)]) for j in range(3)]
            plan += [(f"aq{j}", items[0], "f", cols(0, P * j, P), P, 0, [(s_q[:, j, :], ACT.Copy, 1.0)]) for j in range(3)]
            plan += [("ak", items[0], "f", cols(0, 384, HD), HD, 0, both(s_k))]
            plan += [(f"av{t}", items[0], f"t{t}", cols(0, 448, HD), HD, 0, [(s_v[:, t, :], ACT.Copy, 1.0)]) for t in range(2)]
            plan += [(f"iq{j}", items[1], "f", cols(1, P * j, P), P, 0, [(s_iq[:, j, :], ACT.Copy, 1.0)]) for j in range(2)]
            plan += [("ik", items[1], "f", cols(1, 256, HD), HD, 0, both(s_ik))]
            plan += [(f"iw{t}", items[1], f"t{t}", cols(1, 320, 4), 4, 0, [(s_iw[:, t, :], ACT.Copy, 0.5)]) for t in range(2)]
            plan += [(f"bg{j}", items[5], "f", cols(5, P * j, P), P, 0, [(b_g[:, j, :], ACT.Silu, 1.0)]) for j in range(3)]
            plan += [(f"cu{j}", items[6], "f", cols(6, P * j, P), P, 0, [(c_u[:, j, :], ACT.Gelu, 1.0)]) for j in range(2)]
            plan += [(f"cv{t}", items[6], f"t{t}", cols(6, 256, 256), 256, 0, [(c_v[:, t, :], ACT.Gelu, 1.0)]) for t in range(2)]
            return plan

        def rope1(l):
            tiles = [("iq0", s_iq[:, 0, :]), ("iq1", s_iq[:, 1, :]), ("ik", s_ik[:, 0, :])]
            tiles += [(f"aq{j}", s_q[:, j, :]) for j in range(3)] + [("ak", s_k[:, 0, :])]
            return [(name, tile, "turn64", 0, 0, P) for name, tile in tiles]

        def index_pe(pe, l):
            pe.wait_ge(dve_done, at("dve", "states", l, 2))
            for h in range(4):
                p0 = HD * (h % 2)
                q, k = s_iq[p0:p0 + HD, h // 2, :], s_ik[p0:p0 + HD, 0, :]
                pe.matmul(wrk[:, h, 0:P], q[:, T0], k[:, T0], start=True, stop=True)
                pe.matmul(wrk[:, h, P:384], q[:, T1], k[:, 0:S], start=True, stop=True)\
                  .then_inc(pe_done, up("pe", "index", l, h))

        def index_act(act, l):
            for h in range(4):
                act.wait_ge(pe_done, at("pe", "index", l, h))
                if h >= 2:
                    act.wait_ge(dve_done, at("dve", "index", l, h - 2))
                act.activation(s_relu[h % 2], wrk[:, h, 0:384], ACT.Relu, scale=IDX_SCALE).then_inc(act_done, up("act", "index", l, h))

        IDX_SCALE = float(HD) ** -0.5
        QT = ((0, P), (P, 384))

        def index_dve(dve, l):
            for h in range(4):
                dve.wait_ge(act_done, at("act", "index", l, h))
                for t, (lo, hi) in enumerate(QT):
                    if h == 0:
                        ins = dve.tensor_scalar(s_work[:, lo:hi], s_relu[0][:, lo:hi], s_iw[:, t, 0:1], None, ALU.mult)
                    else:
                        ins = dve.scalar_tensor_tensor(s_work[:, lo:hi], s_relu[h % 2][:, lo:hi], s_iw[:, t, h:h + 1],
                                                       s_work[:, lo:hi], ALU.mult, ALU.add)
                    ins.then_inc(dve_done, up("dve", "index", l, h) if t else up("dve"))
                settle(dve, "dve", dve_done)
            dve.tensor_tensor(s_work, s_work, K("causal"), ALU.add).then_inc(dve_done, up("dve"))
            for _ in range(TOPK // 8):
                settle(dve, "dve", dve_done)
                for t, (lo, hi) in enumerate(QT):
                    dve.max(stat[:, 8 * t:8 * t + 8], s_work[:, lo:hi]).then_inc(dve_done, up("dve"))
                settle(dve, "dve", dve_done)
                for t, (lo, hi) in enumerate(QT):
                    dve.match_replace(s_work[:, lo:hi], stat[:, 8 * t:8 * t + 8], s_work[:, lo:hi], TAKEN)\
                       .then_inc(dve_done, up("dve"))
            settle(dve, "dve", dve_done)
            dve.tensor_scalar(s_mask, s_work, TAKEN / 2, NEG, ALU.is_gt, ALU.mult).then_inc(dve_done, up("dve"))
            settle(dve, "dve", dve_done)
            dve.tensor_tensor(s_mask, s_mask, K("causal"), ALU.add).then_inc(dve_done, up("dve", "mask", l))

        def branches1(l):
            out = []
            for h in range(6):
                p0, j = HD * (h % 2), h // 2
                out.append(dict(q=s_q[p0:p0 + HD, j, :], k=s_k[p0:p0 + HD, 0, :], v=lambda t: s_v[:, t, :], mask=s_mask,
                                kind="causal", scale=float(HD) ** -0.5, gate=None, first=True, last=True, p0=p0,
                                place=mixT[p0:p0 + HD, j, :],
                                ready=[(dve_done, at("dve", "rope", ("1", l), "ak")), (act_done, at("act", "index", l, 3))] if h == 0 else [],
                                mask_ready=[(dve_done, at("dve", "mask", l))] if h == 0 else []))
            return out

        def gmlp_parts(l):
            s = slot_of(("gmlp", l))
            return (s[:, 0:256], s[:, 256:512], s[:, 512:1024].rearrange("p (g s) -> p g s", g=4), s[0:1, 1024:1536],
                    s[:, 1536:2048].rearrange("p (g t) -> p g t", g=4))

        def gmlp_pe(pe, l):
            g_row, b_row, ws, bs, wsT = gmlp_parts(l)
            pe.wait_ge(*landing(("gmlp", l)))
            pe.wait_ge(act_done, now_act_read(l))
            for i in range(4):
                mm = pe.transpose(wrk[:, 0, i * P:(i + 1) * P], ws[:, i, :], ident)
            mm.then_inc(pe_done, up("pe", "ws turned", l))
            pe.wait_ge(dve_done, at("dve", "wsT", l))
            pe.wait_ge(dve_done, at("dve", "cv", l))
            for j in range(2):
                for p in range(2):
                    i, p0 = 2 * j + p, HD * p
                    for n in range(2):
                        o = acc[p0:p0 + HD, j, n * P:(n + 1) * P]
                        pe.matmul(o, c_v[:, n, i * HD:(i + 1) * HD], wsT[:, i, :], start=True, stop=False, skip_group_check=True)
                        mm = pe.matmul(o, ones[0:1, 0:HD], bs[:, i * P:(i + 1) * P], start=False, stop=True, skip_group_check=True)
                if j == 0:
                    mm.then_inc(pe_done, up("pe", "mixed", l, j))
                else:
                    mm.then_inc(freed_by_pe, 1)

        def now_act_read(l):
            return at("act", "probT", ("1", l), 5)

        def gmlp_dve(dve, l):
            g_row, b_row, ws, bs, wsT = gmlp_parts(l)
            dve.wait_ge(act_done, at("act", "proj", ("1", l), "cv1"))
            for t in range(2):
                dve.bn_stats(stat[:, 8 * t:8 * t + 6], c_v[:, t, :]).then_inc(dve_done, up("dve"))
            settle(dve, "dve", dve_done)
            for t in range(2):
                dve.bn_aggr(stat[:, 16 + 2 * t:18 + 2 * t], stat[:, 8 * t:8 * t + 6]).then_inc(dve_done, up("dve"))
            settle(dve, "dve", dve_done)
            for t in range(2):
                dve.tensor_scalar(stat[:, 20 + t:21 + t], stat[:, 17 + 2 * t:18 + 2 * t], EPS, None, ALU.add)\
                   .then_inc(dve_done, up("dve", "cv variance", l) if t else up("dve"))
            inverse_root_dve(dve, ("cv root", l), stat[:, 20:22])
            settle(dve, "dve", dve_done)
            for t in range(2):
                dve.tensor_scalar(c_v[:, t, :], c_v[:, t, :], stat[:, 16 + 2 * t:17 + 2 * t], stat[:, 20 + t:21 + t],
                                  ALU.subtract, ALU.mult).then_inc(dve_done, up("dve"))
            dve.wait_ge(*landing(("gmlp", l)))
            settle(dve, "dve", dve_done)
            dve.tensor_tensor(c_v, c_v, g_row.unsqueeze(1).broadcast_to([P, 2, S]), ALU.mult).then_inc(dve_done, up("dve"))
            settle(dve, "dve", dve_done)
            dve.tensor_tensor(c_v, c_v, b_row.unsqueeze(1).broadcast_to([P, 2, S]), ALU.add).then_inc(dve_done, up("dve", "cv", l))
            dve.wait_ge(pe_done, at("pe", "ws turned", l))
            dve.tensor_tensor(wsT, wrk[:, 0, :].rearrange("p (g t) -> p g t", g=4),
                              K("upper").unsqueeze(1).broadcast_to([P, 4, P]), ALU.mult).then_inc(dve_done, up("dve", "wsT", l))
            for j in range(2):
                if j == 0:
                    dve.wait_ge(pe_done, at("pe", "mixed", l, 0))
                else:
                    dve.wait_ge(freed_by_pe, freeing(("gmlp", l)))
                dve.tensor_tensor(mixT[:, 6 + j, :], acc[:, j, 0:S], c_u[:, j, :], ALU.mult).then_inc(dve_done, up("dve", "c out", l, j))

        def grid(v):
            return v.rearrange("p a (b c) -> p (a b) c", c=C)

        NP3 = 3 * NB
        r_w = [b_kk, Z(6800, 3, S)]
        r_kdec, r_v = Z(7568, 3, S), Z(8336, 3, S)
        r_qw = [Z(9104, 768), Z(9872, 768)]
        r_t, r_p, r_o = Z(10640, 3, S), Z(11408, 3, S), mixT[:, 3:6, :]
        r_state = Z(6800, 3, NB * HD).rearrange("p a (b v) -> p a b v", v=HD)
        r_kT = Z(10640, 6, P)
        r_pick = [Z(512 * i, P // C, HD) for i in range(3)]
        r_whole = stat[:, 64:64 + NP3]

        def band(j):
            n = C - j
            return n, r_qw[j % 2][:, 0:NP3 * n].rearrange("p (a c) -> p a c", c=n)

        def band_psum(j, half):
            n = C - j
            return wrk[:, 2 * (j % 2) + half, 0:24 * n]

        wrkv = wrk[:, :, :].rearrange("p b (h t) -> p (b h) t", t=S)

        def turn_values_pe(pe, l):
            pe.wait_ge(act_done, at("act", "proj", ("1", l), "bi1"))
            for a in range(3):
                for t in range(2):
                    mm = pe.transpose(wrkv[:, a, t * P:(t + 1) * P], b_i[:, t, a * P:(a + 1) * P], ident)
            mm.then_inc(pe_done, up("pe", "v turned", l))

        def band_pe(pe, l, j):
            n, qw = band(j)
            if j == 0:
                pe.wait_ge(act_done, at("act", "v", l))
            pe.wait_ge(dve_done, at("dve", "qw", l, j))
            if j >= 2:
                pe.wait_ge(dve_done, at("dve", "band", l, j - 2))
            for half in range(2):
                mm = pe.matmul(band_psum(j, half), headsum, r_qw[j % 2][:, 24 * n * half:24 * n * (half + 1)],
                               start=True, stop=True)
            mm.then_inc(pe_done, up("pe", "band", l, j))

        def turn_keys_pe(pe, l):
            pe.wait_ge(act_done, at("act", "kdec", l))
            if l == 0:
                pe.wait_ge(dve_done, at("dve", "mods", 0, 9))
            for a in range(3):
                for t in range(2):
                    mm = pe.transpose(accv[:, a, t * P:(t + 1) * P], r_kdec[:, a, t * P:(t + 1) * P], ident)
            mm.then_inc(pe_done, up("pe", "k turned", l))

        def kv_pe(pe, l):
            pe.wait_ge(act_done, at("act", "kT", l))
            pe.wait_ge(act_done, at("act", "proj", ("1", l), "cv1"))
            pe.wait_ge(dve_done, at("dve", "band", l, C - 1))
            n = 0
            for a in range(3):
                for h in range(2):
                    for t in range(2):
                        o = wrk[HD * h:HD * h + HD, 2 * a + t, :] if a < 2 else acc[HD * h:HD * h + HD, 2 + t, :]
                        pe.wait_ge(dve_done, at("dve", "pick", l, n))
                        pe.matmul(o, r_kT[:, 2 * a + t, HD * h:HD * h + HD], r_pick[n % 3].rearrange("p b v -> p (b v)"),
                                  start=True, stop=True).then_inc(pe_done, up("pe", "kv", l, n))
                        n += 1

        def inter_pe(pe, l):
            for a in range(3):
                pe.wait_ge(dve_done, at("dve", "states", l, 2))
                for b in range(NB):
                    for h in range(2):
                        rows = slice(HD * h, HD * h + HD)
                        mm = pe.matmul(accv[rows, 4 + a, b * C:(b + 1) * C], r_state[rows, a, b, :],
                                       r_p[rows, a, b * C:(b + 1) * C], start=True, stop=True, skip_group_check=True)
                mm.then_inc(pe_done, up("pe", "inter", l, a))

        def head_norm_pe(pe, l):
            pe.wait_ge(act_done, at("act", "o squares", l))
            for half in range(2):
                mm = pe.matmul(wrk[:, half, 0:384], headsum, r_qw[1][:, 384 * half:384 * (half + 1)], start=True, stop=True)
            mm.then_inc(pe_done, up("pe", "o sums", l))

        def turned_values_act(act, l):
            act.wait_ge(pe_done, at("pe", "v turned", l))
            act.activation(r_v, wrkv[:, 0:3, :], ACT.Copy).then_inc(act_done, up("act", "v", l))

        def block_keys_act(act, l, j):
            act.wait_ge(dve_done, at("dve", "w", l, j))
            act.activation(grid(r_kdec)[:, :, C - 1 - j:C - j], grid(r_w[j % 2])[:, :, C - 1:C], ACT.Copy)\
               .then_inc(act_done, up("act", "kdec", l) if j == C - 1 else up("act", "kdec part", l, j))

        def turned_keys_act(act, l):
            act.wait_ge(pe_done, at("pe", "k turned", l))
            act.wait_ge(dve_done, at("dve", "band end", l))
            act.activation(r_kT.rearrange("p (a t) d -> p a (t d)", t=2), accv[:, 0:3, :], ACT.Copy).then_inc(act_done, up("act", "kT", l))

        def head_norm_act(act, l):
            act.wait_ge(dve_done, at("dve", "o", l))
            act.activation(r_qw[1], r_o.rearrange("p a t -> p (a t)"), ACT.Square).then_inc(act_done, up("act", "o squares", l))
            root_act(act, at("dve", "o mean square", l), ("o root", l), r_t)

        def gates_dve(dve, l):
            dve.tensor_scalar(stat[:, 24:27], lower[:, l, :], -1.0, 1.0, ALU.mult, ALU.add).then_inc(dve_done, up("dve"))
            settle(dve, "dve", dve_done)
            for a in range(3):
                dve.wait_ge(act_done, at("act", "proj", ("1", l), f"bf{a}"))
                dve.tensor_scalar(b_f[:, a, :], b_f[:, a, :], stat[:, 24 + a:25 + a], lower[:, l, a:a + 1], ALU.mult, ALU.add)\
                   .then_inc(dve_done, up("dve"))
                dve.tensor_scalar(b_kk[:, a, :], b_kk[:, a, :], stat[:, 24 + a:25 + a], None, ALU.mult)\
                   .then_inc(dve_done, up("dve", "w", l, 0) if a == 2 else up("dve"))
            settle(dve, "dve", dve_done)
            dve.tensor_copy(grid(r_p)[:, :, 0:1], grid(b_f)[:, :, 0:1]).then_inc(dve_done, up("dve"))

        def weigh_dve(dve, l, j):
            f, q, p = grid(b_f), grid(b_q), grid(r_p)
            n, qw = band(j)
            if j:
                settle(dve, "dve", dve_done)
                if j >= 2:
                    dve.wait_ge(act_done, at("act", "kdec part", l, j - 2))
                dve.tensor_tensor(grid(r_w[j % 2])[:, :, j:C], grid(r_w[(j - 1) % 2])[:, :, j - 1:C - 1], f[:, :, j:C], ALU.mult)\
                   .then_inc(dve_done, up("dve", "w", l, j))
                dve.tensor_tensor(p[:, :, j:j + 1], p[:, :, j - 1:j], f[:, :, j:j + 1], ALU.mult).then_inc(dve_done, up("dve"))
                settle(dve, "dve", dve_done)
            if j >= 2:
                dve.wait_ge(pe_done, at("pe", "band", l, j - 2))
            dve.tensor_tensor(qw, q[:, :, j:C], grid(r_w[j % 2])[:, :, j:C], ALU.mult).then_inc(dve_done, up("dve", "qw", l, j))

        def band_dve(dve, l, j):
            v = grid(r_v)
            if j == 0:
                dve.wait_ge(act_done, at("act", "v", l))
            dve.wait_ge(pe_done, at("pe", "band", l, j))
            if j == C - 1:
                settle(dve, "dve", dve_done)
            n = C - j
            o = grid(r_o if j == 0 else r_t)[:, :, j:C]
            for half in range(2):
                dve.tensor_tensor(o[:, 24 * half:24 * half + 24, :], band_psum(j, half).rearrange("p (a c) -> p a c", c=n),
                                  v[:, 24 * half:24 * half + 24, 0:n], ALU.mult)\
                   .then_inc(dve_done, up("dve", "band", l, j) if half else up("dve"))
            if j:
                settle(dve, "dve", dve_done)
                dve.tensor_tensor(grid(r_o)[:, :, j:C], grid(r_o)[:, :, j:C], o, ALU.add)\
                   .then_inc(dve_done, up("dve", "band end", l) if j == C - 1 else up("dve"))

        def picks_dve(dve, l):
            settle(dve, "dve", dve_done)
            dve.tensor_copy(r_whole, grid(r_p)[:, :, C - 1:C].rearrange("p a c -> p (a c)")).then_inc(dve_done, up("dve"))
            settle(dve, "dve", dve_done)
            dve.tensor_tensor(r_p, r_p, b_q, ALU.mult).then_inc(dve_done, up("dve"))
            settle(dve, "dve", dve_done)
            dve.wait_ge(act_done, at("act", "kdec", l))
            n = 0
            for a in range(3):
                for h in range(2):
                    for t in range(2):
                        if n >= 3:
                            dve.wait_ge(pe_done, at("pe", "kv", l, n - 3))
                        dve.tensor_tensor(r_pick[n % 3], K("blocks").unsqueeze(2).broadcast_to([P, P // C, HD]),
                                          b_i[:, t, (2 * a + h) * HD:(2 * a + h + 1) * HD].unsqueeze(1).broadcast_to([P, P // C, HD]),
                                          ALU.mult).then_inc(dve_done, up("dve", "pick", l, n))
                        n += 1

        def states_dve(dve, l):
            dve.wait_ge(pe_done, at("pe", "k turned", l))
            dve.memset(r_state[:, :, 0, :], 0.0).then_inc(dve_done, up("dve"))
            dve.wait_ge(pe_done, at("pe", "kv", l, 11))
            for b in range(1, NB):
                settle(dve, "dve", dve_done)
                for a in range(3):
                    bank = wrk[:, 2 * a + (b - 1) // 8, :] if a < 2 else acc[:, 2 + (b - 1) // 8, :]
                    c = (b - 1) % 8
                    dve.scalar_tensor_tensor(r_state[:, a, b, :], r_state[:, a, b - 1, :], r_whole[:, a * NB + b - 1:a * NB + b],
                                             bank[:, c * HD:(c + 1) * HD], ALU.mult, ALU.add)\
                       .then_inc(dve_done, up("dve", "states", l, a) if b == NB - 1 else up("dve"))

        def head_norm_dve(dve, l):
            for a in range(3):
                dve.wait_ge(pe_done, at("pe", "inter", l, max(a, 1)))
                dve.tensor_tensor(r_o[:, a, :], r_o[:, a, :], accv[:, 4 + a, :], ALU.add)\
                   .then_inc(dve_done, up("dve", "o", l) if a == 2 else up("dve"))
            dve.wait_ge(pe_done, at("pe", "o sums", l))
            rt = r_t.rearrange("p a t -> p (a t)").rearrange("p (h n) -> p h n", h=2)
            dve.tensor_scalar(rt, wrk[:, 0:2, 0:384], 1.0 / HD, EPS, ALU.mult, ALU.add).then_inc(dve_done, up("dve", "o mean square", l))
            inverse_root_dve(dve, ("o root", l), r_t)
            settle(dve, "dve", dve_done)
            dve.tensor_tensor(r_o, r_o, r_t, ALU.mult).then_inc(dve_done, up("dve"))
            settle(dve, "dve", dve_done)
            dve.scalar_tensor_tensor(mixT[:, 3:6, :], r_o, column("onorm", l), b_g, ALU.mult, ALU.mult)\
               .then_inc(dve_done, up("dve", "b out", l))

        F_ACT = Z(0, 8, S)
        F_SIL = Z(2048, 4, S)
        def tile_base(kind, l):
            return {"dense": 0, "moe": F_DENSE // P, "mlp": F_DENSE // P + NE * UP_TILES + l * (D_FF // P)}[kind]

        def group_base(kind, l):
            n_d, n_e, n_m = (len(ffn_groups(w)) for w in (F_DENSE, F_EXPERT, D_FF))
            return {"dense": 0, "moe": n_d, "mlp": n_d + NE * n_e + l * n_m}[kind]

        def dense_items(g):
            return ("gate", g), ("up", g), ("down", g)

        def ffn_up_pe(pe, g, width, items, base, gbase):
            f, n = ffn_groups(width)[g]
            gate, up_ = items
            for j in range(n // P):
                i = base + 4 * g + j
                if i >= 3:
                    pe.wait_ge(ffn_act, i - 2)
                for item, lo in ((gate, 0), (up_, S)):
                    if item is None:
                        continue
                    if j == 0:
                        pe.wait_ge(*landing(item))
                    w = w_cols(item, n)
                    for k in range(KD):
                        mm = pe.matmul(wrk[:, i % 3, lo:lo + S], w[:, k, j * P:(j + 1) * P], hT[:, k, :],
                                       start=(k == 0), stop=(k == KD - 1))
                    if item is gate and j == n // P - 1:
                        mm.then_inc(freed_by_pe, 1)
                mm.then_inc(ffn_up, 1)

        def ffn_down_pe(pe, g, width, item, base, gbase, tag):
            groups = ffn_groups(width)
            f, n = groups[g]
            w = slot_of(item)[:, 0:n * KD].rearrange("p (j d) -> p j d", d=D)
            pe.wait_ge(*landing(item))
            pe.wait_ge(ffn_act, base + 4 * g + n // P)
            for m in range(KD):
                for j in range(n // P):
                    mm = pe.matmul(accv[:, m, :], w[:, j, m * P:(m + 1) * P], F_ACT[:, 4 * (g % 2) + j, :],
                                   start=(g == 0 and j == 0 and m % 2 == 0), stop=(g == len(groups) - 1 and j == n // P - 1),
                                   skip_group_check=True)
            mm.then_inc(freed_by_pe, 1)

        def dense_pe(pe):
            n = len(ffn_groups(F_DENSE))
            pe.wait_ge(act_done, at("act", "h", ("ffn", 0), KD - 1))
            for g in range(n + 1):
                if g < n:
                    ffn_up_pe(pe, g, F_DENSE, dense_items(g)[:2], 0, 0)
                if g >= 1:
                    ffn_down_pe(pe, g - 1, F_DENSE, dense_items(g - 1)[2], 0, 0, "dense")
                if g < n:
                    for i in dense_ada(g):
                        ada_pe(pe, *DENSE_ADA[i])

        def dense_act(act):
            for i in range(F_DENSE // P):
                act.wait_ge(ffn_up, i + 1)
                if i >= 4:
                    act.wait_ge(ffn_act, i - 3)
                act.activation(F_SIL[:, i % 4, :], wrk[:, i % 3, 0:S], ACT.Silu).then_inc(ffn_silu, 1)

        def dense_dve(dve):
            groups = ffn_groups(F_DENSE)
            for g, (f, n) in enumerate(groups):
                if g >= 2:
                    dve.wait_ge(freed_by_pe, freeing(("down", g - 2)))
                for j in range(n // P):
                    i = 4 * g + j
                    dve.wait_ge(ffn_silu, i + 1)
                    dve.tensor_tensor(F_ACT[:, 4 * (g % 2) + j, :], F_SIL[:, i % 4, :], wrk[:, i % 3, S:2 * S], ALU.mult)\
                       .then_inc(ffn_act, 1)
                for i in dense_ada(g):
                    ada_dve(dve, *DENSE_ADA[i])
            ada_end_dve(dve, 1, 0, 11)
            ada_end_dve(dve, 0, 10, 11)
            dve.wait_ge(freed_by_pe, freeing(("down", len(groups) - 1)))
            for m in range(KD):
                dve.scalar_tensor_tensor(xT[:, m, :], accv[:, m, :], mods[:, 0, 40 + m:41 + m], xT[:, m, :], ALU.mult, ALU.add)\
                   .then_inc(dve_done, up("dve", "residual", ("ffn", 0), m))

        def out_items(kind, l):
            return [(kind, l, 0), (kind, l, 1)]

        def mod_col(l, o):
            return lambda k: mods[:, l, o + k:o + k + 1]

        def gain_col(i):
            return lambda k: gain[:, i, k:k + 1]

        def x_ready(l):
            if l == 0:
                return [(act_done, at("act", "x"))]
            return [(dve_done, at("dve", "residual", ("ffn", 0), KD - 1))]

        def act_from(wait_names):
            return lambda name: at("act", "proj", wait_names, name)

        PLAN1_TILES, FIRST_BAND = 26, 8
        ADA_STEPS_DVE = {1: 6, 4: 7, 7: 8, 10: 9}
        ADA_STEPS_PE = {3: 6, 6: 7, 9: 8, 12: 9}

        def block1_pe(pe, l):
            tag = ("1", l)
            if l == 0:
                for i in range(2):
                    ada_pe(pe, 0, i)
            norm_pe(pe, ("mix", l))
            if l == 0:
                for i in range(2, 4):
                    ada_pe(pe, 0, i)
            pe.wait_ge(act_done, at("act", "h", ("mix", l), KD - 1))
            plan = plan1(l)
            assert len(plan) == PLAN1_TILES
            for i in range(PLAN1_TILES):
                project_pe(pe, tag, plan, i)
                if i in (FIRST_BAND - 2, FIRST_BAND - 1) and l == 0:
                    ada_pe(pe, 0, i - FIRST_BAND + 6)
                if i == FIRST_BAND - 1:
                    turn_values_pe(pe, l)
                j = i - FIRST_BAND
                if 0 <= j < C:
                    band_pe(pe, l, j)
                    if l == 0 and j in ADA_STEPS_PE:
                        ada_pe(pe, 0, ADA_STEPS_PE[j])
            turn_keys_pe(pe, l)
            pe.wait_ge(act_done, at("act", "kT", l))
            kv_pe(pe, l)
            rope_pe(pe, tag, rope1(l), act_from(tag))
            index_pe(pe, l)
            inter_pe(pe, l)
            att_pe(pe, tag, branches1(l))
            gmlp_pe(pe, l)
            head_norm_pe(pe, l)
            outproj_pe(pe, tag, out_items("out1", l), [(dve_done, at("dve", "b out", l))])
            norm_pe(pe, ("ffn", l))

        def block1_act(act, l):
            tag = ("1", l)
            norm_act(act, ("mix", l), x_ready(l), gain_col(2 * l), mod_col(l, 0), None, [(dve_done, at("dve", "gain", l, 0))])
            plan = plan1(l)
            for i in range(PLAN1_TILES):
                project_act(act, tag, plan, i)
                if i == 3 and l == 0:
                    tables_act(act)
                if i == FIRST_BAND - 1:
                    turned_values_act(act, l)
                j = i - FIRST_BAND
                if 0 <= j < C:
                    block_keys_act(act, l, j)
            turned_keys_act(act, l)
            index_act(act, l)
            att_act(act, tag, branches1(l))
            root_act(act, at("dve", "cv variance", l), ("cv root", l), stat[:, 20:22])
            head_norm_act(act, l)
            norm_act(act, ("ffn", l), [(dve_done, at("dve", "residual", ("mix", l), KD - 1))], gain_col(2 * l + 1), mod_col(l, 24),
                     None, [(dve_done, at("dve", "gain", l, 1))])

        def block1_dve(dve, l):
            tag = ("1", l)
            if l == 0:
                ada_dve(dve, 0, 0)
                vec_dve(dve)
                ada_dve(dve, 0, 1)
            norm_dve(dve, ("mix", l))
            if l == 0:
                ada_dve(dve, 0, 2)
                ada_dve(dve, 0, 3)
                ada_end_dve(dve, 0, 0, 3)
                tables_dve(dve)
                ada_dve(dve, 0, 4)
                ada_dve(dve, 0, 5)
            gates_dve(dve, l)
            weigh_dve(dve, l, 0)
            for j in range(C):
                if j + 1 < C:
                    weigh_dve(dve, l, j + 1)
                band_dve(dve, l, j)
                if l == 0 and j in ADA_STEPS_DVE:
                    ada_dve(dve, 0, ADA_STEPS_DVE[j])
            if l == 0:
                ada_end_dve(dve, 0, 4, 9)
            picks_dve(dve, l)
            rope_dve(dve, tag, rope1(l), act_from(tag))
            states_dve(dve, l)
            index_dve(dve, l)
            att_dve(dve, tag, branches1(l))
            gmlp_dve(dve, l)
            head_norm_dve(dve, l)
            residual_dve(dve, ("mix", l), mod_col(l, 16), out_waits(tag, out_items("out1", l)))
            norm_dve(dve, ("ffn", l))

        m_h = Z(3072, 2, D)
        m_rows = Z(5120, 2, D)
        m_pick, m_wpick, m_wpickT = Z(7168, 2, S), Z(7680, 2, S), Z(8192, 2, S)
        m_logit, m_gate, m_pos, m_sel = (Z(8704 + 16 * i, 2, NE) for i in range(4))
        m_cmp = [Z(8800 + 64 * i, NE, NE) for i in range(4)]
        m_part = Z(9072, 2, 4)
        m_many = sb("m_many", [1, NE], I32)
        y_sum = mixT
        MOE = tile_base("moe", 0)
        flat_mix = mixT[:, :, :].rearrange("p k t -> p (k t)")
        flat_acc = acc[:, :, :].rearrange("p b n -> p (b n)")

        def route_pe(pe):
            pe.wait_ge(act_done, at("act", "h", ("ffn", 1), KD - 1))
            pe.wait_ge(*landing(("router",)))
            wr = slot_of(("router",))[:, 0:64].rearrange("p (k e) -> p k e", k=KD)
            for t in range(2):
                for k in range(KD):
                    mm = pe.matmul(wrk[:, 3, t * NE:(t + 1) * NE], hT[:, k, t * P:(t + 1) * P], wr[:, k, :],
                                   start=(k == 0), stop=(k == KD - 1))
            mm.then_inc(freed_by_pe, 1)
            for t in range(2):
                for k in range(KD):
                    mm = pe.transpose(flat_acc[:, t * D + k * P:t * D + (k + 1) * P], hT[:, k, t * P:(t + 1) * P], ident)
            mm.then_inc(pe_done, up("pe", "h turned"))
            pe.wait_ge(dve_done, at("dve", "selected"))
            pe.matmul(wrk[:, 2, 0:NE], K("upper"), m_sel[:, 0, :], start=True, stop=True)
            pe.matmul(wrk[:, 2, NE:2 * NE], ones, m_sel[:, 0, :], start=True, stop=False)
            pe.matmul(wrk[:, 2, NE:2 * NE], K("upper"), m_sel[:, 1, :], start=False, stop=True)
            pe.matmul(wrk[0:1, 2, 2 * NE:3 * NE], ones[:, 0:1], m_sel[:, 0, :], start=True, stop=False)
            pe.matmul(wrk[0:1, 2, 2 * NE:3 * NE], ones[:, 0:1], m_sel[:, 1, :], start=False, stop=True).then_inc(pe_done, up("pe", "counted"))

        def route_act(act):
            act.wait_ge(pe_done, at("pe", "h turned"))
            act.activation(m_h.rearrange("p t d -> p (t d)"), flat_acc, ACT.Copy).then_inc(act_done, up("act", "h tokens"))
            act.wait_ge(dve_done, at("dve", "logits less max"))
            act.activation(m_gate, m_gate, ACT.Exp).then_inc(act_done, up("act", "router exp"))

        def route_dve(dve):
            dve.wait_ge(freed_by_pe, freeing(("router",)))
            dve.tensor_copy(m_logit, wrk[:, 3, 0:2 * NE].rearrange("p (t e) -> p t e", t=2)).then_inc(dve_done, up("dve"))
            settle(dve, "dve", dve_done)
            for t in range(2):
                own = m_logit[:, t, :].unsqueeze(2).broadcast_to([P, NE, NE])
                other = m_logit[:, t, :].unsqueeze(1).broadcast_to([P, NE, NE])
                dve.tensor_tensor(m_cmp[t], other, own, ALU.is_gt).then_inc(dve_done, up("dve"))
                dve.tensor_tensor(m_cmp[2 + t], other, own, ALU.is_equal).then_inc(dve_done, up("dve"))
            settle(dve, "dve", dve_done)
            for t in range(2):
                dve.tensor_tensor(m_cmp[2 + t], m_cmp[2 + t], K("before").rearrange("p (a b) -> p a b", a=NE), ALU.mult)\
                   .then_inc(dve_done, up("dve"))
            settle(dve, "dve", dve_done)
            for t in range(2):
                dve.tensor_tensor(m_cmp[t], m_cmp[t], m_cmp[2 + t], ALU.add).then_inc(dve_done, up("dve"))
                dve.tensor_reduce(m_part[:, t, 0:1], m_logit[:, t, :], AX, ALU.max).then_inc(dve_done, up("dve"))
            settle(dve, "dve", dve_done)
            for t in range(2):
                dve.tensor_reduce(m_sel[:, t, :], m_cmp[t], AX, ALU.add).then_inc(dve_done, up("dve"))
                dve.tensor_scalar(m_gate[:, t, :], m_logit[:, t, :], m_part[:, t, 0:1], None, ALU.subtract)\
                   .then_inc(dve_done, up("dve", "logits less max") if t else up("dve"))
            settle(dve, "dve", dve_done)
            dve.tensor_scalar(m_sel, m_sel, 1.5, None, ALU.is_lt).then_inc(dve_done, up("dve", "selected"))
            dve.wait_ge(act_done, at("act", "router exp"))
            settle(dve, "dve", dve_done)
            dve.tensor_tensor(m_gate, m_gate, m_sel, ALU.mult).then_inc(dve_done, up("dve"))
            settle(dve, "dve", dve_done)
            dve.tensor_reduce(m_part[:, :, 1:2].rearrange("p a b -> p (a b)"), m_gate, AX, ALU.add).then_inc(dve_done, up("dve"))
            settle(dve, "dve", dve_done)
            dve.reciprocal(m_part[:, :, 2:3], m_part[:, :, 1:2]).then_inc(dve_done, up("dve"))
            settle(dve, "dve", dve_done)
            for t in range(2):
                dve.tensor_scalar(m_gate[:, t, :], m_gate[:, t, :], m_part[:, t, 2:3], None, ALU.mult).then_inc(dve_done, up("dve"))
            dve.wait_ge(pe_done, at("pe", "counted"))
            dve.tensor_tensor(m_pos, wrk[:, 2, 0:2 * NE].rearrange("p (t e) -> p t e", t=2), m_sel, ALU.mult).then_inc(dve_done, up("dve"))
            dve.tensor_scalar(m_many[:, :], wrk[0:1, 2, 2 * NE:3 * NE], P + 0.5, None, ALU.is_gt).then_inc(dve_done, up("dve"))
            settle(dve, "dve", dve_done)
            dve.tensor_scalar(m_pos, m_pos, -1.0, None, ALU.add).then_inc(dve_done, up("dve", "routed"))
            dve.memset(mixT[:, :, :], 0.0).then_inc(share_added, 1)

        def by_count(eng, e, body):
            many = eng.value_load(m_many[0:1, bass.ds(e, 1)], min_val=0, max_val=1)
            with eng.If(many == 0):
                body(e, 1)
            with eng.Else():
                body(e, 2)

        def experts_pe(pe):
            groups = ffn_groups(F_EXPERT)
            base = MOE

            def arrive(e, item):
                n = PLACE[item]
                mine = (n - FIRST_EXPERT) // SLOTS + 1
                pe.wait_ge(landed[n % SLOTS], e * (16 * (len(EXPERTS) // SLOTS)) + (at_experts[n % SLOTS] + 16 * mine))

            def rise(e, g, width):
                for j in range(4):
                    i = base + 4 * g + j
                    pe.wait_ge(ffn_act, e * UP_TILES + (i - 3))
                    for item, lo in ((("egate", g), 0), (("eup", g), S)):
                        if j == 0:
                            arrive(e, item)
                        w = w_cols(item, 512)
                        for k in range(KD):
                            mm = pe.matmul(wrk[:, j, lo:lo + width], w[:, k, j * P:(j + 1) * P], hT[:, k, 0:width],
                                           start=(k == 0), stop=(k == KD - 1))
                        if lo == 0 and j == 3:
                            mm.then_inc(freed_by_pe, 1)
                    mm.then_inc(ffn_up, 1)

            def fall(e, g, blocks):
                arrive(e, ("edown", g))
                w = slot_of(("edown", g)).rearrange("p (j d) -> p j d", d=D)
                pe.wait_ge(ffn_act, e * UP_TILES + (base + 4 * g + 4))
                for b in range(blocks):
                    for n in range(2):
                        for j in range(4):
                            mm = pe.matmul(acc[:, 2 * b + n, :], F_ACT[:, 4 * (g % 2) + j, b * P:(b + 1) * P],
                                           w[:, j, n * 512:(n + 1) * 512], start=(g == 0 and j == 0),
                                           stop=(g == len(groups) - 1 and j == 3), skip_group_check=True)
                mm.then_inc(freed_by_pe, 1)

            def expert(e, blocks):
                width = blocks * P
                pe.wait_ge(picked, e * 4 + 4)
                for b in range(blocks):
                    for t in range(2):
                        mm = pe.transpose(wrk[:, 3, b * S + t * P:b * S + (t + 1) * P], m_wpick[:, t, b * P:(b + 1) * P], ident)
                mm.then_inc(pick_turned, 1)
                pe.wait_ge(share_added, e + 1)
                for k in range(KD):
                    for t in range(2):
                        mm = pe.matmul(accv[:, k, 0:width], m_h[:, t, k * P:(k + 1) * P], m_pick[:, t, 0:width],
                                       start=(t == 0), stop=(t == 1))
                mm.then_inc(gathered, 1)
                pe.wait_ge(tokens_ready, e + 1)
                pe.wait_ge(pick_ready, e + 1)
                for g in range(len(groups) + 1):
                    if g < len(groups):
                        rise(e, g, width)
                    if g >= 1:
                        fall(e, g - 1, blocks)
                pe.wait_ge(rows_ready, e + 1)
                for k in range(KD):
                    for b in range(blocks):
                        mm = pe.matmul(accv[:, k, :], m_rows[:, b, k * P:(k + 1) * P], m_wpickT[:, b, :],
                                       start=(b == 0), stop=(b == blocks - 1))
                mm.then_inc(scattered, 1)

            pe.wait_ge(act_done, at("act", "h tokens"))
            pe.wait_ge(dve_done, at("dve", "routed"))
            with pe.Fori(0, NE) as e:
                by_count(pe, e, expert)

        def experts_act(act):
            n = len(ffn_groups(F_EXPERT))

            def expert(e, blocks):
                width = blocks * P
                act.wait_ge(pick_turned, e + 1)
                act.activation(m_wpickT[:, 0:blocks, :].rearrange("p b t -> p (b t)"), wrk[:, 3, 0:blocks * S], ACT.Copy)\
                   .then_inc(pick_ready, 1)
                act.wait_ge(gathered, e + 1)
                act.activation(hT[:, :, 0:width], accv[:, :, 0:width], ACT.Copy).then_inc(tokens_ready, 1)
                for i in range(UP_TILES):
                    act.wait_ge(ffn_up, e * UP_TILES + (MOE + i + 1))
                    act.wait_ge(ffn_act, e * UP_TILES + (MOE + i - 3))
                    act.activation(F_SIL[:, i % 4, 0:width], wrk[:, i % 4, 0:width], ACT.Silu).then_inc(ffn_silu, 1)
                act.wait_ge(freed_by_pe, e * FREED + freeing(("edown", n - 1)))
                act.activation(m_rows[:, 0:blocks, :].rearrange("p b d -> p (b d)"), flat_acc[:, 0:blocks * D], ACT.Copy)\
                   .then_inc(rows_ready, 1)

            act.wait_ge(dve_done, at("dve", "routed"))
            with act.Fori(0, NE) as e:
                by_count(act, e, expert)

        def experts_dve(dve):
            def expert(e, blocks):
                width = blocks * P
                for t in range(2):
                    dve.tensor_scalar(m_pick[:, t, 0:width], K("slot_ids")[:, 0:width], m_pos[:, t, bass.ds(e, 1)], None, ALU.is_equal)\
                       .then_inc(picked, 1)
                    dve.tensor_scalar(m_wpick[:, t, 0:width], K("slot_ids")[:, 0:width], m_pos[:, t, bass.ds(e, 1)],
                                      m_gate[:, t, bass.ds(e, 1)], ALU.is_equal, ALU.mult).then_inc(picked, 1)
                for i in range(UP_TILES):
                    g, j = i // 4, i % 4
                    if j == 0 and g >= 2:
                        dve.wait_ge(freed_by_pe, e * FREED + freeing(("edown", g - 2)))
                    dve.wait_ge(ffn_silu, e * UP_TILES + (MOE + i + 1))
                    dve.tensor_tensor(F_ACT[:, 4 * (g % 2) + j, 0:width], F_SIL[:, j, 0:width], wrk[:, j, S:S + width], ALU.mult)\
                       .then_inc(ffn_act, 1)
                dve.wait_ge(scattered, e + 1)
                dve.tensor_tensor(y_sum[:, :, :], accv, y_sum[:, :, :], ALU.add).then_inc(share_added, 1)

            settle(dve, "dve", dve_done)
            dve.wait_ge(share_added, 1)
            with dve.Fori(0, NE) as e:
                by_count(dve, e, expert)

        def experts_end_dve(dve):
            dve.wait_ge(share_added, NE + 1)
            for m in range(KD):
                dve.scalar_tensor_tensor(xT[:, m, :], y_sum[:, m, :], mods[:, 1, 40 + m:41 + m], xT[:, m, :], ALU.mult, ALU.add)\
                   .then_inc(dve_done, up("dve", "residual", ("ffn", 1), m))

        n_q, n_ks, n_kw, n_kc, n_vc = Z(0, 3, S), Z(768, 1, S), Z(1024, 1, S), Z(1280, 1, S), Z(1536, 1, S)
        n_vs, n_vw, n_gate = Z(1792, 2, P), Z(2048, 2, P), Z(2304, 2, 18)
        l_cq, l_ckv, l_kpe = Z(2344, 2, S), Z(2856, 1, S), Z(3112, 1, S)
        l_q = Z(3368, 5, S)
        t_q, t_k, t_g, t_v = Z(4648, 3, S), Z(5416, 3, S), Z(6184, 3, S), Z(6952, 2, 320)
        n_hid, n_kcT, n_vcT = Z(7592, 2, 32), Z(7656, 16), Z(7672, P)
        l_tmp = Z(7800, 640)
        n_blk = Z(8448, 2, 16, 30)
        l_k = flat_h[:, 0:1280].rearrange("p (h t) -> p h t", h=5)
        l_v = flat_h[:, 1280:1920].rearrange("p (t n) -> p t n", t=2)

        def plan2(l):
            items = [("in2", l, i) for i in range(len(IN2))]
            w = [w_cols(items[i], b - a) for i, (a, b) in enumerate(IN2)]

            def cols(i, c, n):
                return lambda k: w[i][:, k, c:c + n]

            def tile(name, i, c, place, func=ACT.Copy, scale=1.0, m=P, p0=0):
                return (name, items[i], "f", cols(i, c, m), m, p0, [(place[p0:p0 + m], func, scale)])

            def rows(name, i, c, n, place, func=ACT.Copy):
                return [(f"{name}{t}", items[i], f"t{t}", cols(i, c, n), n, 0, [(place[:, t, 0:n], func, 1.0)]) for t in range(2)]

            def heads5(name, i, c, place, func=ACT.Copy, scale=1.0):
                return [tile(name + "0", i, c, place[:, 0, :], func, scale, HD, HD),
                        tile(name + "1", i, c + HD, place[:, 1, :], func, scale),
                        tile(name + "2", i, c + HD + P, place[:, 2, :], func, scale)]

            plan = [tile(f"nq{j}", 0, P * j, n_q[:, j, :]) for j in range(3)] + [tile("nkc", 0, 384, n_kc[:, 0, :])]
            plan += [tile("nvc", 1, 0, n_vc[:, 0, :]), tile("nks", 1, 128, n_ks[:, 0, :])]
            plan += rows("nvs", 1, 256, P, n_vs) + [tile("nkw", 1, 384, n_kw[:, 0, :])]
            plan += rows("nvw", 2, 0, P, n_vw) + rows("ng", 2, 128, 18, n_gate, ACT.Sigmoid)
            plan += [tile(f"cq{j}", 2, 146 + P * j, l_cq[:, j, :]) for j in range(2)]
            plan += [tile("ckv", 3, 0, l_ckv[:, 0, :]), tile("kpe", 3, 128, l_kpe[:, 0, :], m=32, p0=64)]
            plan += heads5("rq", 3, 160, t_q) + heads5("rk", 4, 0, t_k, ACT.Copy, float(HD) ** -0.5)
            plan += rows("rv", 5, 0, 320, t_v) + heads5("rg", 6, 0, t_g, ACT.Silu)
            return plan

        def rope2(l):
            plan = [("nkc", n_kc[:, 0, :], "turn16", 2, 0, P), ("nks", n_ks[:, 0, :], "turn16", 2, 0, P),
                    ("nkw", n_kw[:, 0, :], "turn16", 2, 0, P)]
            plan += [(f"nq{j}", n_q[:, j, :], "turn16", 2, 0, P) for j in range(3)]
            plan += [("kpe", l_kpe[64:96, 0, :], "turn32", 3, 64, 32)]
            for n, z in (("rq", t_q), ("rk", t_k)):
                plan += [(n + "0", z[HD:P, 0, :], "turn64", 1, HD, HD)]
                plan += [(f"{n}{j}", z[:, j, :], "turn64", 1, 0, P) for j in (1, 2)]
            return plan

        def rope_mla(l):
            return [(f"mq{h}", l_q[0:96, h, :], "turn32", 3, 0, 96) for h in range(5)]

        def cmp_act(act, l):
            act.wait_ge(dve_done, at("dve", "rope", ("2", l), "nkc"))
            for a, src in enumerate((n_kc, n_vc)):
                for g_ in range(2):
                    v = src[HD * g_:HD * g_ + HD, 0, :].rearrange("p (c b) -> p b c", b=16)
                    for par in range(2):
                        for later in range(2):
                            act.activation(n_blk[HD * par:HD * par + HD, a, 8 * later:8 * later + 8, 15 * g_:15 * g_ + 15],
                                           v[:, par:16:2, later:later + 15], ACT.Copy)\
                               .then_inc(act_done, up("act", "blocks", l) if (a, g_, par, later) == (1, 1, 1, 1) else up("act"))
            act.wait_ge(pe_done, at("pe", "hidden", l))
            act.activation(n_hid[:, :, 0:30], wrk[:, 0, 0:64].rearrange("p (a n) -> p a n", a=2)[:, :, 0:30], ACT.Gelu_apprx_tanh)\
               .then_inc(act_done, up("act", "hidden", l))
            act.wait_ge(freed_by_pe, freeing(("cmp", l)))
            act.activation(n_kcT[:, 0:15], wrk[:, 1, 0:15], ACT.Copy).then_inc(act_done, up("act"))
            act.activation(n_vcT[0:15, :], wrk[0:15, 2, 0:P], ACT.Copy).then_inc(act_done, up("act", "compressed", l))

        def cmp_dve(dve, l):
            dve.wait_ge(act_done, at("act", "blocks", l))
            for a, name in enumerate(("cmp_pos_k_2", "cmp_pos_v_2")):
                dve.tensor_tensor(n_blk[:, a], n_blk[:, a], columns(name, 16 * l, 16).unsqueeze(2).broadcast_to([P, 16, 30]), ALU.add)\
                   .then_inc(dve_done, up("dve", "blocks", l) if a else up("dve"))

        def cmp_pe(pe, l):
            w1 = slot_of(("cmp", l)).rearrange("p (a j h) -> p a j h", a=2, j=16)
            w2 = slot_of(("mla", l))[:, 1600:1728]
            pe.wait_ge(*landing(("cmp", l)))
            pe.wait_ge(dve_done, at("dve", "blocks", l))
            for a in range(2):
                for j in range(16):
                    mm = pe.matmul(wrk[:, 0, 32 * a:32 * a + 30], w1[:, a, j, :], n_blk[:, a, j, :], start=(j == 0), stop=(j == 15))
            mm.then_inc(pe_done, up("pe", "hidden", l))
            pe.wait_ge(*landing(("mla", l)))
            pe.wait_ge(act_done, at("act", "hidden", l))
            for g_ in range(2):
                mm = pe.matmul(wrk[HD * g_:HD * g_ + HD, 1, 0:15], w2[:, 0:HD], n_hid[:, 0, 15 * g_:15 * g_ + 15], start=True, stop=True)
            for g_ in range(2):
                mm = pe.matmul(wrk[0:15, 2, HD * g_:HD * g_ + HD], n_hid[:, 1, 15 * g_:15 * g_ + 15], w2[:, HD:P], start=True, stop=True)
            mm.then_inc(freed_by_pe, 1)

        def mla_entries(l):
            s = slot_of(("mla", l))
            uq = s[:, 0:960].rearrange("p (k f) -> p k f", k=2)
            ukv = s[:, 960:1600]
            out = []
            for h in range(5):
                out.append((f"mq{h}", 96, S, [(uq[:, k, 96 * h:96 * h + 96], l_cq[:, k, :]) for k in range(2)], l_q[0:96, h, :]))
            for h in range(5):
                out.append((f"mk{h}", HD, S, [(ukv[:, P * h:P * h + HD], l_ckv[:, 0, :])], l_k[0:HD, h, :]))
            v_cols = ukv.rearrange("p (h c) -> p h c", c=P)[:, :, HD:P]
            for t in range(2):
                out.append((f"mv{t}", P, 320, [(l_ckv[:, 0, t * P:(t + 1) * P], v_cols)], l_v[:, t, :]))
            return out

        def mla_pe(pe, l):
            pe.wait_ge(act_done, at("act", "latent squares", l))
            pe.matmul(wrk[:, 3, 0:S], ones, l_tmp3[:, 0, :], start=True, stop=False)
            pe.matmul(wrk[:, 3, 0:S], ones, l_tmp3[:, 1, :], start=False, stop=True)
            pe.matmul(wrk[:, 3, S:2 * S], ones, l_tmp3[:, 2, :], start=True, stop=True).then_inc(pe_done, up("pe", "latent sums", l))
            pe.wait_ge(dve_done, at("dve", "latents", l))
            entries = mla_entries(l)
            for i, (name, m, n, parts, place) in enumerate(entries):
                if i >= 4:
                    pe.wait_ge(act_done, at("act", "mla", l, entries[i - 4][0]))
                elif i < 3:
                    pe.wait_ge(act_done, at("act", "compressed", l))
                for k, (lhsT, rhs) in enumerate(parts):
                    mm = pe.matmul(wrk[0:m, i % 4, 0:n], lhsT, rhs, start=(k == 0), stop=(k == len(parts) - 1))
                if i == len(entries) - 1:
                    mm.then_inc(freed_by_pe, 1)
                else:
                    mm.then_inc(pe_done, up("pe", "mla", l, name))

        l_tmp3 = Z(9408, 3, S)

        def mla_act(act, l):
            act.wait_ge(act_done, at("act", "proj", ("2", l), "ckv"))
            act.activation(l_tmp3[:, 0:2, :], l_cq, ACT.Square).then_inc(act_done, up("act"))
            act.activation(l_tmp3[:, 2:3, :], l_ckv, ACT.Square).then_inc(act_done, up("act", "latent squares", l))
            root_act(act, at("dve", "latent mean squares", l), ("latent root", l), l_tmp[:, 0:512])
            act.wait_ge(dve_done, at("dve", "rope", ("2", l), "kpe"))
            act.wait_ge(pe_done, at("pe", "mla", l, "mq0"))
            for h in range(5):
                act.activation(l_k[64:96, h, :], l_kpe[64:96, 0, :], ACT.Copy).then_inc(act_done, up("act", "kpe", l) if h == 4 else up("act"))
            for i, (name, m, n, parts, place) in enumerate(mla_entries(l)):
                if name == "mv1":
                    act.wait_ge(freed_by_pe, freeing(("mla", l)))
                else:
                    act.wait_ge(pe_done, at("pe", "mla", l, name))
                act.activation(place, wrk[0:m, i % 4, 0:n], ACT.Copy).then_inc(act_done, up("act", "mla", l, name))

        def mla_dve(dve, l):
            dve.wait_ge(pe_done, at("pe", "latent sums", l))
            dve.tensor_scalar(l_tmp[:, 0:S], wrk[:, 3, 0:S], 1.0 / 256, EPS, ALU.mult, ALU.add).then_inc(dve_done, up("dve"))
            dve.tensor_scalar(l_tmp[:, S:2 * S], wrk[:, 3, S:2 * S], 1.0 / 128, EPS, ALU.mult, ALU.add)\
               .then_inc(dve_done, up("dve", "latent mean squares", l))
            inverse_root_dve(dve, ("latent root", l), l_tmp[:, 0:512])
            settle(dve, "dve", dve_done)
            for k in range(2):
                dve.scalar_tensor_tensor(l_cq[:, k, :], l_cq[:, k, :], column("mla_q_norm_2", 2 * l + k), l_tmp[:, 0:S],
                                         ALU.mult, ALU.mult).then_inc(dve_done, up("dve"))
            dve.scalar_tensor_tensor(l_ckv[:, 0, :], l_ckv[:, 0, :], column("mla_kv_norm_2", l), l_tmp[:, S:2 * S],
                                     ALU.mult, ALU.mult).then_inc(dve_done, up("dve", "latents", l))

        def branches2(l):
            out = []
            for h in range(6):
                g_, i = h // 3, h % 3
                rows = slice(HD * g_, HD * g_ + HD)
                q = n_q[rows, i, :]
                for br, kind in enumerate(("cmp", "slc", "win")):
                    k = (n_kcT[rows, :], n_ks[rows, 0, :], n_kw[rows, 0, :])[br]
                    if br == 0:
                        v = lambda t, g_=g_: n_vcT[0:15, HD * g_:HD * g_ + HD]
                    else:
                        z = (None, n_vs, n_vw)[br]
                        v = lambda t, z=z, g_=g_: z[:, t, HD * g_:HD * g_ + HD]
                    out.append(dict(q=q, k=k, v=v, mask=K("cmp_hide") if br == 0 else K("causal"), kind="cmp" if br == 0 else "causal",
                                    scale=float(HD) ** -0.5, gate=lambda t, c=3 * h + br: n_gate[:, t, c:c + 1], first=br == 0,
                                    last=br == 2, p0=HD * (h % 2), place=mixT[HD * (h % 2):HD * (h % 2) + HD, h // 2, :],
                                    ready=[(act_done, at("act", "mla", l, "mv1")),
                                           (dve_done, at("dve", "rope", ("mla", l), "mq4"))] if (h, br) == (0, 0) else [],
                                    mask_ready=[]))
            for h in range(5):
                p0 = HD * (h % 2)
                out.append(dict(q=l_q[0:96, h, :], k=l_k[0:96, h, :], v=lambda t, h=h: l_v[:, t, HD * h:HD * h + HD],
                                mask=K("causal"), kind="causal", scale=96.0 ** -0.5, gate=None, first=True, last=True, p0=p0,
                                place=mixT[p0:p0 + HD, 3 + h // 2, :], ready=[(act_done, at("act", "kpe", l))] if h == 0 else [],
                                mask_ready=[]))
            return out

        t_a = a_prob["2"]
        UPPER = slice(HD, P)

        def ret_at(h):
            return (h + 1) // 2, HD * ((h + 1) % 2)

        def ret_pe(pe, l):
            units = len(branches2(l))
            pe.wait_ge(act_done, at("act", "probT", ("2", l), units - 1))
            pe.wait_ge(dve_done, at("dve", "head out", ("2", l), 10))
            for h in range(6):
                if h < 5:
                    j, p0 = ret_at(h)
                    q, k = t_q[p0:p0 + HD, j, :], t_k[p0:p0 + HD, j, :]
                    if h >= 2:
                        pe.wait_ge(dve_done, at("dve", "decayed", l, h - 2))
                    pe.matmul(wrk[:, h % 2, 0:S], k[:, T0], q, start=True, stop=True)
                    pe.matmul(wrk[:, h % 2, S:384], k[:, T1], q[:, T1], start=True, stop=True).then_inc(pe_done, up("pe", "ret scores", l, h))
                if h >= 1:
                    j, p0 = ret_at(h - 1)
                    if h < 5:
                        pe.wait_ge(dve_done, at("dve", "decayed", l, h - 1))
                    else:
                        pe.wait_ge(*free_of(PLACE[("decay", l)]))
                    a = t_a[(h - 1) % 2]
                    pe.matmul(acc[p0:p0 + HD, j, 0:S], t_v[:, 0, HD * (h - 1):HD * h], a[:, 0:S], start=True, stop=False, skip_group_check=True)
                    pe.matmul(acc[p0:p0 + HD, j, P:S], t_v[:, 1, HD * (h - 1):HD * h], a[:, S:384], start=False, stop=True,
                              skip_group_check=True).then_inc(pe_done, up("pe", "ret out", l, h - 1))

            def head_sums(src, name):
                pe.matmul(wrk[UPPER, 2, 0:S], headsum[UPPER, UPPER], src[UPPER, 0, :], start=True, stop=True)
                pe.matmul(wrk[:, 3, :], headsum, src[:, 1:3, :].rearrange("p a t -> p (a t)"), start=True, stop=True)\
                  .then_inc(pe_done, up("pe", name, l))

            pe.wait_ge(act_done, at("act", "ret o", l))
            head_sums(t_q, "ret means")
            pe.wait_ge(act_done, at("act", "ret squares", l))
            head_sums(t_k, "ret variances")

        def ret_act(act, l):
            act.wait_ge(pe_done, at("pe", "ret out", l, 4))
            act.activation(t_q[UPPER, 0, :], acc[UPPER, 0, 0:S], ACT.Copy).then_inc(act_done, up("act"))
            act.activation(t_q[:, 1:3, :], acc[:, 1:3, 0:S], ACT.Copy).then_inc(act_done, up("act", "ret o", l))
            act.wait_ge(dve_done, at("dve", "ret centred", l))
            act.activation(t_k[UPPER, 0, :], t_q[UPPER, 0, :], ACT.Square).then_inc(act_done, up("act"))
            act.activation(t_k[:, 1:3, :], t_q[:, 1:3, :], ACT.Square).then_inc(act_done, up("act", "ret squares", l))
            act.wait_ge(dve_done, at("dve", "ret spreads", l))
            act.activation(t_k[UPPER, 0, :], t_k[UPPER, 0, :], ACT.Sqrt).then_inc(act_done, up("act"))
            act.activation(t_k[:, 1:3, :], t_k[:, 1:3, :], ACT.Sqrt).then_inc(act_done, up("act", "ret roots", l))

        def ret_dve(dve, l):
            decay = slot_of(("decay", l))[:, 0:5 * 384].rearrange("p (h n) -> p h n", h=5)
            dve.wait_ge(*landing(("decay", l)))
            for h in range(5):
                dve.wait_ge(pe_done, at("pe", "ret scores", l, h))
                if h >= 2:
                    dve.wait_ge(pe_done, at("pe", "ret out", l, h - 2))
                ins = dve.tensor_tensor(t_a[h % 2], wrk[:, h % 2, 0:384], decay[:, h, :], ALU.mult)
                if h < 4:
                    ins.then_inc(dve_done, up("dve", "decayed", l, h))
                else:
                    ins.then_inc(freed_by_dve, 1)
            parts = ((UPPER, slice(0, 1), wrk[UPPER, 2:3, 0:S]),
                     (slice(0, P), slice(1, 3), wrk[:, 3, :].rearrange("p (a t) -> p a t", a=2)))
            dve.wait_ge(pe_done, at("pe", "ret means", l))
            for i, (rows, tiles, sums) in enumerate(parts):
                dve.scalar_tensor_tensor(t_q[rows, tiles, :], sums, -1.0 / HD, t_q[rows, tiles, :], ALU.mult, ALU.add)\
                   .then_inc(dve_done, up("dve", "ret centred", l) if i else up("dve"))
            dve.wait_ge(pe_done, at("pe", "ret variances", l))
            for i, (rows, tiles, sums) in enumerate(parts):
                dve.tensor_scalar(t_k[rows, tiles, :], sums, 1.0 / HD, EPS, ALU.mult, ALU.add)\
                   .then_inc(dve_done, up("dve", "ret spreads", l) if i else up("dve"))
            dve.wait_ge(act_done, at("act", "ret roots", l))
            for rows, tiles, sums in parts:
                dve.reciprocal(t_k[rows, tiles, :], t_k[rows, tiles, :]).then_inc(dve_done, up("dve"))
            settle(dve, "dve", dve_done)
            for rows, tiles, sums in parts:
                dve.tensor_tensor(t_q[rows, tiles, :], t_q[rows, tiles, :], t_k[rows, tiles, :], ALU.mult).then_inc(dve_done, up("dve"))
            settle(dve, "dve", dve_done)
            for j in range(3):
                rows = UPPER if j == 0 else slice(0, P)
                col = column("ret_gain", 3 * l + j)[rows]
                dve.scalar_tensor_tensor(mixT[rows, 5 + j, :], t_q[rows, j, :], col, t_g[rows, j, :], ALU.mult, ALU.mult)\
                   .then_inc(dve_done, up("dve", "r out", l) if j == 2 else up("dve"))

        def mlp_pe(pe, l):
            n = len(ffn_groups(D_FF))
            base = tile_base("mlp", l)
            pe.wait_ge(act_done, at("act", "h", ("mlp", l), KD - 1))
            for g_ in range(n + 1):
                if g_ < n:
                    item = ("mup", l, g_)
                    pe.wait_ge(*landing(item))
                    w = w_cols(item, 512)
                    for j in range(4):
                        i = base + 4 * g_ + j
                        pe.wait_ge(ffn_act, i - 3)
                        for k in range(KD):
                            mm = pe.matmul(wrk[:, j, 0:S], w[:, k, j * P:(j + 1) * P], hT[:, k, :], start=(k == 0), stop=(k == KD - 1))
                        mm.then_inc(ffn_up, 1)
                if g_ >= 1:
                    ffn_down_pe(pe, g_ - 1, D_FF, ("mdown", l, g_ - 1), base, 0, "mlp")

        def mlp_dve(dve, l):
            base = tile_base("mlp", l)
            groups = ffn_groups(D_FF)
            for g_ in range(len(groups)):
                if g_ >= 2:
                    dve.wait_ge(freed_by_pe, freeing(("mdown", l, g_ - 2)))
                for j in range(4):
                    i = base + 4 * g_ + j
                    dve.wait_ge(ffn_up, i + 1)
                    dve.tensor_scalar(F_SIL[:, j, :], wrk[:, j, 0:S], 0.0, None, ALU.max).then_inc(dve_done, up("dve"))
                    settle(dve, "dve", dve_done)
                    dve.tensor_tensor(F_ACT[:, 4 * (g_ % 2) + j, :], F_SIL[:, j, :], F_SIL[:, j, :], ALU.mult).then_inc(ffn_act, 1)
            dve.wait_ge(freed_by_pe, freeing(("mdown", l, len(groups) - 1)))
            for m in range(KD):
                dve.tensor_tensor(xT[:, m, :], accv[:, m, :], xT[:, m, :], ALU.add).then_inc(dve_done, up("dve", "residual", ("mlp", l), m))

        def vec_cols(name, l):
            return lambda k: column(name, 8 * l + k)

        def x_ready2(l):
            if l == 0:
                return [(act_done, at("act", "h", ("between",), KD - 1))]
            return [(dve_done, at("dve", "residual", ("mlp", 0), KD - 1))]

        def block2_pe(pe, l):
            tag = ("2", l)
            norm_pe(pe, ("ln1", l))
            pe.wait_ge(act_done, at("act", "h", ("ln1", l), KD - 1))
            plan = plan2(l)
            for i in range(len(plan)):
                project_pe(pe, tag, plan, i)
            rope_pe(pe, tag, rope2(l), act_from(tag))
            pe.wait_ge(act_done, at("act", "proj", tag, "rg2"))
            cmp_pe(pe, l)
            mla_pe(pe, l)
            rope_pe(pe, ("mla", l), rope_mla(l), lambda name: at("act", "mla", l, name))
            att_pe(pe, tag, branches2(l))
            ret_pe(pe, l)
            outproj_pe(pe, tag, out_items("out2", l), [(dve_done, at("dve", "r out", l))])
            norm_pe(pe, ("mlp", l))
            mlp_pe(pe, l)

        def block2_act(act, l):
            tag = ("2", l)
            norm_act(act, ("ln1", l), x_ready2(l), vec_cols("ln1_gain_2", l), None)
            plan = plan2(l)
            for i in range(len(plan)):
                project_act(act, tag, plan, i)
            cmp_act(act, l)
            mla_act(act, l)
            att_act(act, tag, branches2(l))
            ret_act(act, l)
            norm_act(act, ("mlp", l), [(dve_done, at("dve", "residual", ("out2", l), KD - 1))], vec_cols("ln2_gain_2", l), None)

        def block2_dve(dve, l):
            tag = ("2", l)
            norm_dve(dve, ("ln1", l))
            rope_dve(dve, tag, rope2(l), act_from(tag))
            cmp_dve(dve, l)
            mla_dve(dve, l)
            rope_dve(dve, ("mla", l), rope_mla(l), lambda name: at("act", "mla", l, name))
            att_dve(dve, tag, branches2(l))
            ret_dve(dve, l)
            residual_dve(dve, ("out2", l), None, out_waits(tag, out_items("out2", l)))
            norm_dve(dve, ("mlp", l))
            mlp_dve(dve, l)

        y_tok = flat_mix.rearrange("p (t d) -> p t d", t=2)

        def end_pe(pe):
            pe.wait_ge(act_done, at("act", "h", ("end",), KD - 1))
            for t in range(2):
                for k in range(KD):
                    mm = pe.transpose(flat_acc[:, t * D + k * P:t * D + (k + 1) * P], hT[:, k, t * P:(t + 1) * P], ident)
                mm.then_inc(pe_done, up("pe", "result", t))

        def end_act(act):
            for t in range(2):
                act.wait_ge(pe_done, at("pe", "result", t))
                act.activation(y_tok[:, t, :], flat_acc[:, t * D:(t + 1) * D], ACT.Copy).then_inc(act_done, up("act", "result", t))

        @block.sync
        def _(sp):
            body_sync(sp)
            for t in range(2):
                sp.wait_ge(act_done, at("act", "result", t))
                sp.dma_start(out[0, t * P:(t + 1) * P, :], y_tok[:, t, :]).then_inc(out_landed, 16)
            sp.wait_ge(out_landed, 32)

        @block.scalar
        def _(act):
            start_act(act)
            block1_act(act, 0)
            dense_act(act)
            block1_act(act, 1)
            route_act(act)
            experts_act(act)
            norm_act(act, ("between",), [(dve_done, at("dve", "residual", ("ffn", 1), KD - 1))], vec_cols("g_final", 0), None, xT)
            for l in range(DEPTH):
                block2_act(act, l)
            norm_act(act, ("end",), [(dve_done, at("dve", "residual", ("mlp", 1), KD - 1))], vec_cols("final_gain_2", 0), None)
            end_act(act)

        @block.tensor
        def _(pe):
            start_pe(pe)
            block1_pe(pe, 0)
            dense_pe(pe)
            block1_pe(pe, 1)
            route_pe(pe)
            experts_pe(pe)
            norm_pe(pe, ("between",))
            for l in range(DEPTH):
                block2_pe(pe, l)
            norm_pe(pe, ("end",))
            end_pe(pe)

        @block.vector
        def _(dve):
            start_dve(dve)
            block1_dve(dve, 0)
            dense_dve(dve)
            block1_dve(dve, 1)
            route_dve(dve)
            experts_dve(dve)
            experts_end_dve(dve)
            norm_dve(dve, ("between",))
            for l in range(DEPTH):
                block2_dve(dve, l)
            norm_dve(dve, ("end",))

    return count


_INS = ["x", "c", "positions", "w_ada", "b_ada", "g_norm_mix", "g_norm_ffn", "w_in", "w_out", "hgrn_lb_logits",
        "hgrn_out_norm", "gmlp_vnorm_g", "gmlp_vnorm_b", "gmlp_w_s", "gmlp_b_s", "ffn_w_gate", "ffn_w_up", "ffn_w_down",
        "moe_w_router", "moe_w_gate", "moe_w_up", "moe_w_down", "g_final", "positions_2", "ln1_gain_2", "w_in_2",
        "cmp_pos_k_2", "cmp_w1_k_2", "cmp_w2_k_2", "cmp_pos_v_2", "cmp_w1_v_2", "cmp_w2_v_2", "mla_q_norm_2", "mla_w_uq_2",
        "mla_kv_norm_2", "mla_w_ukv_2", "ret_gn_gain_2", "w_out_2", "ln2_gain_2", "w_up_2", "w_down_2", "final_gain_2"]


def written(known, arrays, bacc):
    nc = bacc.Bacc("TRN2", target_bir_lowering=False, num_devices=1)
    given = {}
    for name, a in arrays.items():
        given[name] = nc.dram_tensor(f"in_{name}_dram", a.shape, mybir.dt.from_np(a.dtype), kind="ExternalInput").ap()
    out = nc.dram_tensor("out_0_dram", (1, S, D), F32, kind="ExternalOutput").ap()
    return nc, program(nc, given, out, known)


def kernel(**inputs):
    import concourse.bacc as _bacc
    from concourse.bass_utils import run_bass_kernel_spmd as _run

    arrays = {name: np.ascontiguousarray(inputs[name]) for name in _INS}
    arrays["consts"], arrays["decay"] = CONSTS, DECAY
    _, count = written(None, arrays, _bacc)
    nc, _ = written(count.names, arrays, _bacc)
    r = _run(nc, [{f"in_{name}_dram": a for name, a in arrays.items()}], core_ids=[0])
    return r.results[0]["out_0_dram"]
```

```python
from contextlib import ExitStack

import numpy as np

import concourse.bass as bass
from concourse import mybir

F32 = mybir.dt.float32
I32 = mybir.dt.int32
ALU = mybir.AluOpType
ACT = mybir.ActivationFunctionType
AX = mybir.AxisListType.X

P = 128
S = 256
D = 1024
KD = D // P
DEPTH = 2
HD = 64
EPS = 1e-6
NEG = -1e30
TAKEN = -3e38
TOPK = 64
F_DENSE, F_EXPERT, D_FF, NE = 2816, 3584, 4096, 8
SLOTS, SLOT = 7, 4096
C = 16
NB = S // C
NCMP = 15


CONST = {}


def constants():
    parts = []
    eye = np.eye(P, dtype=np.float32)
    row = np.arange(P)[:, None]
    col = np.arange(P)[None, :]

    def add(name, a):
        a = np.asarray(a, np.float32)
        a = a.reshape(a.shape[0], -1)
        if a.shape[0] < P:
            a = np.concatenate([a, np.zeros((P - a.shape[0], a.shape[1]), np.float32)])
        CONST[name] = (sum(x.shape[1] for x in parts), a.shape[1])
        parts.append(a)

    add("ident", eye)
    add("ones", np.ones((P, P)))
    add("headsum", (row // HD) == (col // HD))
    tri = np.where(col <= row, 0.0, NEG)
    add("causal", np.concatenate([tri, np.zeros((P, P)), tri], 1))
    add("upper", row <= col)

    def turn(heads, at, half):
        m = np.zeros((P, P), np.float32)
        for h in heads:
            for d in range(half):
                a, b = h + at + d, h + at + half + d
                m[b, a] = -1.0
                m[a, b] = 1.0
        return m

    add("turn64", turn((0, 64), 0, 32))
    add("turn16", turn((0, 64), 0, 8))
    add("turn32", turn((0,), 64, 16))

    def rates(theta, dim, heads, at, width=P):
        v = np.zeros((P, 1), np.float32)
        inv = (np.float32(1.0) / (np.float32(theta) ** (np.arange(0, dim, 2, dtype=np.float32) / np.float32(dim)))).astype(np.float32)
        for h in heads:
            v[h + at:h + at + dim // 2, 0] = inv
            v[h + at + dim // 2:h + at + dim, 0] = inv
        return v

    add("rate64", rates(10000.0, 64, (0, 64), 0))
    add("rate16", rates(500000.0, 16, (0, 64), 0))
    add("rate32", rates(500000.0, 32, (0,), 64))
    t = np.arange(S).reshape(2, P).T[:, :, None]
    end = (np.arange(NCMP) * 16 + 31)[None, None, :]
    see = np.zeros((P, 2, 16), np.float32)
    see[:, :, :NCMP] = end <= t
    add("cmp_see", see)
    add("cmp_hide", np.where(see > 0, 0.0, NEG))
    decay = np.zeros((P, 5, 384), np.float64)
    for h in range(5):
        g = np.log(1.0 - 2.0 ** (-5.0 - h))
        j = np.arange(P)[:, None]
        i = np.arange(S)[None, :]
        decay[:, h, :S] = np.where(i >= j, np.exp(np.maximum(i - j, 0) * g), 0.0)
        decay[:, h, S:] = decay[:, h, :P]
    CONST["decay"] = decay.reshape(P, -1).astype(np.float32)
    add("blocks", (np.arange(P)[:, None] // C) == np.arange(P // C)[None, :])
    add("slot_ids", np.broadcast_to(np.arange(S)[None, :], (P, S)))
    add("before", np.broadcast_to((np.arange(NE)[None, :] < np.arange(NE)[:, None]).reshape(1, -1), (P, NE * NE)))
    return np.concatenate(parts, 1).astype(np.float32)


CONSTS = constants()
DECAY = CONST.pop("decay")

VEC, VEC_LOADS = {}, []


def vector_rows():
    at = [0, 0, 0]
    for tile, name, rows in ((0, "c", 8), (0, "g_norm_mix", 16), (0, "g_norm_ffn", 16), (0, "g_final", 8),
                             (0, "ln1_gain_2", 16), (0, "ln2_gain_2", 16), (0, "final_gain_2", 8),
                             (0, "mla_q_norm_2", 4), (0, "mla_kv_norm_2", 2), (0, "hgrn_lb_logits", 6),
                             (1, "b_ada", 96), (2, "cmp_pos_k_2", 32), (2, "cmp_pos_v_2", 32)):
        VEC[name] = (tile, at[tile])
        VEC_LOADS.append((name, tile, at[tile], rows))
        at[tile] += rows
    for name, rows in (("onorm", 2), ("ret_gain", 6)):
        VEC[name] = (0, at[0])
        at[0] += rows
    assert max(at) <= P


vector_rows()


IN1 = [(0, 512), (512, 836), (836, 1220), (1220, 1604), (1604, 1988), (1988, 2372), (2372, 2884)]
IN2 = [(0, 512), (512, 1024), (1024, 1426), (1426, 1906), (1906, 2226), (2226, 2546), (2546, 2866)]


IN1_ORDER = (4, 2, 3, 0, 1, 5, 6)
DENSE_ADA = [(0, 10), (0, 11)] + [(1, i) for i in range(12)]


def dense_ada(g):
    return range(3 * g, 3 * g + 3) if g < 2 else range(6 + 2 * (g - 2), 8 + 2 * (g - 2))


def ffn_groups(width):
    return [(f, min(512, width - f)) for f in range(0, width, 512)]


def stream_items():
    before = [("ada", 0, i) for i in range(4)]
    experts, after = [], []
    for layer in range(DEPTH):
        out = before
        for n, i in enumerate(IN1_ORDER):
            out.append(("in1", layer, i))
            if layer == 0 and n >= 1:
                out.append(("ada", 0, 3 + n))
        out += [("gmlp", layer)] + [("out1", layer, h) for h in range(2)]
        if layer == 0:
            groups = ffn_groups(F_DENSE)
            for g in range(len(groups)):
                out += [("gate", g), ("up", g)]
                if g:
                    out.append(("down", g - 1))
                out += [("ada", *DENSE_ADA[n]) for n in dense_ada(g)]
            out.append(("down", len(groups) - 1))
    before.append(("router",))
    n = len(ffn_groups(F_EXPERT))
    for g in range(n):
        experts += [("egate", g), ("eup", g)]
        if g:
            experts.append(("edown", g - 1))
    experts.append(("edown", n - 1))
    for layer in range(DEPTH):
        after += [("in2", layer, i) for i in range(3)] + [("cmp", layer)]
        after += [("in2", layer, i) for i in range(3, len(IN2))] + [("mla", layer), ("decay", layer)] + [("out2", layer, h) for h in range(2)]
        n = len(ffn_groups(D_FF))
        for g in range(n):
            after.append(("mup", layer, g))
            if g:
                after.append(("mdown", layer, g - 1))
        after.append(("mdown", layer, n - 1))
    assert len(experts) % SLOTS == 0
    return before, experts, after


BEFORE, EXPERTS, AFTER = stream_items()
FIRST_EXPERT = len(BEFORE)
FIRST_AFTER = FIRST_EXPERT + NE * len(EXPERTS)
PLACE = {item: n for n, item in enumerate(BEFORE)}
PLACE.update({item: FIRST_EXPERT + n for n, item in enumerate(EXPERTS)})
PLACE.update({item: FIRST_AFTER + n for n, item in enumerate(AFTER)})


class Counts:

    def __init__(self, known):
        self.known, self.names, self.last = known, {}, {}

    def up(self, engine, *name):
        self.last[engine] = self.last.get(engine, 0) + 1
        if name:
            assert (engine, *name) not in self.names, name
            self.names[(engine, *name)] = self.last[engine]
        return 1

    def at(self, engine, *name):
        if self.known is None:
            return 1
        return self.known[(engine, *name)]

    def now(self, engine):
        return self.last[engine]


def program(nc, given, out, known, stop=None, dumps=None):
    count = Counts(known)
    up, at, now = count.up, count.at, count.now

    with ExitStack() as ctx:
        def sb(name, shape, dt=F32):
            return ctx.enter_context(nc.sbuf_tensor(name, shape, dt))

        def sem(name):
            return ctx.enter_context(nc.semaphore(name))

        ring = sb("ring", [P, SLOTS, SLOT])
        const = sb("const", list(CONSTS.shape))
        vec_rows = sb("vec_rows", [P, 3, P])
        vec = sb("vec", [P, 3, P])
        xT = sb("xT", [P, KD, S])
        hT = sb("hT", [P, KD, S])
        mixT = sb("mixT", [P, KD, S])
        cond = sb("cond", [P, KD])
        mods = sb("mods", [P, DEPTH, 48])
        gain = sb("gain", [P, 4, KD])
        lower = sb("lower", [P, DEPTH, 3])
        stat = sb("stat", [P, 128])
        table = sb("table", [P, 4, 2, S])
        SCR = sb("scratch", [P, 13200])
        acc = ctx.enter_context(nc.psum_tensor("acc", [P, 4, 512], F32))
        wrk = ctx.enter_context(nc.psum_tensor("wrk", [P, 4, 512], F32))

        def K(name):
            o, n = CONST[name]
            return const[:, o:o + n]

        def carve(tensor, offset, *shape):
            n = int(np.prod(shape))
            flat = tensor if tensor is not SCR else SCR[:, :]
            v = flat[:, offset:offset + n]
            if len(shape) == 2:
                v = v.rearrange("p (a b) -> p a b", a=shape[0])
            if len(shape) == 3:
                v = v.rearrange("p (a b c) -> p a b c", a=shape[0], b=shape[1])
            return v

        def column(name, i):
            t, r = VEC[name]
            return vec[:, t, r + i:r + i + 1]

        def columns(name, i, n):
            t, r = VEC[name]
            return vec[:, t, r + i:r + i + n]

        params_landed = sem("params_landed")
        landed = [sem(f"landed{i}") for i in range(SLOTS)]
        freed_by_pe = sem("freed_by_pe")
        freed_by_dve = sem("freed_by_dve")
        pe_done, act_done = sem("pe_done"), sem("act_done")
        dve_done, pool_done = sem("dve_done"), sem("pool_done")
        ffn_up = sem("ffn_up")
        ffn_silu = sem("ffn_silu")
        ffn_act = sem("ffn_act")
        ffn_read = sem("ffn_read")
        picked = sem("picked")
        pick_turned = sem("pick_turned")
        pick_ready = sem("pick_ready")
        gathered = sem("gathered")
        tokens_ready = sem("tokens_ready")
        rows_ready = sem("rows_ready")
        scattered = sem("scattered")
        share_added = sem("share_added")
        out_landed = sem("out_landed")

        free, counts = {}, {"pe": 0, "dve": 0, "up": 0}
        UP_TILES = sum(n // P for _, n in ffn_groups(F_EXPERT))
        FREED = sum(1 for i in EXPERTS if i[0] != "eup")

        def note(n, item):
            kind = item[0]
            if kind in ("ada", "decay"):
                counts["dve"] += 1
                free[n] = (freed_by_dve, counts["dve"], 0)
            elif kind in ("up", "eup", "mup"):
                width = {"up": F_DENSE, "eup": F_EXPERT, "mup": D_FF}[kind]
                counts["up"] += ffn_groups(width)[item[-1]][1] // P
                free[n] = (ffn_up, counts["up"], UP_TILES)
            else:
                counts["pe"] += 1
                free[n] = (freed_by_pe, counts["pe"], FREED)

        for n, item in enumerate(BEFORE):
            note(n, item)
        before_experts = dict(counts)
        for i, item in enumerate(EXPERTS):
            note(FIRST_EXPERT + i, item)
        assert counts["pe"] - before_experts["pe"] == FREED and counts["up"] - before_experts["up"] == UP_TILES
        counts["pe"] += FREED * (NE - 1)
        counts["up"] += UP_TILES * (NE - 1)
        for i in range(SLOTS):
            s_, v_, d_ = free[FIRST_EXPERT + len(EXPERTS) - SLOTS + i]
            free[FIRST_AFTER - SLOTS + i] = (s_, v_ + d_ * (NE - 1), 0)
        for i, item in enumerate(AFTER):
            note(FIRST_AFTER + i, item)

        def free_of(n):
            return free[n][0], free[n][1]

        def freeing(item):
            assert free[PLACE[item]][0] is freed_by_pe
            return free[PLACE[item]][1]

        def slot_of(item):
            return ring[:, PLACE[item] % SLOTS, :]

        def w_cols(item, width):
            return slot_of(item)[:, 0:KD * width].rearrange("p (k f) -> p k f", k=KD)

        def by_rows(w):
            return w.rearrange("(k p) f -> p k f", p=P)

        g = given

        def loads(item):
            kind = item[0]
            s = slot_of(item)
            if kind == "ada":
                return [(w_cols(item, 512), by_rows(g["w_ada"][item[1]])[:, :, item[2] * 512:item[2] * 512 + 512])]
            if item[0] == "in2" and item[2] == 0:
                w = by_rows(g["w_in_2"][item[1]])
                v = w_cols(item, 512)
                heads = v[:, :, 0:384].rearrange("p k (i g d) -> p k i g d", i=3, g=2)
                src = w[:, :, 0:384].rearrange("p k (g i d) -> p k i g d", i=3, g=2)
                return [(heads[:, :, i, q], src[:, :, i, q]) for i in range(3) for q in range(2)] + [(v[:, :, 384:512], w[:, :, 384:512])]
            if kind in ("in1", "in2"):
                a, b = (IN1 if kind == "in1" else IN2)[item[2]]
                w = g["w_in" if kind == "in1" else "w_in_2"][item[1]]
                return [(w_cols(item, b - a), by_rows(w)[:, :, a:b])]
            if kind in ("out1", "out2"):
                w = g["w_out" if kind == "out1" else "w_out_2"][item[1]]
                return [(w_cols(item, 512), by_rows(w)[:, :, item[2] * 512:item[2] * 512 + 512])]
            if kind in ("gate", "up"):
                f, n = ffn_groups(F_DENSE)[item[1]]
                return [(w_cols(item, n), by_rows(g["ffn_w_" + kind][0])[:, :, f:f + n])]
            if kind == "down":
                f, n = ffn_groups(F_DENSE)[item[1]]
                return [(s[:, 0:n * KD].rearrange("p (j d) -> p j d", d=D),
                         g["ffn_w_down"][0, f:f + n].rearrange("(j p) d -> p j d", p=P))]
            if kind == "mup":
                f, n = ffn_groups(D_FF)[item[2]]
                return [(w_cols(item, n), by_rows(g["w_up_2"][item[1]])[:, :, f:f + n])]
            if kind == "mdown":
                f, n = ffn_groups(D_FF)[item[2]]
                return [(s[:, 0:n * KD].rearrange("p (j d) -> p j d", d=D),
                         g["w_down_2"][item[1], f:f + n].rearrange("(j p) d -> p j d", p=P))]
            if kind == "gmlp":
                l = item[1]
                return [(s[:, 0:256], rows_of(g["gmlp_vnorm_g"], l)),
                        (s[:, 256:512], rows_of(g["gmlp_vnorm_b"], l)),
                        (s[:, 512:1024].rearrange("p (g s) -> p g s", g=4), g["gmlp_w_s"][l].rearrange("g t s -> t g s")),
                        (s[0:1, 1024:1536], g["gmlp_b_s"][l:l + 1].rearrange("a g t -> a (g t)"))]
            if kind == "decay":
                return [(s[:, 0:5 * 384], g["decay"])]
            if kind == "router":
                return [(s[:, 0:64].rearrange("p (k e) -> p k e", k=KD), by_rows(g["moe_w_router"][0]))]
            if kind == "cmp":
                l = item[1]
                v = s.rearrange("p (a j h) -> p a j h", a=2, j=16)
                return [(v[:, 0], g["cmp_w1_k_2"][l].rearrange("(j p) h -> p j h", p=P)),
                        (v[:, 1], g["cmp_w1_v_2"][l].rearrange("(j p) h -> p j h", p=P))]
            if kind == "mla":
                l = item[1]
                return [(s[:, 0:960].rearrange("p (k f) -> p k f", k=2), by_rows(g["mla_w_uq_2"][l])),
                        (s[:, 960:1600], g["mla_w_ukv_2"][l]),
                        (s[:, 1600:1664], g["cmp_w2_k_2"][l]),
                        (s[:, 1664:1728], g["cmp_w2_v_2"][l])]
            raise KeyError(item)

        def rows_of(w, l):
            r = w[l:l + 1, :]
            return bass.AP(tensor=r.tensor, offset=r.offset, ap=[[0, P], [1, r.shape[1]]])

        land = {}
        total = [0] * SLOTS
        for n, item in enumerate(BEFORE):
            total[n % SLOTS] += 16 * len(loads(item))
            land[n] = total[n % SLOTS]
        at_experts = list(total)
        for i in range(SLOTS):
            total[i] += 16 * NE * (len(EXPERTS) // SLOTS)
        for i, item in enumerate(AFTER):
            n = FIRST_AFTER + i
            total[n % SLOTS] += 16 * len(loads(item))
            land[n] = total[n % SLOTS]

        def landing(item):
            n = PLACE[item]
            return landed[n % SLOTS], land[n]

        xin = carve(hT[:, :, :].rearrange("p k t -> p (k t)"), 0, 2, D)
        pos = SCR[:, 6800:6800 + 2 * S].bitcast(I32).rearrange("p (b t) -> p b t", b=2)
        c_rows = sb("c_rows", [KD, P])

        def flat_rows(src):
            letters = "abcd"[:len(src.shape)]
            flat = src.rearrange(f"{' '.join(letters)} -> ({' '.join(letters)})") if len(src.shape) > 1 else src
            return flat.rearrange("(r p) -> r p", p=P)

        IDENT = slice(CONST["ident"][0], CONST["ident"][0] + P)
        REST = slice(P, CONSTS.shape[1])
        x_landed, c_landed, rest_landed = sem("x_landed"), sem("c_landed"), sem("rest_landed")
        vec_loads = [(vec_rows[r:r + rows, t, :], flat_rows(g[name])) for name, t, r, rows in VEC_LOADS if name != "c"]
        t, r = VEC["onorm"]
        for half in range(2):
            vec_loads.append((vec_rows[r:r + 2, t, half * HD:(half + 1) * HD], g["hgrn_out_norm"]))
        t, r = VEC["ret_gain"]
        for l in range(DEPTH):
            gl = g["ret_gn_gain_2"][l].rearrange("h d -> (h d)")
            vec_loads.append((vec_rows[r + 3 * l:r + 3 * l + 1, t, HD:P], gl[0:HD].rearrange("(a d) -> a d", a=1)))
            vec_loads.append((vec_rows[r + 3 * l + 1:r + 3 * l + 3, t, :], gl[HD:5 * HD].rearrange("(r p) -> r p", p=P)))
        PARAMS = 16 * len(vec_loads)

        block = ctx.enter_context(nc.Block())
        stops = {}

        def body_sync(sp):
            sp.dma_start(const[:, IDENT], g["consts"][:, IDENT]).then_inc(c_landed, 16)
            sp.dma_start(c_rows[:, :], flat_rows(g["c"])).then_inc(c_landed, 16)
            sp.dma_start(xin, g["x"][0].rearrange("(t p) d -> p t d", p=P)).then_inc(x_landed, 16)
            sp.wait_ge(params_landed, PARAMS)
            sp.dma_start(const[:, REST], g["consts"][:, REST]).then_inc(rest_landed, 16)
            for n, item in enumerate(BEFORE):
                if stop is not None and n >= stop[0]:
                    break
                if n >= SLOTS:
                    sp.wait_ge(*free_of(n - SLOTS))
                for place, src in loads(item):
                    sp.dma_start(place, src).then_inc(landed[n % SLOTS], 16)
            if stop is None:
                sources = {"egate": g["moe_w_gate"], "eup": g["moe_w_up"], "edown": g["moe_w_down"]}
                groups = ffn_groups(F_EXPERT)
                with sp.Fori(0, NE) as e:
                    for i, item in enumerate(EXPERTS):
                        n = FIRST_EXPERT + i
                        if i >= SLOTS:
                            s, v, d = free[n - SLOTS]
                            sp.wait_ge(s, e * d + v)
                        else:
                            s, v, d = free[n - SLOTS + len(EXPERTS)]
                            sp.wait_ge(*free_of(n - SLOTS))
                            sp.wait_ge(s, e * d + (v - d))
                        f, w = groups[item[1]]
                        src = sources[item[0]][0][e]
                        if item[0] == "edown":
                            sp.dma_start(ring[:, n % SLOTS, 0:w * KD].rearrange("p (j d) -> p j d", d=D),
                                         src[f:f + w].rearrange("(j p) d -> p j d", p=P)).then_inc(landed[n % SLOTS], 16)
                        else:
                            sp.dma_start(ring[:, n % SLOTS, 0:w * KD].rearrange("p (k f) -> p k f", k=KD),
                                         by_rows(src)[:, :, f:f + w]).then_inc(landed[n % SLOTS], 16)
                for i, item in enumerate(AFTER):
                    n = FIRST_AFTER + i
                    sp.wait_ge(*free_of(n - SLOTS))
                    for place, src in loads(item):
                        sp.dma_start(place, src).then_inc(landed[n % SLOTS], 16)

        accv = acc[:, :, :].rearrange("p b (h t) -> p (b h) t", t=S)
        T0, T1 = slice(0, P), slice(P, S)
        ident, ones, headsum = K("ident"), K("ones"), K("headsum")
        rstd = mixT[:, 0, :]

        def settle(eng, name, s):
            eng.wait_ge(s, now(name))

        ang = carve(SCR, 7312, 4, S)
        turns = carve(SCR, 8336, 4, S)
        fpos = carve(SCR, 9360, 2, S)
        TWO_PI_PARTS = (6.28125, 0.0019340515136718750, 2 * np.pi - 6.28125 - 0.0019340515136718750)
        ROUND = 12582912.0

        def start_act(act):
            act.wait_ge(dve_done, at("dve", "rows cleared"))
            for place, src in vec_loads:
                act.dma_start(place, src).then_inc(params_landed, 16)
            for b, name in enumerate(("positions", "positions_2")):
                r = g[name]
                act.dma_start(pos[:, b, :], bass.AP(tensor=r.tensor, offset=r.offset, ap=[[0, P], [1, S]])).then_inc(rest_landed, 16)
            act.wait_ge(pe_done, at("pe", "c turned"))
            act.activation(cond[:, :], wrk[:, 0, 0:KD], ACT.Silu).then_inc(act_done, up("act", "cond"))
            act.wait_ge(pe_done, at("pe", "x turned"))
            act.activation(xT[:, 0:4, :], accv[:, 0:4, :], ACT.Copy).then_inc(act_done, up("act"))
            act.activation(xT[:, 4:8, :], accv[:, 4:8, :], ACT.Copy).then_inc(act_done, up("act", "x"))

        def tables_act(act):
            act.wait_ge(dve_done, at("dve", "lower in"))
            act.activation(stat[:, 3:9], stat[:, 3:9], ACT.Exp).then_inc(act_done, up("act", "lower exp"))
            act.wait_ge(dve_done, at("dve", "angles"))
            act.activation(table[:, :, 1, :], ang, ACT.Sin).then_inc(act_done, up("act"))
            act.activation(table[:, :, 0, :], turns, ACT.Sin).then_inc(act_done, up("act", "tables"))

        def start_pe(pe):
            pe.wait_ge(c_landed, 32)
            pe.transpose(wrk[:, 0, 0:KD], c_rows[:, :], ident[0:KD, 0:KD]).then_inc(pe_done, up("pe", "c turned"))
            pe.wait_ge(x_landed, 16)
            for k in range(KD):
                for t in range(2):
                    mm = pe.transpose(accv[:, k, t * P:(t + 1) * P], xin[:, t, k * P:(k + 1) * P], ident)
            mm.then_inc(pe_done, up("pe", "x turned"))
            pe.wait_ge(params_landed, PARAMS)
            for t in range(3):
                mm = pe.transpose(wrk[:, 1, t * P:(t + 1) * P], vec_rows[:, t, :], ident)
            mm.then_inc(pe_done, up("pe", "vec"))
            pe.wait_ge(rest_landed, 48)

        def start_dve(dve):
            dve.memset(vec_rows[:, :, :], 0.0).then_inc(dve_done, up("dve", "rows cleared"))

        def vec_dve(dve):
            dve.wait_ge(pe_done, at("pe", "vec"))
            dve.tensor_copy(vec[:, :, :].rearrange("p a b -> p (a b)"), wrk[:, 1, 0:3 * P]).then_inc(dve_done, up("dve", "vec"))

        def tables_dve(dve):
            a0, a1 = columns("hgrn_lb_logits", 0, 3), columns("hgrn_lb_logits", 3, 3)
            dve.tensor_tensor(stat[:, 0:3], a0, a1, ALU.max).then_inc(dve_done, up("dve"))
            settle(dve, "dve", dve_done)
            dve.tensor_tensor(stat[:, 3:6], a0, stat[:, 0:3], ALU.subtract).then_inc(dve_done, up("dve"))
            dve.tensor_tensor(stat[:, 6:9], a1, stat[:, 0:3], ALU.subtract).then_inc(dve_done, up("dve", "lower in"))
            dve.wait_ge(act_done, at("act", "lower exp"))
            dve.tensor_tensor(stat[:, 9:12], stat[:, 3:6], stat[:, 6:9], ALU.add).then_inc(dve_done, up("dve"))
            settle(dve, "dve", dve_done)
            dve.reciprocal(stat[:, 12:15], stat[:, 9:12]).then_inc(dve_done, up("dve"))
            settle(dve, "dve", dve_done)
            dve.tensor_tensor(stat[:, 15:18], stat[:, 3:6], stat[:, 12:15], ALU.mult).then_inc(dve_done, up("dve"))
            dve.tensor_tensor(stat[:, 18:21], stat[:, 6:9], stat[:, 12:15], ALU.mult).then_inc(dve_done, up("dve"))
            settle(dve, "dve", dve_done)
            dve.tensor_tensor(stat[:, 21:24], stat[:, 15:18], stat[:, 18:21], ALU.add).then_inc(dve_done, up("dve"))
            dve.tensor_tensor(lower[:, 0, :], stat[:, 15:18], stat[:, 15:18], ALU.subtract).then_inc(dve_done, up("dve"))
            settle(dve, "dve", dve_done)
            dve.tensor_tensor(lower[:, 1, :], stat[:, 21:24], stat[:, 15:18], ALU.subtract).then_inc(dve_done, up("dve", "lower"))
            dve.wait_ge(rest_landed, 48)
            dve.tensor_copy(fpos, pos).then_inc(dve_done, up("dve"))
            settle(dve, "dve", dve_done)
            for i, (b, rate) in enumerate(((0, "rate64"), (1, "rate64"), (1, "rate16"), (1, "rate32"))):
                dve.tensor_scalar(ang[:, i, :], fpos[:, b, :], K(rate), None, ALU.mult).then_inc(dve_done, up("dve"))
            settle(dve, "dve", dve_done)
            dve.tensor_scalar(turns, ang, float(1 / (2 * np.pi)), ROUND, ALU.mult, ALU.add).then_inc(dve_done, up("dve"))
            settle(dve, "dve", dve_done)
            dve.tensor_scalar(turns, turns, ROUND, None, ALU.subtract).then_inc(dve_done, up("dve"))
            for part in TWO_PI_PARTS:
                settle(dve, "dve", dve_done)
                for i in range(4):
                    dve.scalar_tensor_tensor(ang[:, i, :], turns[:, i, :], -float(part), ang[:, i, :], ALU.mult, ALU.add)\
                       .then_inc(dve_done, up("dve"))
            settle(dve, "dve", dve_done)
            dve.tensor_scalar(ang, ang, 3.1415925, -3.1415925, ALU.min, ALU.max).then_inc(dve_done, up("dve"))
            settle(dve, "dve", dve_done)
            dve.scalar_tensor_tensor(turns, ang, -1.0, ang, ALU.mult, ALU.max).then_inc(dve_done, up("dve"))
            settle(dve, "dve", dve_done)
            dve.tensor_scalar(turns, turns, -1.0, float(np.pi / 2), ALU.mult, ALU.add).then_inc(dve_done, up("dve", "angles"))

        part_sum = [SCR[:, 12176 + 512 * i:12176 + 512 * (i + 1)] for i in range(2)]

        def ada_dve(dve, l, i):
            item = ("ada", l, i)
            w = w_cols(item, 512)
            dve.wait_ge(*landing(item))
            n = 12 * l + i
            if n == 0:
                dve.wait_ge(act_done, at("act", "cond"))
            if n >= 2:
                dve.wait_ge(pe_done, at("pe", "ada", n - 2))
            dst = part_sum[n % 2]
            for k in range(KD):
                if k == 0:
                    ins = dve.tensor_scalar(dst, w[:, k, :], cond[:, k:k + 1], None, ALU.mult)
                else:
                    settle(dve, "dve", dve_done)
                    ins = dve.scalar_tensor_tensor(dst, w[:, k, :], cond[:, k:k + 1], dst, ALU.mult, ALU.add)
                if k < KD - 1:
                    ins.then_inc(dve_done, up("dve"))
                else:
                    ins.then_inc(freed_by_dve, 1)

        def ada_bank(l, i):
            return acc[:, 1, :] if (l, i) < (0, 10) else wrk[:, 3, 64 * l:64 * l + 48]

        def ada_pe(pe, l, i):
            n = 12 * l + i
            if n == 0:
                pe.wait_ge(act_done, at("act", "x"))
            pe.wait_ge(freed_by_dve, n + 1)
            for j in range(4):
                mm = pe.matmul(ada_bank(l, i)[:, 4 * i + j:4 * i + j + 1], part_sum[n % 2][:, j * P:(j + 1) * P], ones[:, 0:1],
                               start=True, stop=True)
            mm.then_inc(pe_done, up("pe", "ada", n))

        def ada_end_dve(dve, l, first, last):
            dve.wait_ge(pe_done, at("pe", "ada", 12 * l + last))
            a, b = 4 * first, 4 * last + 4
            dve.tensor_tensor(mods[:, l, a:b], ada_bank(l, last)[:, a:b], columns("b_ada", 48 * l + a, b - a), ALU.add)\
               .then_inc(dve_done, up("dve", "mods", l, last))
            settle(dve, "dve", dve_done)
            for j, (sc, name) in enumerate(((8, "g_norm_mix"), (32, "g_norm_ffn"))):
                if a <= sc < b:
                    dve.scalar_tensor_tensor(gain[:, 2 * l + j, :], mods[:, l, sc:sc + 8], 1.0, columns(name, 8 * l, 8),
                                             ALU.add, ALU.mult).then_inc(dve_done, up("dve", "gain", l, j))

        def norm_act(act, tag, x_ready, scale_of, shift_of, place=None, wait_scale=()):
            place = hT if place is None else place
            for k in range(KD):
                act.wait_ge(*x_ready(k))
                act.activation(hT[:, k, :], xT[:, k, :], ACT.Square).then_inc(act_done, up("act", "squares", tag, k))
            root_act(act, at("dve", "mean square", tag), ("root", tag), rstd)
            for s, v in wait_scale:
                act.wait_ge(s, v)
            for k in range(KD):
                act.wait_ge(dve_done, at("dve", "scaled", tag, k))
                act.activation(place[:, k, :], hT[:, k, :], ACT.Identity, scale=scale_of(k),
                               bias=shift_of(k) if shift_of else 0.0).then_inc(act_done, up("act", "h", tag, k))

        def norm_pe(pe, tag):
            for k in range(KD):
                pe.wait_ge(act_done, at("act", "squares", tag, k))
                mm = pe.matmul(wrk[:, 3, 0:S], ones, hT[:, k, :], start=(k == 0), stop=(k == KD - 1))
            mm.then_inc(pe_done, up("pe", "sum of squares", tag))

        def norm_dve(dve, tag):
            dve.wait_ge(pe_done, at("pe", "sum of squares", tag))
            dve.tensor_scalar(rstd, wrk[:, 3, 0:S], 1.0 / D, EPS, ALU.mult, ALU.add).then_inc(dve_done, up("dve", "mean square", tag))
            inverse_root_dve(dve, ("root", tag), rstd)
            settle(dve, "dve", dve_done)
            for k in range(KD):
                dve.tensor_tensor(hT[:, k, :], xT[:, k, :], rstd, ALU.mult).then_inc(dve_done, up("dve", "scaled", tag, k))

        def root_act(act, wait, name, place):
            act.wait_ge(dve_done, wait)
            act.activation(place, place, ACT.Sqrt).then_inc(act_done, up("act", *name))

        def inverse_root_dve(dve, name, place):
            dve.wait_ge(act_done, at("act", *name))
            dve.reciprocal(place, place).then_inc(dve_done, up("dve"))

        NORM_OF = {"1": lambda l: ("mix", l), "2": lambda l: ("ln1", l)}

        def project_pe(pe, tag, plan, i, bank, bank_read):
            name, item, mode, cols, m, p0, places = plan[i]
            if i == 0 or plan[i - 1][1] != item:
                pe.wait_ge(*landing(item))
            if bank_read:
                pe.wait_ge(*bank_read)
            for k in range(KD):
                if i == 0:
                    pe.wait_ge(act_done, at("act", "h", NORM_OF[tag[0]](tag[1]), k))
                if mode == "f":
                    mm = pe.matmul(acc[p0:p0 + m, bank, 0:S], cols(k), hT[:, k, :], start=(k == 0), stop=(k == KD - 1))
                else:
                    t = T0 if mode == "t0" else T1
                    mm = pe.matmul(acc[:, bank, 0:m], hT[:, k, t], cols(k), start=(k == 0), stop=(k == KD - 1))
            if i + 1 == len(plan) or plan[i + 1][1] != item:
                mm.then_inc(freed_by_pe, 1)
            else:
                mm.then_inc(pe_done, up("pe", "proj", tag, name))

        def project_act(act, tag, plan, i, bank):
            name, item, mode, cols, m, p0, places = plan[i]
            if i + 1 == len(plan) or plan[i + 1][1] != item:
                act.wait_ge(freed_by_pe, freeing(item))
            else:
                act.wait_ge(pe_done, at("pe", "proj", tag, name))
            n = S if mode == "f" else m
            lo, hi = (p0, p0 + m) if mode == "f" else (0, P)
            for j, (place, func, scale) in enumerate(places):
                act.activation(place, acc[lo:hi, bank, 0:n], func, scale=scale)\
                   .then_inc(act_done, up("act", "proj", tag, name) if j == len(places) - 1 else up("act"))

        rope_tmp = [SCR[:, 12176 + 256 * i:12176 + 256 * (i + 1)] for i in range(4)]

        def rope_tile_pe(pe, tag, entry, bank, bank_read, tile_ready):
            name, tile, turn, tab, p0, rows = entry
            pe.wait_ge(*tile_ready)
            if bank_read:
                pe.wait_ge(*bank_read)
            pe.matmul(acc[p0:p0 + rows, bank, 0:S], K(turn)[p0:p0 + rows, p0:p0 + rows], tile, start=True, stop=True)\
              .then_inc(pe_done, up("pe", "rope", tag, name))

        def rope_tile_dve(dve, tag, i, entry, bank, tile_ready):
            name, tile, turn, tab, p0, rows = entry
            a, b = rope_tmp[2 * (i % 2)][p0:p0 + rows], rope_tmp[2 * (i % 2) + 1][p0:p0 + rows]
            dve.wait_ge(*tile_ready)
            settle(dve, "dve", dve_done)
            dve.tensor_tensor(a, tile, table[p0:p0 + rows, tab, 0, :], ALU.mult).then_inc(dve_done, up("dve"))
            dve.wait_ge(pe_done, at("pe", "rope", tag, name))
            dve.tensor_tensor(b, acc[p0:p0 + rows, bank, 0:S], table[p0:p0 + rows, tab, 1, :], ALU.mult)\
               .then_inc(dve_done, up("dve"))
            settle(dve, "dve", dve_done)
            dve.tensor_tensor(tile, a, b, ALU.add).then_inc(dve_done, up("dve", "rope", tag, name))

        def rope_pe(pe, tag, plan, ready):
            for i, entry in enumerate(plan):
                before = (dve_done, at("dve", "rope", tag, plan[i - 2][0])) if i >= 2 else None
                rope_tile_pe(pe, tag, entry, i % 2, before, (act_done, ready(entry[0])))

        def rope_dve(dve, tag, plan, ready):
            for i, entry in enumerate(plan):
                rope_tile_dve(dve, tag, i, entry, i % 2, (act_done, ready(entry[0])))

        def outproj_pe(pe, tag, items, waits):
            for s, v in waits:
                pe.wait_ge(s, v)
            for h, item in enumerate(items):
                w = w_cols(item, 512)
                pe.wait_ge(*landing(item))
                for m in range(4):
                    for k in range(KD):
                        mm = pe.matmul(accv[:, 4 * h + m, :], w[:, k, m * P:(m + 1) * P], mixT[:, k, :],
                                       start=(k == 0), stop=(k == KD - 1))
                    if m < 3:
                        mm.then_inc(pe_done, up("pe", "out", tag, 4 * h + m))
                mm.then_inc(freed_by_pe, 1)

        def residual_dve(dve, tag, gate_of, waits):
            for m in range(KD):
                dve.wait_ge(*waits[m])
                if gate_of is None:
                    ins = dve.tensor_tensor(xT[:, m, :], accv[:, m, :], xT[:, m, :], ALU.add)
                else:
                    ins = dve.scalar_tensor_tensor(xT[:, m, :], accv[:, m, :], gate_of(m), xT[:, m, :], ALU.mult, ALU.add)
                ins.then_inc(dve_done, up("dve", "residual", tag, m))

        def out_waits(tag, items):
            return [(freed_by_pe, freeing(items[m // 4])) if m % 4 >= 2 else (pe_done, at("pe", "out", tag, m | 1))
                    for m in range(KD)]

        Z = lambda o, *shape: carve(SCR, o, *shape)
        AT2 = 8448

        flat_h = hT[:, :, :].rearrange("p k t -> p (k t)")
        part_h = lambda o: [flat_h[:, o + 384 * i:o + 384 * i + 384] for i in range(2)]
        a_score = {"1": [Z(1536 + 384 * i, 384) for i in range(2)], "2": [Z(AT2 + 384 * i, 384) for i in range(2)]}
        a_prob = {"1": part_h(384), "2": [Z(AT2 + 768 + 384 * i, 384) for i in range(2)]}
        a_probT = {"1": part_h(1152), "2": [Z(AT2 + 1536 + 384 * i, 384) for i in range(2)]}

        def a_stat(u, what):
            return stat[:, 32 + 8 * (u % 4) + 2 * what:32 + 8 * (u % 4) + 2 * what + 2]

        def spans(kind):
            return ((0, 15), (16, 31)) if kind == "cmp" else ((0, P), (P, 384))

        def att_scores_pe(pe, tag, u, b):
            for s, v in b["ready"]:
                pe.wait_ge(s, v)
            if u >= 2:
                pe.wait_ge(dve_done, at("dve", "masked", tag, u - 2))
            for t, (lo, hi) in enumerate(spans(b["kind"])):
                mm = pe.matmul(wrk[:, u % 2, lo:hi], b["q"][:, t * P:(t + 1) * P], b["k"][:, 0:hi - lo], start=True, stop=True)
            mm.then_inc(pe_done, up("pe", "scores", tag, u))

        def att_turn_pe(pe, tag, u, b):
            pe.wait_ge(dve_done, at("dve", "probs", tag, u))
            if u >= 2:
                pe.wait_ge(act_done, at("act", "probT", tag, u - 2))
            if b["kind"] == "cmp":
                for t, (lo, hi) in enumerate(spans("cmp")):
                    mm = pe.transpose(wrk[0:15, 2 + u % 2, t * P:(t + 1) * P], a_prob[tag[0]][u % 2][:, lo:hi], ident)
            else:
                for j in range(3):
                    mm = pe.transpose(wrk[:, 2 + u % 2, j * P:(j + 1) * P], a_prob[tag[0]][u % 2][:, j * P:(j + 1) * P], ident)
            mm.then_inc(pe_done, up("pe", "turned", tag, u))

        def att_value_pe(pe, tag, u, b, head):
            pe.wait_ge(act_done, at("act", "probT", tag, u))
            for s, v in b.get("v_ready", ()):
                pe.wait_ge(s, v)
            if b["first"] and head >= 2:
                pe.wait_ge(dve_done, at("dve", "head out", tag, head - 2))
            p0 = b["p0"]
            o = acc[p0:p0 + HD, head % 2, 0:S]
            if b["kind"] == "cmp":
                mm = pe.matmul(o, b["v"](0), a_probT[tag[0]][u % 2][0:15, 0:S], start=b["first"], stop=b["last"], skip_group_check=True)
            else:
                pe.matmul(o, b["v"](0), a_probT[tag[0]][u % 2][:, 0:S], start=b["first"], stop=False, skip_group_check=True)
                mm = pe.matmul(acc[p0:p0 + HD, head % 2, P:S], b["v"](1), a_probT[tag[0]][u % 2][:, S:S + P],
                               start=False, stop=b["last"], skip_group_check=True)
            mm.then_inc(pe_done, up("pe", "value", tag, u))

        def att_pe(pe, tag, branches, beside=lambda u: None):
            att_scores_pe(pe, tag, 0, branches[0])
            heads = head_numbers(branches)
            for u in range(len(branches) + 1):
                if u + 1 < len(branches):
                    att_scores_pe(pe, tag, u + 1, branches[u + 1])
                if u >= 1:
                    att_value_pe(pe, tag, u - 1, branches[u - 1], heads[u - 1])
                if u < len(branches):
                    beside(u)
                    att_turn_pe(pe, tag, u, branches[u])

        def head_numbers(branches):
            n, outs = -1, []
            for b in branches:
                n += b["first"]
                outs.append(n)
            return outs

        def att_dve(dve, tag, branches, beside=lambda u: None):
            heads = head_numbers(branches)

            def masked(u, b):
                dve.wait_ge(pe_done, at("pe", "scores", tag, u))
                for s, v in b["mask_ready"]:
                    dve.wait_ge(s, v)
                if u >= 2:
                    dve.wait_ge(act_done, at("act", "exp", tag, u - 2))
                for t, (lo, hi) in enumerate(spans(b["kind"])):
                    dve.tensor_tensor_reduce(out=a_score[tag[0]][u % 2][:, lo:hi], in0=wrk[:, u % 2, lo:hi], in1=b["mask"][:, lo:hi],
                                             scale=b["scale"], scalar=3 * NEG, op0=ALU.add, op1=ALU.max,
                                             accum_out=a_stat(u, 0)[:, t:t + 1]).then_inc(dve_done, up("dve"))
                settle(dve, "dve", dve_done)
                dve.tensor_scalar(a_stat(u, 1), a_stat(u, 0), -1.0, None, ALU.mult).then_inc(dve_done, up("dve", "masked", tag, u))

            def probs(u, b):
                dve.wait_ge(act_done, at("act", "exp", tag, u))
                if b["kind"] == "cmp":
                    for t, (lo, hi) in enumerate(spans("cmp")):
                        dve.tensor_tensor_reduce(out=a_prob[tag[0]][u % 2][:, lo:hi], in0=a_prob[tag[0]][u % 2][:, lo:hi],
                                                 in1=K("cmp_see")[:, lo:hi], scale=1.0, scalar=0.0, op0=ALU.mult, op1=ALU.add,
                                                 accum_out=a_stat(u, 2)[:, t:t + 1]).then_inc(dve_done, up("dve"))
                    settle(dve, "dve", dve_done)
                    dve.tensor_scalar(a_stat(u, 2), a_stat(u, 2), 1e-30, None, ALU.max).then_inc(dve_done, up("dve"))
                    settle(dve, "dve", dve_done)
                dve.reciprocal(a_stat(u, 3), a_stat(u, 2)).then_inc(dve_done, up("dve"))
                settle(dve, "dve", dve_done)
                for t, (lo, hi) in enumerate(spans(b["kind"])):
                    if b["gate"] is None:
                        ins = dve.tensor_scalar(a_prob[tag[0]][u % 2][:, lo:hi], a_prob[tag[0]][u % 2][:, lo:hi], a_stat(u, 3)[:, t:t + 1],
                                                None, ALU.mult)
                    else:
                        ins = dve.tensor_scalar(a_prob[tag[0]][u % 2][:, lo:hi], a_prob[tag[0]][u % 2][:, lo:hi], a_stat(u, 3)[:, t:t + 1],
                                                b["gate"](t), ALU.mult, ALU.mult)
                    ins.then_inc(dve_done, up("dve", "probs", tag, u) if t else up("dve"))

            masked(0, branches[0])
            for u, b in enumerate(branches):
                if u + 1 < len(branches):
                    masked(u + 1, branches[u + 1])
                probs(u, b)
                if u >= 1 and branches[u - 1]["last"]:
                    head_out(dve, tag, u - 1, branches[u - 1], heads[u - 1])
                beside(u)
            head_out(dve, tag, len(branches) - 1, branches[-1], heads[-1])

        def head_out(dve, tag, u, b, head):
            dve.wait_ge(pe_done, at("pe", "value", tag, u))
            dve.tensor_copy(b["place"], acc[b["p0"]:b["p0"] + HD, head % 2, 0:S]).then_inc(dve_done, up("dve", "head out", tag, head))

        def att_act(act, tag, branches, beside=lambda u: None):
            def exps(u, b):
                act.wait_ge(dve_done, at("dve", "masked", tag, u))
                if u >= 2:
                    act.wait_ge(pe_done, at("pe", "turned", tag, u - 2))
                for t, (lo, hi) in enumerate(spans(b["kind"])):
                    act.activation(a_prob[tag[0]][u % 2][:, lo:hi], a_score[tag[0]][u % 2][:, lo:hi], ACT.Exp, bias=a_stat(u, 1)[:, t:t + 1],
                                   accum_out=a_stat(u, 2)[:, t:t + 1])\
                       .then_inc(act_done, up("act", "exp", tag, u) if t else up("act"))

            exps(0, branches[0])
            for u, b in enumerate(branches):
                if u + 1 < len(branches):
                    exps(u + 1, branches[u + 1])
                beside(u)
                act.wait_ge(pe_done, at("pe", "turned", tag, u))
                if u >= 2:
                    act.wait_ge(pe_done, at("pe", "value", tag, u - 2))
                if b["kind"] == "cmp":
                    ins = act.activation(a_probT[tag[0]][u % 2][0:15, 0:S], wrk[0:15, 2 + u % 2, 0:S], ACT.Copy)
                else:
                    ins = act.activation(a_probT[tag[0]][u % 2], wrk[:, 2 + u % 2, 0:384], ACT.Copy)
                ins.then_inc(act_done, up("act", "probT", tag, u))

        b_q, b_kk, b_f, b_g = Z(0, 3, S), Z(768, 3, S), Z(1536, 3, S), Z(2304, 3, S)
        b_i, c_u, c_v = Z(3072, 2, 384), Z(3840, 2, S), Z(4352, 2, S)
        s_q, s_k, s_iq, s_ik = Z(4864, 3, S), Z(5632, 1, S), Z(5888, 2, S), Z(6400, 1, S)
        s_v, s_iw = Z(6656, 2, HD), Z(6784, 2, 4)
        s_mask, s_work = flat_h[:, 0:384], flat_h[:, 384:768]
        s_relu = [flat_h[:, 768:1152], flat_h[:, 1152:1536]]

        def plan1(l):
            items = [("in1", l, i) for i in range(len(IN1))]
            w = [w_cols(items[i], b - a) for i, (a, b) in enumerate(IN1)]

            def cols(i, c, n):
                return lambda k: w[i][:, k, c:c + n]

            def both(tile, scale=1.0):
                return [(tile[HD * p:HD * p + HD, 0, :], ACT.Copy, scale) for p in range(2)]

            plan = []
            plan += [(f"bi{t}", items[4], f"t{t}", cols(4, 0, 384), 384, 0, [(b_i[:, t, :], ACT.Copy, 1.0)]) for t in range(2)]
            plan += [(f"bq{j}", items[2], "f", cols(2, P * j, P), P, 0, [(b_q[:, j, :], ACT.Copy, 1.0)]) for j in range(3)]
            plan += [(f"bf{j}", items[3], "f", cols(3, P * j, P), P, 0,
                      [(b_f[:, j, :], ACT.Sigmoid, 1.0), (b_kk[:, j, :], ACT.Sigmoid, -1.0)]) for j in range(3)]
            plan += [(f"aq{j}", items[0], "f", cols(0, P * j, P), P, 0, [(s_q[:, j, :], ACT.Copy, 1.0)]) for j in range(3)]
            plan += [("ak", items[0], "f", cols(0, 384, HD), HD, 0, both(s_k))]
            plan += [(f"av{t}", items[0], f"t{t}", cols(0, 448, HD), HD, 0, [(s_v[:, t, :], ACT.Copy, 1.0)]) for t in range(2)]
            plan += [(f"iq{j}", items[1], "f", cols(1, P * j, P), P, 0, [(s_iq[:, j, :], ACT.Copy, 1.0)]) for j in range(2)]
            plan += [("ik", items[1], "f", cols(1, 256, HD), HD, 0, both(s_ik))]
            plan += [(f"iw{t}", items[1], f"t{t}", cols(1, 320, 4), 4, 0, [(s_iw[:, t, :], ACT.Copy, 0.5)]) for t in range(2)]
            plan += [(f"bg{j}", items[5], "f", cols(5, P * j, P), P, 0, [(b_g[:, j, :], ACT.Silu, 1.0)]) for j in range(3)]
            plan += [(f"cu{j}", items[6], "f", cols(6, P * j, P), P, 0, [(c_u[:, j, :], ACT.Gelu, 1.0)]) for j in range(2)]
            plan += [(f"cv{t}", items[6], f"t{t}", cols(6, 256, 256), 256, 0, [(c_v[:, t, :], ACT.Gelu, 1.0)]) for t in range(2)]
            return plan

        def rope1(l):
            tiles = [("iq0", s_iq[:, 0, :]), ("iq1", s_iq[:, 1, :]), ("ik", s_ik[:, 0, :])]
            tiles += [(f"aq{j}", s_q[:, j, :]) for j in range(3)] + [("ak", s_k[:, 0, :])]
            return [(name, tile, "turn64", 0, 0, P) for name, tile in tiles]

        def index_pe(pe, l):
            pe.wait_ge(dve_done, at("dve", "band", l, C - 1))
            for h in range(4):
                p0 = HD * (h % 2)
                q, k = s_iq[p0:p0 + HD, h // 2, :], s_ik[p0:p0 + HD, 0, :]
                pe.matmul(wrk[:, h, 0:P], q[:, T0], k[:, T0], start=True, stop=True)
                pe.matmul(wrk[:, h, P:384], q[:, T1], k[:, 0:S], start=True, stop=True)\
                  .then_inc(pe_done, up("pe", "index", l, h))

        def index_act(act, l):
            for h in range(4):
                act.wait_ge(pe_done, at("pe", "index", l, h))
                if h >= 2:
                    act.wait_ge(dve_done, at("dve", "index", l, h - 2))
                act.activation(s_relu[h % 2], wrk[:, h, 0:384], ACT.Relu, scale=IDX_SCALE).then_inc(act_done, up("act", "index", l, h))

        IDX_SCALE = float(HD) ** -0.5
        QT = ((0, P), (P, 384))

        def index_dve(dve, l):
            for h in range(4):
                dve.wait_ge(act_done, at("act", "index", l, h))
                for t, (lo, hi) in enumerate(QT):
                    if h == 0:
                        ins = dve.tensor_scalar(s_work[:, lo:hi], s_relu[0][:, lo:hi], s_iw[:, t, 0:1], None, ALU.mult)
                    else:
                        ins = dve.scalar_tensor_tensor(s_work[:, lo:hi], s_relu[h % 2][:, lo:hi], s_iw[:, t, h:h + 1],
                                                       s_work[:, lo:hi], ALU.mult, ALU.add)
                    ins.then_inc(dve_done, up("dve", "index", l, h) if t else up("dve"))
                settle(dve, "dve", dve_done)
            dve.tensor_tensor(s_work, s_work, K("causal"), ALU.add).then_inc(dve_done, up("dve"))
            for _ in range(TOPK // 8):
                settle(dve, "dve", dve_done)
                for t, (lo, hi) in enumerate(QT):
                    dve.max(stat[:, 8 * t:8 * t + 8], s_work[:, lo:hi]).then_inc(dve_done, up("dve"))
                settle(dve, "dve", dve_done)
                for t, (lo, hi) in enumerate(QT):
                    dve.match_replace(s_work[:, lo:hi], stat[:, 8 * t:8 * t + 8], s_work[:, lo:hi], TAKEN)\
                       .then_inc(dve_done, up("dve"))
            settle(dve, "dve", dve_done)
            dve.tensor_scalar(s_mask, s_work, TAKEN / 2, NEG, ALU.is_gt, ALU.mult).then_inc(dve_done, up("dve"))
            settle(dve, "dve", dve_done)
            dve.tensor_tensor(s_mask, s_mask, K("causal"), ALU.add).then_inc(dve_done, up("dve", "mask", l))

        def branches1(l):
            out = []
            for h in range(6):
                p0, j = HD * (h % 2), h // 2
                out.append(dict(q=s_q[p0:p0 + HD, j, :], k=s_k[p0:p0 + HD, 0, :], v=lambda t: s_v[:, t, :], mask=s_mask,
                                kind="causal", scale=float(HD) ** -0.5, gate=None, first=True, last=True, p0=p0,
                                place=mixT[p0:p0 + HD, j, :],
                                ready=[(dve_done, at("dve", "rope", ("1", l), "ak")), (act_done, at("act", "index", l, 3))] if h == 0 else [],
                                mask_ready=[(dve_done, at("dve", "mask", l))] if h == 0 else []))
            return out

        def gmlp_parts(l):
            s = slot_of(("gmlp", l))
            return (s[:, 0:256], s[:, 256:512], s[:, 512:1024].rearrange("p (g s) -> p g s", g=4), s[0:1, 1024:1536],
                    s[:, 1536:2048].rearrange("p (g t) -> p g t", g=4))

        def gmlp_turn_pe(pe, l):
            g_row, b_row, ws, bs, wsT = gmlp_parts(l)
            pe.wait_ge(*landing(("gmlp", l)))
            pe.wait_ge(act_done, now_act_read(l))
            for i in range(4):
                mm = pe.transpose(wrk[:, 2, i * P:(i + 1) * P], ws[:, i, :], ident)
            mm.then_inc(pe_done, up("pe", "ws turned", l))

        def gmlp_mix_pe(pe, l):
            g_row, b_row, ws, bs, wsT = gmlp_parts(l)
            pe.wait_ge(dve_done, at("dve", "wsT", l))
            pe.wait_ge(dve_done, at("dve", "cv", l))
            for j in range(2):
                for p in range(2):
                    i, p0 = 2 * j + p, HD * p
                    for n in range(2):
                        o = acc[p0:p0 + HD, j, n * P:(n + 1) * P]
                        pe.matmul(o, c_v[:, n, i * HD:(i + 1) * HD], wsT[:, i, :], start=True, stop=False, skip_group_check=True)
                        mm = pe.matmul(o, ones[0:1, 0:HD], bs[:, i * P:(i + 1) * P], start=False, stop=True, skip_group_check=True)
                if j == 0:
                    mm.then_inc(pe_done, up("pe", "mixed", l, j))
                else:
                    mm.then_inc(freed_by_pe, 1)

        def now_act_read(l):
            return at("act", "probT", ("1", l), 5)

        def gmlp_stats_dve(dve, l):
            dve.wait_ge(act_done, at("act", "proj", ("1", l), "cv1"))
            for t in range(2):
                dve.bn_stats(stat[:, 8 * t:8 * t + 6], c_v[:, t, :]).then_inc(dve_done, up("dve"))
            settle(dve, "dve", dve_done)
            for t in range(2):
                dve.bn_aggr(stat[:, 16 + 2 * t:18 + 2 * t], stat[:, 8 * t:8 * t + 6]).then_inc(dve_done, up("dve"))
            settle(dve, "dve", dve_done)
            for t in range(2):
                dve.tensor_scalar(stat[:, 20 + t:21 + t], stat[:, 17 + 2 * t:18 + 2 * t], EPS, None, ALU.add)\
                   .then_inc(dve_done, up("dve", "cv variance", l) if t else up("dve"))

        def gmlp_norm_dve(dve, l):
            g_row, b_row, ws, bs, wsT = gmlp_parts(l)
            inverse_root_dve(dve, ("cv root", l), stat[:, 20:22])
            settle(dve, "dve", dve_done)
            for t in range(2):
                dve.tensor_scalar(c_v[:, t, :], c_v[:, t, :], stat[:, 16 + 2 * t:17 + 2 * t], stat[:, 20 + t:21 + t],
                                  ALU.subtract, ALU.mult).then_inc(dve_done, up("dve"))
            dve.wait_ge(*landing(("gmlp", l)))
            settle(dve, "dve", dve_done)
            dve.tensor_tensor(c_v, c_v, g_row.unsqueeze(1).broadcast_to([P, 2, S]), ALU.mult).then_inc(dve_done, up("dve"))
            settle(dve, "dve", dve_done)
            dve.tensor_tensor(c_v, c_v, b_row.unsqueeze(1).broadcast_to([P, 2, S]), ALU.add).then_inc(dve_done, up("dve", "cv", l))
            dve.wait_ge(pe_done, at("pe", "ws turned", l))
            dve.tensor_tensor(wsT, wrk[:, 2, :].rearrange("p (g t) -> p g t", g=4),
                              K("upper").unsqueeze(1).broadcast_to([P, 4, P]), ALU.mult).then_inc(dve_done, up("dve", "wsT", l))

        def gmlp_out_dve(dve, l):
            for j in range(2):
                if j == 0:
                    dve.wait_ge(pe_done, at("pe", "mixed", l, 0))
                else:
                    dve.wait_ge(freed_by_pe, freeing(("gmlp", l)))
                dve.tensor_tensor(mixT[:, 6 + j, :], acc[:, j, 0:S], c_u[:, j, :], ALU.mult).then_inc(dve_done, up("dve", "c out", l, j))

        def grid(v):
            return v.rearrange("p a (b c) -> p (a b) c", c=C)

        NP3 = 3 * NB
        r_w = [b_kk, Z(6800, 3, S)]
        r_kdec, r_v = Z(7568, 3, S), Z(8336, 3, S)
        r_qw = [Z(9104, 768), Z(9872, 768)]
        r_t, r_p, r_o = Z(10640, 3, S), Z(11408, 3, S), mixT[:, 3:6, :]
        r_state = Z(6800, 3, NB * HD).rearrange("p a (b v) -> p a b v", v=HD)
        r_kT = Z(10640, 6, P)
        r_pick = [Z(o, P // C, HD) for o in (0, 512, 1024, 9872)]
        r_whole = stat[:, 64:64 + NP3]

        def band(j):
            n = C - j
            return n, r_qw[j % 2][:, 0:NP3 * n].rearrange("p (a c) -> p a c", c=n)

        def band_psum(j, half):
            n = C - j
            return wrk[:, 2 * (j % 2) + half, 0:24 * n]

        wrkv = wrk[:, :, :].rearrange("p b (h t) -> p (b h) t", t=S)

        def turn_values_pe(pe, l):
            pe.wait_ge(act_done, at("act", "proj", ("1", l), "bi1"))
            for a in range(3):
                for t in range(2):
                    mm = pe.transpose(wrkv[:, a, t * P:(t + 1) * P], b_i[:, t, a * P:(a + 1) * P], ident)
            mm.then_inc(pe_done, up("pe", "v turned", l))

        def band_pe(pe, l, j):
            n, qw = band(j)
            if j == 0:
                pe.wait_ge(act_done, at("act", "v", l))
            pe.wait_ge(dve_done, at("dve", "qw", l, j))
            if j >= 2:
                pe.wait_ge(dve_done, at("dve", "band", l, j - 2))
            for half in range(2):
                mm = pe.matmul(band_psum(j, half), headsum, r_qw[j % 2][:, 24 * n * half:24 * n * (half + 1)],
                               start=True, stop=True)
            mm.then_inc(pe_done, up("pe", "band", l, j))

        def turn_keys_pe(pe, l):
            pe.wait_ge(act_done, at("act", "kdec", l))
            if l == 0:
                pe.wait_ge(dve_done, at("dve", "mods", 0, 9))
            for a in range(3):
                for t in range(2):
                    mm = pe.transpose(accv[:, a, t * P:(t + 1) * P], r_kdec[:, a, t * P:(t + 1) * P], ident)
            mm.then_inc(pe_done, up("pe", "k turned", l))

        def kv_pe(pe, l, a):
            if a == 0:
                pe.wait_ge(act_done, at("act", "kT", l))
                pe.wait_ge(act_done, at("act", "proj", ("1", l), "cv1"))
            else:
                pe.wait_ge(act_done, at("act", "kv", l, a - 1))
            for n in range(4 * a, 4 * a + 4):
                h, t = n % 4 // 2, n % 2
                pe.wait_ge(dve_done, at("dve", "pick", l, n))
                pe.matmul(acc[HD * h:HD * h + HD, 2 + t, :], r_kT[:, 2 * a + t, HD * h:HD * h + HD],
                          r_pick[n % 4].rearrange("p b v -> p (b v)"), start=True, stop=True).then_inc(pe_done, up("pe", "kv", l, n))

        def kv_act(act, l, a):
            act.wait_ge(pe_done, at("pe", "kv", l, 4 * a + 3))
            act.activation(r_state[:, a, 1:NB, :].rearrange("p b v -> p (b v)"),
                           acc[:, 2:4, :].rearrange("p b n -> p (b n)")[:, 0:(NB - 1) * HD], ACT.Copy).then_inc(act_done, up("act", "kv", l, a))

        def inter_pe(pe, l):
            for a in range(3):
                pe.wait_ge(dve_done, at("dve", "states", l, 2))
                for b in range(NB):
                    for h in range(2):
                        rows = slice(HD * h, HD * h + HD)
                        mm = pe.matmul(accv[rows, 4 + a, b * C:(b + 1) * C], r_state[rows, a, b, :],
                                       r_p[rows, a, b * C:(b + 1) * C], start=True, stop=True, skip_group_check=True)
                mm.then_inc(pe_done, up("pe", "inter", l, a))

        def head_norm_pe(pe, l):
            pe.wait_ge(act_done, at("act", "o squares", l))
            for half in range(2):
                mm = pe.matmul(wrk[:, half, 0:384], headsum, r_qw[1][:, 384 * half:384 * (half + 1)], start=True, stop=True)
            mm.then_inc(pe_done, up("pe", "o sums", l))

        def turned_values_act(act, l):
            act.wait_ge(pe_done, at("pe", "v turned", l))
            act.activation(r_v, wrkv[:, 0:3, :], ACT.Copy).then_inc(act_done, up("act", "v", l))

        def block_keys_act(act, l, j):
            act.wait_ge(dve_done, at("dve", "w", l, j))
            act.activation(grid(r_kdec)[:, :, C - 1 - j:C - j], grid(r_w[j % 2])[:, :, C - 1:C], ACT.Copy)\
               .then_inc(act_done, up("act", "kdec", l) if j == C - 1 else up("act", "kdec part", l, j))

        def turned_keys_act(act, l):
            act.wait_ge(pe_done, at("pe", "k turned", l))
            act.wait_ge(dve_done, at("dve", "band end", l))
            act.activation(r_kT.rearrange("p (a t) d -> p a (t d)", t=2), accv[:, 0:3, :], ACT.Copy).then_inc(act_done, up("act", "kT", l))

        def head_squares_act(act, l):
            act.wait_ge(dve_done, at("dve", "o", l))
            act.activation(r_qw[1], r_o.rearrange("p a t -> p (a t)"), ACT.Square).then_inc(act_done, up("act", "o squares", l))

        def gates_dve(dve, l):
            dve.tensor_scalar(stat[:, 24:27], lower[:, l, :], -1.0, 1.0, ALU.mult, ALU.add).then_inc(dve_done, up("dve"))
            settle(dve, "dve", dve_done)
            for a in range(3):
                dve.wait_ge(act_done, at("act", "proj", ("1", l), f"bf{a}"))
                dve.tensor_scalar(b_f[:, a, :], b_f[:, a, :], stat[:, 24 + a:25 + a], lower[:, l, a:a + 1], ALU.mult, ALU.add)\
                   .then_inc(dve_done, up("dve"))
                dve.tensor_scalar(b_kk[:, a, :], b_kk[:, a, :], stat[:, 24 + a:25 + a], None, ALU.mult)\
                   .then_inc(dve_done, up("dve", "w", l, 0) if a == 2 else up("dve"))
            settle(dve, "dve", dve_done)
            dve.tensor_copy(grid(r_p)[:, :, 0:1], grid(b_f)[:, :, 0:1]).then_inc(dve_done, up("dve"))

        def weigh_dve(dve, l, j):
            f, q, p = grid(b_f), grid(b_q), grid(r_p)
            n, qw = band(j)
            if j:
                settle(dve, "dve", dve_done)
                if j >= 2:
                    dve.wait_ge(act_done, at("act", "kdec part", l, j - 2))
                dve.tensor_tensor(grid(r_w[j % 2])[:, :, j:C], grid(r_w[(j - 1) % 2])[:, :, j - 1:C - 1], f[:, :, j:C], ALU.mult)\
                   .then_inc(dve_done, up("dve", "w", l, j))
                dve.tensor_tensor(p[:, :, j:j + 1], p[:, :, j - 1:j], f[:, :, j:j + 1], ALU.mult).then_inc(dve_done, up("dve"))
                settle(dve, "dve", dve_done)
            if j >= 2:
                dve.wait_ge(pe_done, at("pe", "band", l, j - 2))
            dve.tensor_tensor(qw, q[:, :, j:C], grid(r_w[j % 2])[:, :, j:C], ALU.mult).then_inc(dve_done, up("dve", "qw", l, j))

        def band_dve(dve, l, j):
            v = grid(r_v)
            if j == 0:
                dve.wait_ge(act_done, at("act", "v", l))
            dve.wait_ge(pe_done, at("pe", "band", l, j))
            if j == C - 1:
                settle(dve, "dve", dve_done)
            n = C - j
            o = grid(r_o if j == 0 else r_t)[:, :, j:C]
            for half in range(2):
                dve.tensor_tensor(o[:, 24 * half:24 * half + 24, :], band_psum(j, half).rearrange("p (a c) -> p a c", c=n),
                                  v[:, 24 * half:24 * half + 24, 0:n], ALU.mult)\
                   .then_inc(dve_done, up("dve", "band", l, j) if half else up("dve"))
            if j:
                settle(dve, "dve", dve_done)
                dve.tensor_tensor(grid(r_o)[:, :, j:C], grid(r_o)[:, :, j:C], o, ALU.add)\
                   .then_inc(dve_done, up("dve", "band end", l) if j == C - 1 else up("dve"))

        def whole_decays_dve(dve, l):
            settle(dve, "dve", dve_done)
            dve.tensor_copy(r_whole, grid(r_p)[:, :, C - 1:C].rearrange("p a c -> p (a c)")).then_inc(dve_done, up("dve"))
            settle(dve, "dve", dve_done)
            dve.tensor_tensor(r_p, r_p, b_q, ALU.mult).then_inc(dve_done, up("dve"))
            settle(dve, "dve", dve_done)
            dve.wait_ge(act_done, at("act", "kdec", l))

        def picks_dve(dve, l, a):
            for n in range(4 * a, 4 * a + 4):
                h, t = n % 4 // 2, n % 2
                if n >= 4:
                    dve.wait_ge(pe_done, at("pe", "kv", l, n - 4))
                dve.tensor_tensor(r_pick[n % 4], K("blocks").unsqueeze(2).broadcast_to([P, P // C, HD]),
                                  b_i[:, t, (2 * a + h) * HD:(2 * a + h + 1) * HD].unsqueeze(1).broadcast_to([P, P // C, HD]),
                                  ALU.mult).then_inc(dve_done, up("dve", "pick", l, n))

        def states_dve(dve, l, first, last):
            if first == 1:
                dve.memset(r_state[:, :, 0, :], 0.0).then_inc(dve_done, up("dve"))
                dve.wait_ge(act_done, at("act", "kv", l, 2))
            for b in range(first, last + 1):
                settle(dve, "dve", dve_done)
                for a in range(3):
                    dve.scalar_tensor_tensor(r_state[:, a, b, :], r_state[:, a, b - 1, :], r_whole[:, a * NB + b - 1:a * NB + b],
                                             r_state[:, a, b, :], ALU.mult, ALU.add)\
                       .then_inc(dve_done, up("dve", "states", l, a) if b == NB - 1 else up("dve"))

        def head_sum_dve(dve, l):
            for a in range(3):
                dve.wait_ge(pe_done, at("pe", "inter", l, max(a, 1)))
                dve.tensor_tensor(r_o[:, a, :], r_o[:, a, :], accv[:, 4 + a, :], ALU.add)\
                   .then_inc(dve_done, up("dve", "o", l) if a == 2 else up("dve"))

        def head_mean_dve(dve, l):
            dve.wait_ge(pe_done, at("pe", "o sums", l))
            rt = r_t.rearrange("p a t -> p (a t)").rearrange("p (h n) -> p h n", h=2)
            dve.tensor_scalar(rt, wrk[:, 0:2, 0:384], 1.0 / HD, EPS, ALU.mult, ALU.add).then_inc(dve_done, up("dve", "o mean square", l))

        def head_norm_dve(dve, l):
            inverse_root_dve(dve, ("o root", l), r_t)
            settle(dve, "dve", dve_done)
            dve.tensor_tensor(r_o, r_o, r_t, ALU.mult).then_inc(dve_done, up("dve"))
            settle(dve, "dve", dve_done)
            dve.scalar_tensor_tensor(mixT[:, 3:6, :], r_o, column("onorm", l), b_g, ALU.mult, ALU.mult)\
               .then_inc(dve_done, up("dve", "b out", l))

        F_ACT = Z(0, 8, S)
        F_SIL = Z(2048, 4, S)
        def tile_base(kind, l):
            return {"dense": 0, "moe": F_DENSE // P, "mlp": F_DENSE // P + NE * UP_TILES + l * (D_FF // P)}[kind]

        def group_base(kind, l):
            n_d, n_e, n_m = (len(ffn_groups(w)) for w in (F_DENSE, F_EXPERT, D_FF))
            return {"dense": 0, "moe": n_d, "mlp": n_d + NE * n_e + l * n_m}[kind]

        def dense_items(g):
            return ("gate", g), ("up", g), ("down", g)

        def ffn_up_pe(pe, g, width, items, base, gbase):
            f, n = ffn_groups(width)[g]
            gate, up_ = items
            for j in range(n // P):
                i = base + 4 * g + j
                if i >= 3:
                    pe.wait_ge(ffn_act, i - 2)
                for item, lo in ((gate, 0), (up_, S)):
                    if item is None:
                        continue
                    if j == 0:
                        pe.wait_ge(*landing(item))
                    w = w_cols(item, n)
                    for k in range(KD):
                        if i == 0 and lo == 0:
                            pe.wait_ge(act_done, at("act", "h", ("ffn", 0), k))
                        mm = pe.matmul(wrk[:, i % 3, lo:lo + S], w[:, k, j * P:(j + 1) * P], hT[:, k, :],
                                       start=(k == 0), stop=(k == KD - 1))
                    if item is gate and j == n // P - 1:
                        mm.then_inc(freed_by_pe, 1)
                mm.then_inc(ffn_up, 1)

        def ffn_down_pe(pe, g, width, item, base, gbase, tag):
            groups = ffn_groups(width)
            f, n = groups[g]
            w = slot_of(item)[:, 0:n * KD].rearrange("p (j d) -> p j d", d=D)
            pe.wait_ge(*landing(item))
            pe.wait_ge(ffn_act, base + 4 * g + n // P)
            for m in range(KD):
                for j in range(n // P):
                    mm = pe.matmul(accv[:, m, :], w[:, j, m * P:(m + 1) * P], F_ACT[:, 4 * (g % 2) + j, :],
                                   start=(g == 0 and j == 0 and m % 2 == 0), stop=(g == len(groups) - 1 and j == n // P - 1),
                                   skip_group_check=True)
                if g == len(groups) - 1 and m in (1, 3, 5):
                    mm.then_inc(pe_done, up("pe", "down", tag, m))
            mm.then_inc(freed_by_pe, 1)

        def down_wait(tag, item, m):
            return (freed_by_pe, freeing(item)) if m >= 6 else (pe_done, at("pe", "down", tag, m | 1))

        def dense_pe(pe):
            n = len(ffn_groups(F_DENSE))
            for g in range(n + 1):
                if g < n:
                    ffn_up_pe(pe, g, F_DENSE, dense_items(g)[:2], 0, 0)
                if g >= 1:
                    ffn_down_pe(pe, g - 1, F_DENSE, dense_items(g - 1)[2], 0, 0, ("ffn", 0))
                if g < n:
                    for i in dense_ada(g):
                        ada_pe(pe, *DENSE_ADA[i])

        def dense_act(act):
            for i in range(F_DENSE // P):
                act.wait_ge(ffn_up, i + 1)
                if i >= 4:
                    act.wait_ge(ffn_act, i - 3)
                act.activation(F_SIL[:, i % 4, :], wrk[:, i % 3, 0:S], ACT.Silu).then_inc(ffn_silu, 1)

        def dense_dve(dve):
            groups = ffn_groups(F_DENSE)
            for g, (f, n) in enumerate(groups):
                if g >= 2:
                    dve.wait_ge(freed_by_pe, freeing(("down", g - 2)))
                for j in range(n // P):
                    i = 4 * g + j
                    dve.wait_ge(ffn_silu, i + 1)
                    dve.tensor_tensor(F_ACT[:, 4 * (g % 2) + j, :], F_SIL[:, i % 4, :], wrk[:, i % 3, S:2 * S], ALU.mult)\
                       .then_inc(ffn_act, 1)
                for i in dense_ada(g):
                    ada_dve(dve, *DENSE_ADA[i])
            ada_end_dve(dve, 1, 0, 11)
            ada_end_dve(dve, 0, 10, 11)
            for m in range(KD):
                dve.wait_ge(*down_wait(("ffn", 0), ("down", len(groups) - 1), m))
                dve.scalar_tensor_tensor(xT[:, m, :], accv[:, m, :], mods[:, 0, 40 + m:41 + m], xT[:, m, :], ALU.mult, ALU.add)\
                   .then_inc(dve_done, up("dve", "residual", ("ffn", 0), m))

        def out_items(kind, l):
            return [(kind, l, 0), (kind, l, 1)]

        def mod_col(l, o):
            return lambda k: mods[:, l, o + k:o + k + 1]

        def gain_col(i):
            return lambda k: gain[:, i, k:k + 1]

        def residual_of(tag):
            return lambda k: (dve_done, at("dve", "residual", tag, k))

        def x_ready(l):
            return residual_of(("ffn", 0)) if l else (lambda k: (act_done, at("act", "x")))

        def act_from(wait_names):
            return lambda name: at("act", "proj", wait_names, name)

        PLAN1_TILES, FIRST_BAND = 26, 8
        ADA_STEPS_DVE = {1: 6, 4: 7, 7: 8, 10: 9}
        ADA_STEPS_PE = {3: 6, 6: 7, 9: 8, 12: 9}

        def block1_pe(pe, l):
            tag = ("1", l)
            if l == 0:
                for i in range(2):
                    ada_pe(pe, 0, i)
            norm_pe(pe, ("mix", l))
            if l == 0:
                for i in range(2, 4):
                    ada_pe(pe, 0, i)
            plan = plan1(l)
            assert len(plan) == PLAN1_TILES
            for i in range(PLAN1_TILES):
                before = (act_done, at("act", "proj", tag, plan[i - 2][0])) if i >= 2 else None
                project_pe(pe, tag, plan, i, 2 + i % 2, before)
                if i in (FIRST_BAND - 2, FIRST_BAND - 1) and l == 0:
                    ada_pe(pe, 0, i - FIRST_BAND + 6)
                if i == FIRST_BAND - 1:
                    turn_values_pe(pe, l)
                j = i - FIRST_BAND
                if 0 <= j < C:
                    band_pe(pe, l, j)
                    if l == 0 and j in ADA_STEPS_PE:
                        ada_pe(pe, 0, ADA_STEPS_PE[j])
            turn_keys_pe(pe, l)
            pe.wait_ge(act_done, at("act", "kT", l))
            for a in range(3):
                kv_pe(pe, l, a)
            rope_pe(pe, tag, rope1(l), act_from(tag))
            index_pe(pe, l)

            def beside(u):
                if u == 5:
                    inter_pe(pe, l)

            att_pe(pe, tag, branches1(l), beside)
            gmlp_turn_pe(pe, l)
            head_norm_pe(pe, l)
            gmlp_mix_pe(pe, l)
            outproj_pe(pe, tag, out_items("out1", l), [(dve_done, at("dve", "c out", l, 1))])
            norm_pe(pe, ("ffn", l))

        def block1_act(act, l):
            tag = ("1", l)
            norm_act(act, ("mix", l), x_ready(l), gain_col(2 * l), mod_col(l, 0), None, [(dve_done, at("dve", "gain", l, 0))])
            plan = plan1(l)
            for i in range(PLAN1_TILES):
                project_act(act, tag, plan, i, 2 + i % 2)
                if i == 3 and l == 0:
                    tables_act(act)
                if i == FIRST_BAND - 1:
                    turned_values_act(act, l)
                j = i - FIRST_BAND
                if 0 <= j < C:
                    block_keys_act(act, l, j)
            turned_keys_act(act, l)
            for a in range(3):
                kv_act(act, l, a)
            index_act(act, l)
            att_act(act, tag, branches1(l))
            head_squares_act(act, l)
            root_act(act, at("dve", "cv variance", l), ("cv root", l), stat[:, 20:22])
            root_act(act, at("dve", "o mean square", l), ("o root", l), r_t)
            norm_act(act, ("ffn", l), residual_of(("mix", l)), gain_col(2 * l + 1), mod_col(l, 24),
                     None, [(dve_done, at("dve", "gain", l, 1))])

        def block1_dve(dve, l):
            tag = ("1", l)
            if l == 0:
                ada_dve(dve, 0, 0)
                vec_dve(dve)
                ada_dve(dve, 0, 1)
            norm_dve(dve, ("mix", l))
            if l == 0:
                ada_dve(dve, 0, 2)
                ada_dve(dve, 0, 3)
                ada_end_dve(dve, 0, 0, 3)
                tables_dve(dve)
                ada_dve(dve, 0, 4)
                ada_dve(dve, 0, 5)
            gates_dve(dve, l)
            weigh_dve(dve, l, 0)
            for j in range(C):
                if j + 1 < C:
                    weigh_dve(dve, l, j + 1)
                band_dve(dve, l, j)
                if l == 0 and j in ADA_STEPS_DVE:
                    ada_dve(dve, 0, ADA_STEPS_DVE[j])
            if l == 0:
                ada_end_dve(dve, 0, 4, 9)
            whole_decays_dve(dve, l)
            for a in range(3):
                picks_dve(dve, l, a)
            rope_dve(dve, tag, rope1(l), act_from(tag))
            index_dve(dve, l)

            def beside(u):
                if u < 5:
                    states_dve(dve, l, 1 + 3 * u, 3 + 3 * u)

            att_dve(dve, tag, branches1(l), beside)
            head_sum_dve(dve, l)
            gmlp_stats_dve(dve, l)
            head_mean_dve(dve, l)
            gmlp_norm_dve(dve, l)
            head_norm_dve(dve, l)
            gmlp_out_dve(dve, l)
            residual_dve(dve, ("mix", l), mod_col(l, 16), out_waits(tag, out_items("out1", l)))
            norm_dve(dve, ("ffn", l))

        m_h = Z(3072, 2, D)
        m_rows = Z(5120, 2, D)
        m_pick, m_wpick, m_wpickT = Z(7168, 2, S), Z(7680, 2, S), Z(8192, 2, S)
        m_logit, m_sel = Z(8704, 2, NE), Z(8720, 2, NE)
        gate_all, pos_all = Z(9088, 2, NE + 1), Z(9106, 2, NE + 1)
        m_gate, m_pos = gate_all[:, :, 0:NE], pos_all[:, :, 0:NE]
        m_cmp = [Z(8800 + 64 * i, NE, NE) for i in range(4)]
        m_part = Z(9072, 2, 4)
        m_many = sb("m_many", [1, NE], I32)
        y_sum = mixT
        MOE = tile_base("moe", 0)
        flat_mix = mixT[:, :, :].rearrange("p k t -> p (k t)")
        flat_acc = acc[:, :, :].rearrange("p b n -> p (b n)")

        def route_pe(pe):
            pe.wait_ge(act_done, at("act", "h", ("ffn", 1), KD - 1))
            pe.wait_ge(*landing(("router",)))
            wr = slot_of(("router",))[:, 0:64].rearrange("p (k e) -> p k e", k=KD)
            for t in range(2):
                for k in range(KD):
                    mm = pe.matmul(wrk[:, 3, t * NE:(t + 1) * NE], hT[:, k, t * P:(t + 1) * P], wr[:, k, :],
                                   start=(k == 0), stop=(k == KD - 1))
            mm.then_inc(freed_by_pe, 1)
            for t in range(2):
                for k in range(KD):
                    mm = pe.transpose(flat_acc[:, t * D + k * P:t * D + (k + 1) * P], hT[:, k, t * P:(t + 1) * P], ident)
            mm.then_inc(pe_done, up("pe", "h turned"))
            pe.wait_ge(dve_done, at("dve", "selected"))
            pe.matmul(wrk[:, 2, 0:NE], K("upper"), m_sel[:, 0, :], start=True, stop=True)
            pe.matmul(wrk[:, 2, NE:2 * NE], ones, m_sel[:, 0, :], start=True, stop=False)
            pe.matmul(wrk[:, 2, NE:2 * NE], K("upper"), m_sel[:, 1, :], start=False, stop=True)
            pe.matmul(wrk[0:1, 2, 2 * NE:3 * NE], ones[:, 0:1], m_sel[:, 0, :], start=True, stop=False)
            pe.matmul(wrk[0:1, 2, 2 * NE:3 * NE], ones[:, 0:1], m_sel[:, 1, :], start=False, stop=True).then_inc(pe_done, up("pe", "counted"))

        def route_act(act):
            act.wait_ge(pe_done, at("pe", "h turned"))
            act.activation(m_h.rearrange("p t d -> p (t d)"), flat_acc, ACT.Copy).then_inc(act_done, up("act", "h tokens"))
            act.wait_ge(dve_done, at("dve", "logits less max"))
            act.activation(m_gate, m_gate, ACT.Exp).then_inc(act_done, up("act", "router exp"))

        def route_dve(dve):
            dve.wait_ge(freed_by_pe, freeing(("router",)))
            dve.tensor_copy(m_logit, wrk[:, 3, 0:2 * NE].rearrange("p (t e) -> p t e", t=2)).then_inc(dve_done, up("dve"))
            settle(dve, "dve", dve_done)
            for t in range(2):
                own = m_logit[:, t, :].unsqueeze(2).broadcast_to([P, NE, NE])
                other = m_logit[:, t, :].unsqueeze(1).broadcast_to([P, NE, NE])
                dve.tensor_tensor(m_cmp[t], other, own, ALU.is_gt).then_inc(dve_done, up("dve"))
                dve.tensor_tensor(m_cmp[2 + t], other, own, ALU.is_equal).then_inc(dve_done, up("dve"))
            settle(dve, "dve", dve_done)
            for t in range(2):
                dve.tensor_tensor(m_cmp[2 + t], m_cmp[2 + t], K("before").rearrange("p (a b) -> p a b", a=NE), ALU.mult)\
                   .then_inc(dve_done, up("dve"))
            settle(dve, "dve", dve_done)
            for t in range(2):
                dve.tensor_tensor(m_cmp[t], m_cmp[t], m_cmp[2 + t], ALU.add).then_inc(dve_done, up("dve"))
                dve.tensor_reduce(m_part[:, t, 0:1], m_logit[:, t, :], AX, ALU.max).then_inc(dve_done, up("dve"))
            settle(dve, "dve", dve_done)
            for t in range(2):
                dve.tensor_reduce(m_sel[:, t, :], m_cmp[t], AX, ALU.add).then_inc(dve_done, up("dve"))
                dve.tensor_scalar(m_gate[:, t, :], m_logit[:, t, :], m_part[:, t, 0:1], None, ALU.subtract)\
                   .then_inc(dve_done, up("dve", "logits less max") if t else up("dve"))
            settle(dve, "dve", dve_done)
            dve.tensor_scalar(m_sel, m_sel, 1.5, None, ALU.is_lt).then_inc(dve_done, up("dve", "selected"))
            dve.wait_ge(act_done, at("act", "router exp"))
            settle(dve, "dve", dve_done)
            dve.tensor_tensor(m_gate, m_gate, m_sel, ALU.mult).then_inc(dve_done, up("dve"))
            settle(dve, "dve", dve_done)
            dve.tensor_reduce(m_part[:, :, 1:2].rearrange("p a b -> p (a b)"), m_gate, AX, ALU.add).then_inc(dve_done, up("dve"))
            settle(dve, "dve", dve_done)
            dve.reciprocal(m_part[:, :, 2:3], m_part[:, :, 1:2]).then_inc(dve_done, up("dve"))
            settle(dve, "dve", dve_done)
            for t in range(2):
                dve.tensor_scalar(m_gate[:, t, :], m_gate[:, t, :], m_part[:, t, 2:3], None, ALU.mult).then_inc(dve_done, up("dve"))
            dve.wait_ge(pe_done, at("pe", "counted"))
            dve.tensor_tensor(m_pos, wrk[:, 2, 0:2 * NE].rearrange("p (t e) -> p t e", t=2), m_sel, ALU.mult).then_inc(dve_done, up("dve"))
            dve.tensor_scalar(m_many[:, :], wrk[0:1, 2, 2 * NE:3 * NE], P + 0.5, None, ALU.is_gt).then_inc(dve_done, up("dve"))
            settle(dve, "dve", dve_done)
            dve.memset(pos_all[:, :, NE:NE + 1], -1.0).then_inc(dve_done, up("dve"))
            dve.memset(gate_all[:, :, NE:NE + 1], 0.0).then_inc(dve_done, up("dve"))
            dve.tensor_scalar(m_pos, m_pos, -1.0, None, ALU.add).then_inc(dve_done, up("dve", "routed"))
            dve.memset(mixT[:, :, :], 0.0).then_inc(share_added, 1)

        def by_count(eng, e, body):
            many = eng.value_load(m_many[0:1, bass.ds(e, 1)], min_val=0, max_val=1)
            with eng.If(many == 0):
                body(e, 1)
            with eng.Else():
                body(e, 2)

        def experts_pe(pe):
            groups = ffn_groups(F_EXPERT)
            base = MOE

            def arrive(e, item):
                n = PLACE[item]
                mine = (n - FIRST_EXPERT) // SLOTS + 1
                pe.wait_ge(landed[n % SLOTS], e * (16 * (len(EXPERTS) // SLOTS)) + (at_experts[n % SLOTS] + 16 * mine))

            def rise(e, g, width):
                for j in range(4):
                    i = base + 4 * g + j
                    pe.wait_ge(ffn_act, e * UP_TILES + (i - 3))
                    for item, lo in ((("egate", g), 0), (("eup", g), S)):
                        if j == 0:
                            arrive(e, item)
                        w = w_cols(item, 512)
                        for k in range(KD):
                            mm = pe.matmul(wrk[:, j, lo:lo + width], w[:, k, j * P:(j + 1) * P], hT[:, k, 0:width],
                                           start=(k == 0), stop=(k == KD - 1))
                        if lo == 0 and j == 3:
                            mm.then_inc(freed_by_pe, 1)
                    mm.then_inc(ffn_up, 1)

            def fall(e, g, blocks):
                arrive(e, ("edown", g))
                w = slot_of(("edown", g)).rearrange("p (j d) -> p j d", d=D)
                pe.wait_ge(ffn_act, e * UP_TILES + (base + 4 * g + 4))
                if g == 0:
                    pe.wait_ge(share_added, e + 1)
                if g == len(groups) - 1:
                    for b in range(blocks):
                        for t in range(2):
                            mm = pe.transpose(wrk[:, 3, b * S + t * P:b * S + (t + 1) * P], m_wpick[:, t, b * P:(b + 1) * P], ident)
                    mm.then_inc(pick_turned, 1)
                for b in range(blocks):
                    for n in range(2):
                        for j in range(4):
                            mm = pe.matmul(acc[:, 2 * b + n, :], F_ACT[:, 4 * (g % 2) + j, b * P:(b + 1) * P],
                                           w[:, j, n * 512:(n + 1) * 512], start=(g == 0 and j == 0),
                                           stop=(g == len(groups) - 1 and j == 3), skip_group_check=True)
                mm.then_inc(freed_by_pe, 1)

            def expert(e, blocks):
                width = blocks * P
                pe.wait_ge(picked, e * 4 + 4)
                for k in range(KD):
                    for t in range(2):
                        mm = pe.matmul(wrkv[:, k, 0:width], m_h[:, t, k * P:(k + 1) * P], m_pick[:, t, 0:width],
                                       start=(t == 0), stop=(t == 1))
                mm.then_inc(gathered, 1)
                pe.wait_ge(tokens_ready, e + 1)
                for g in range(len(groups) + 1):
                    if g < len(groups):
                        rise(e, g, width)
                    if g >= 1:
                        fall(e, g - 1, blocks)
                pe.wait_ge(pick_ready, e + 1)
                pe.wait_ge(rows_ready, e + 1)
                for k in range(KD):
                    for b in range(blocks):
                        mm = pe.matmul(accv[:, k, :], m_rows[:, b, k * P:(k + 1) * P], m_wpickT[:, b, :],
                                       start=(b == 0), stop=(b == blocks - 1))
                mm.then_inc(scattered, 1)

            pe.wait_ge(act_done, at("act", "h tokens"))
            pe.wait_ge(dve_done, at("dve", "routed"))
            with pe.Fori(0, NE) as e:
                by_count(pe, e, expert)

        def experts_act(act):
            n = len(ffn_groups(F_EXPERT))

            def expert(e, blocks):
                width = blocks * P
                act.wait_ge(gathered, e + 1)
                act.activation(hT[:, :, 0:width], wrkv[:, :, 0:width], ACT.Copy).then_inc(tokens_ready, 1)
                for i in range(UP_TILES):
                    act.wait_ge(ffn_up, e * UP_TILES + (MOE + i + 1))
                    act.wait_ge(ffn_act, e * UP_TILES + (MOE + i - 3))
                    act.activation(F_SIL[:, i % 4, 0:width], wrk[:, i % 4, 0:width], ACT.Silu).then_inc(ffn_silu, 1)
                act.wait_ge(pick_turned, e + 1)
                act.activation(m_wpickT[:, 0:blocks, :].rearrange("p b t -> p (b t)"), wrk[:, 3, 0:blocks * S], ACT.Copy)\
                   .then_inc(pick_ready, 1)
                act.wait_ge(freed_by_pe, e * FREED + freeing(("edown", n - 1)))
                act.activation(m_rows[:, 0:blocks, :].rearrange("p b d -> p (b d)"), flat_acc[:, 0:blocks * D], ACT.Copy)\
                   .then_inc(rows_ready, 1)

            act.wait_ge(dve_done, at("dve", "routed"))
            with act.Fori(0, NE) as e:
                by_count(act, e, expert)

        def experts_dve(dve):
            def pick(e):
                for t in range(2):
                    pos_, gate_ = (v[:, t, bass.ds(e, 1)] for v in (pos_all, gate_all))
                    dve.tensor_scalar(m_pick[:, t, :], K("slot_ids"), pos_, None, ALU.is_equal).then_inc(picked, 1)
                    dve.tensor_scalar(m_wpick[:, t, :], K("slot_ids"), pos_, gate_, ALU.is_equal, ALU.mult).then_inc(picked, 1)

            def expert(e, blocks):
                width = blocks * P
                for i in range(UP_TILES):
                    g, j = i // 4, i % 4
                    if j == 0 and g >= 2:
                        dve.wait_ge(freed_by_pe, e * FREED + freeing(("edown", g - 2)))
                    dve.wait_ge(ffn_silu, e * UP_TILES + (MOE + i + 1))
                    dve.tensor_tensor(F_ACT[:, 4 * (g % 2) + j, 0:width], F_SIL[:, j, 0:width], wrk[:, j, S:S + width], ALU.mult)\
                       .then_inc(ffn_act, 1)
                dve.wait_ge(pick_turned, e + 1)
                pick(e + 1)
                dve.wait_ge(scattered, e + 1)
                dve.tensor_tensor(y_sum[:, :, :], accv, y_sum[:, :, :], ALU.add).then_inc(share_added, 1)

            settle(dve, "dve", dve_done)
            dve.wait_ge(share_added, 1)
            pick(0)
            with dve.Fori(0, NE) as e:
                by_count(dve, e, expert)

        def experts_end_dve(dve):
            dve.wait_ge(share_added, NE + 1)
            for m in range(KD):
                dve.scalar_tensor_tensor(xT[:, m, :], y_sum[:, m, :], mods[:, 1, 40 + m:41 + m], xT[:, m, :], ALU.mult, ALU.add)\
                   .then_inc(dve_done, up("dve", "residual", ("ffn", 1), m))

        n_q, n_ks, n_kw, n_kc, n_vc = Z(0, 3, S), Z(768, 1, S), Z(1024, 1, S), Z(1280, 1, S), Z(1536, 1, S)
        n_vs, n_vw, n_gate = Z(1792, 2, P), Z(2048, 2, P), Z(2304, 2, 18)
        l_cq, l_ckv, l_kpe = Z(2344, 2, S), Z(2856, 1, S), Z(3112, 1, S)
        l_q = Z(3368, 5, S)
        t_q, t_k, t_g, t_v = Z(4648, 3, S), Z(5416, 3, S), Z(6184, 3, S), Z(6952, 2, 320)
        n_hid, n_kcT, n_vcT = Z(7592, 2, 32), Z(7656, 16), Z(7672, P)
        l_tmp = Z(7800, 640)
        n_blk = Z(8448, 2, 16, 30)
        l_k = flat_h[:, 0:1280].rearrange("p (h t) -> p h t", h=5)
        l_v = flat_h[:, 1280:1920].rearrange("p (t n) -> p t n", t=2)

        def plan2(l):
            items = [("in2", l, i) for i in range(len(IN2))]
            w = [w_cols(items[i], b - a) for i, (a, b) in enumerate(IN2)]

            def cols(i, c, n):
                return lambda k: w[i][:, k, c:c + n]

            def tile(name, i, c, place, func=ACT.Copy, scale=1.0, m=P, p0=0):
                return (name, items[i], "f", cols(i, c, m), m, p0, [(place[p0:p0 + m], func, scale)])

            def rows(name, i, c, n, place, func=ACT.Copy):
                return [(f"{name}{t}", items[i], f"t{t}", cols(i, c, n), n, 0, [(place[:, t, 0:n], func, 1.0)]) for t in range(2)]

            def heads5(name, i, c, place, func=ACT.Copy, scale=1.0):
                return [tile(name + "0", i, c, place[:, 0, :], func, scale, HD, HD),
                        tile(name + "1", i, c + HD, place[:, 1, :], func, scale),
                        tile(name + "2", i, c + HD + P, place[:, 2, :], func, scale)]

            plan = [tile(f"nq{j}", 0, P * j, n_q[:, j, :]) for j in range(3)] + [tile("nkc", 0, 384, n_kc[:, 0, :])]
            plan += [tile("nvc", 1, 0, n_vc[:, 0, :]), tile("nks", 1, 128, n_ks[:, 0, :])]
            plan += rows("nvs", 1, 256, P, n_vs) + [tile("nkw", 1, 384, n_kw[:, 0, :])]
            plan += rows("nvw", 2, 0, P, n_vw) + rows("ng", 2, 128, 18, n_gate, ACT.Sigmoid)
            plan += [tile(f"cq{j}", 2, 146 + P * j, l_cq[:, j, :]) for j in range(2)]
            plan += [tile("ckv", 3, 0, l_ckv[:, 0, :]), tile("kpe", 3, 128, l_kpe[:, 0, :], m=32, p0=64)]
            plan += heads5("rq", 3, 160, t_q) + heads5("rk", 4, 0, t_k, ACT.Copy, float(HD) ** -0.5)
            plan += rows("rv", 5, 0, 320, t_v) + heads5("rg", 6, 0, t_g, ACT.Silu)
            return plan

        def rope2(l):
            plan = [("nkc", n_kc[:, 0, :], "turn16", 2, 0, P), ("nks", n_ks[:, 0, :], "turn16", 2, 0, P),
                    ("nkw", n_kw[:, 0, :], "turn16", 2, 0, P)]
            plan += [(f"nq{j}", n_q[:, j, :], "turn16", 2, 0, P) for j in range(3)]
            plan += [("kpe", l_kpe[64:96, 0, :], "turn32", 3, 64, 32)]
            for n, z in (("rq", t_q), ("rk", t_k)):
                plan += [(n + "0", z[HD:P, 0, :], "turn64", 1, HD, HD)]
                plan += [(f"{n}{j}", z[:, j, :], "turn64", 1, 0, P) for j in (1, 2)]
            return plan

        def rope_mla(l):
            return [(f"mq{h}", l_q[0:96, h, :], "turn32", 3, 0, 96) for h in range(5)]

        def cmp_blocks_act(act, l):
            act.wait_ge(dve_done, at("dve", "rope", ("2", l), "nkc"))
            for a, src in enumerate((n_kc, n_vc)):
                for g_ in range(2):
                    v = src[HD * g_:HD * g_ + HD, 0, :].rearrange("p (c b) -> p b c", b=16)
                    for par in range(2):
                        for later in range(2):
                            act.activation(n_blk[HD * par:HD * par + HD, a, 8 * later:8 * later + 8, 15 * g_:15 * g_ + 15],
                                           v[:, par:16:2, later:later + 15], ACT.Copy)\
                               .then_inc(act_done, up("act", "blocks", l) if (a, g_, par, later) == (1, 1, 1, 1) else up("act"))

        def cmp_act(act, l):
            act.wait_ge(pe_done, at("pe", "hidden", l))
            act.activation(n_hid[:, :, 0:30], wrk[:, 0, 0:64].rearrange("p (a n) -> p a n", a=2)[:, :, 0:30], ACT.Gelu_apprx_tanh)\
               .then_inc(act_done, up("act", "hidden", l))
            act.wait_ge(freed_by_pe, freeing(("cmp", l)))
            act.activation(n_kcT[:, 0:15], wrk[:, 1, 0:15], ACT.Copy).then_inc(act_done, up("act"))
            act.activation(n_vcT[0:15, :], wrk[0:15, 2, 0:P], ACT.Copy).then_inc(act_done, up("act", "compressed", l))

        def cmp_dve(dve, l):
            dve.wait_ge(act_done, at("act", "blocks", l))
            for a, name in enumerate(("cmp_pos_k_2", "cmp_pos_v_2")):
                dve.tensor_tensor(n_blk[:, a], n_blk[:, a], columns(name, 16 * l, 16).unsqueeze(2).broadcast_to([P, 16, 30]), ALU.add)\
                   .then_inc(dve_done, up("dve", "blocks", l) if a else up("dve"))

        def cmp_hidden_pe(pe, l):
            w1 = slot_of(("cmp", l)).rearrange("p (a j h) -> p a j h", a=2, j=16)
            pe.wait_ge(*landing(("cmp", l)))
            pe.wait_ge(dve_done, at("dve", "blocks", l))
            for a in range(2):
                for j in range(16):
                    mm = pe.matmul(wrk[:, 0, 32 * a:32 * a + 30], w1[:, a, j, :], n_blk[:, a, j, :], start=(j == 0), stop=(j == 15))
            mm.then_inc(pe_done, up("pe", "hidden", l))

        def cmp_out_pe(pe, l):
            w2 = slot_of(("mla", l))[:, 1600:1728]
            pe.wait_ge(*landing(("mla", l)))
            pe.wait_ge(act_done, at("act", "hidden", l))
            for g_ in range(2):
                mm = pe.matmul(wrk[HD * g_:HD * g_ + HD, 1, 0:15], w2[:, 0:HD], n_hid[:, 0, 15 * g_:15 * g_ + 15], start=True, stop=True)
            for g_ in range(2):
                mm = pe.matmul(wrk[0:15, 2, HD * g_:HD * g_ + HD], n_hid[:, 1, 15 * g_:15 * g_ + 15], w2[:, HD:P], start=True, stop=True)
            mm.then_inc(freed_by_pe, 1)

        def mla_entries(l):
            s = slot_of(("mla", l))
            uq = s[:, 0:960].rearrange("p (k f) -> p k f", k=2)
            ukv = s[:, 960:1600]
            out = []
            for h in range(5):
                out.append((f"mq{h}", 96, S, [(uq[:, k, 96 * h:96 * h + 96], l_cq[:, k, :]) for k in range(2)], l_q[0:96, h, :]))
            for h in range(5):
                out.append((f"mk{h}", HD, S, [(ukv[:, P * h:P * h + HD], l_ckv[:, 0, :])], l_k[0:HD, h, :]))
            v_cols = ukv.rearrange("p (h c) -> p h c", c=P)[:, :, HD:P]
            for t in range(2):
                out.append((f"mv{t}", P, 320, [(l_ckv[:, 0, t * P:(t + 1) * P], v_cols)], l_v[:, t, :]))
            return out

        l_tmp3 = Z(10752, 3, S)

        def latent_sums_pe(pe, l, bank, bank_read):
            pe.wait_ge(act_done, at("act", "latent squares", l))
            pe.wait_ge(*bank_read)
            pe.matmul(acc[:, bank, 0:S], ones, l_tmp3[:, 0, :], start=True, stop=False)
            pe.matmul(acc[:, bank, 0:S], ones, l_tmp3[:, 1, :], start=False, stop=True)
            pe.matmul(acc[:, bank, S:2 * S], ones, l_tmp3[:, 2, :], start=True, stop=True).then_inc(pe_done, up("pe", "latent sums", l))

        def latent_squares_act(act, l):
            act.wait_ge(act_done, at("act", "proj", ("2", l), "ckv"))
            act.activation(l_tmp3[:, 0:2, :], l_cq, ACT.Square).then_inc(act_done, up("act"))
            act.activation(l_tmp3[:, 2:3, :], l_ckv, ACT.Square).then_inc(act_done, up("act", "latent squares", l))

        def latent_sums_dve(dve, l, bank):
            dve.wait_ge(pe_done, at("pe", "latent sums", l))
            dve.tensor_scalar(l_tmp[:, 0:S], acc[:, bank, 0:S], 1.0 / 256, EPS, ALU.mult, ALU.add).then_inc(dve_done, up("dve"))
            dve.tensor_scalar(l_tmp[:, S:2 * S], acc[:, bank, S:2 * S], 1.0 / 128, EPS, ALU.mult, ALU.add)\
               .then_inc(dve_done, up("dve", "latent mean squares", l))

        def latents_dve(dve, l):
            inverse_root_dve(dve, ("latent root", l), l_tmp[:, 0:512])
            settle(dve, "dve", dve_done)
            for k in range(2):
                dve.scalar_tensor_tensor(l_cq[:, k, :], l_cq[:, k, :], column("mla_q_norm_2", 2 * l + k), l_tmp[:, 0:S],
                                         ALU.mult, ALU.mult).then_inc(dve_done, up("dve"))
            dve.scalar_tensor_tensor(l_ckv[:, 0, :], l_ckv[:, 0, :], column("mla_kv_norm_2", l), l_tmp[:, S:2 * S],
                                     ALU.mult, ALU.mult).then_inc(dve_done, up("dve", "latents", l))

        def shared_key_act(act, l):
            act.wait_ge(dve_done, at("dve", "rope", ("2", l), "kpe"))
            for h in range(5):
                act.activation(l_k[64:96, h, :], l_kpe[64:96, 0, :], ACT.Copy).then_inc(act_done, up("act", "kpe", l) if h == 4 else up("act"))

        STEPS_FIRST = ("p nq0", "p nq1", "p nq2", "p nkc", "p nvc", "p nks", "r nkc", "p nvs0", "p nvs1", "r nks", "p nkw",
                       "r nq0", "p nvw0", "r nq1", "p nvw1", "r nkw", "p ng0", "r nq2", "p ng1", "p cq0", "p cq1")
        BESIDE = (("p ckv", "p kpe"), ("p rq0", "sums"), ("p rq1", "r kpe"), ("p rq2", "r rq0"), ("p rk0", "r rq1"),
                  ("p rk1", "r rq2"), ("p rk2", "r rk0"), ("p rv0", "r rk1"), ("p rv1", "r rk2"), ("p rg0", "p rg1"),
                  ("p rg2", "m mq0"), ("m mq1", "m mq2"), ("r mq0", "m mq3"), ("r mq1", "m mq4"), ("r mq2", "m mk0", "m mk1"),
                  ("r mq3", "m mk2", "m mk3"), ("r mq4", "m mk4"), ("m mv0", "m mv1"))
        STEPS = STEPS_FIRST + tuple(step for steps in BESIDE for step in steps)

        def rope_step(l, name):
            plan = rope_mla(l) if name[0] == "m" else rope2(l)
            i = [entry[0] for entry in plan].index(name)
            if name[0] == "m":
                return ("mla", l), i, plan[i], (act_done, at("act", "mla", l, name))
            return ("2", l), i, plan[i], (act_done, at("act", "proj", ("2", l), name))

        def step_read(l, n):
            kind, _, name = STEPS[n].partition(" ")
            if kind == "p":
                return act_done, at("act", "proj", ("2", l), name)
            if kind == "m":
                return act_done, at("act", "mla", l, name)
            if kind == "sums":
                return dve_done, at("dve", "latent mean squares", l)
            return dve_done, at("dve", "rope", rope_step(l, name)[0], name)

        def step_pe(pe, l, n):
            kind, _, name = STEPS[n].partition(" ")
            bank, bank_read = 2 + n % 2, step_read(l, n - 2) if n >= 2 else None
            if kind == "p":
                plan = plan2(l)
                project_pe(pe, ("2", l), plan, [entry[0] for entry in plan].index(name), bank, bank_read)
            elif kind == "r":
                tag, i, entry, ready = rope_step(l, name)
                rope_tile_pe(pe, tag, entry, bank, bank_read, ready)
            elif kind == "sums":
                latent_sums_pe(pe, l, bank, bank_read)
            else:
                entries = mla_entries(l)
                _, m, width, parts, place = [entry for entry in entries if entry[0] == name][0]
                pe.wait_ge(dve_done, at("dve", "latents", l))
                pe.wait_ge(*bank_read)
                for k, (lhsT, rhs) in enumerate(parts):
                    mm = pe.matmul(acc[0:m, bank, 0:width], lhsT, rhs, start=(k == 0), stop=(k == len(parts) - 1))
                if name == entries[-1][0]:
                    mm.then_inc(freed_by_pe, 1)
                else:
                    mm.then_inc(pe_done, up("pe", "mla", l, name))

        def step_act(act, l, n):
            kind, _, name = STEPS[n].partition(" ")
            if kind == "p":
                plan = plan2(l)
                project_act(act, ("2", l), plan, [entry[0] for entry in plan].index(name), 2 + n % 2)
            elif kind == "m":
                entries = mla_entries(l)
                _, m, width, parts, place = [entry for entry in entries if entry[0] == name][0]
                if name == entries[-1][0]:
                    act.wait_ge(freed_by_pe, freeing(("mla", l)))
                else:
                    act.wait_ge(pe_done, at("pe", "mla", l, name))
                act.activation(place, acc[0:m, 2 + n % 2, 0:width], ACT.Copy).then_inc(act_done, up("act", "mla", l, name))

        def step_dve(dve, l, n):
            kind, _, name = STEPS[n].partition(" ")
            if kind == "r":
                tag, i, entry, ready = rope_step(l, name)
                rope_tile_dve(dve, tag, i, entry, 2 + n % 2, ready)
            elif kind == "sums":
                latent_sums_dve(dve, l, 2 + n % 2)

        def steps_beside(u):
            first = len(STEPS_FIRST) + sum(len(steps) for steps in BESIDE[:u])
            return range(first, first + len(BESIDE[u])) if u < len(BESIDE) else ()

        def branches2(l):
            out = []
            for h in range(6):
                g_, i = h // 3, h % 3
                rows = slice(HD * g_, HD * g_ + HD)
                q = n_q[rows, i, :]
                for br, kind in enumerate(("cmp", "slc", "win")):
                    k = (n_kcT[rows, :], n_ks[rows, 0, :], n_kw[rows, 0, :])[br]
                    if br == 0:
                        v = lambda t, g_=g_: n_vcT[0:15, HD * g_:HD * g_ + HD]
                    else:
                        z = (None, n_vs, n_vw)[br]
                        v = lambda t, z=z, g_=g_: z[:, t, HD * g_:HD * g_ + HD]
                    out.append(dict(q=q, k=k, v=v, mask=K("cmp_hide") if br == 0 else K("causal"), kind="cmp" if br == 0 else "causal",
                                    scale=float(HD) ** -0.5, gate=lambda t, c=3 * h + br: n_gate[:, t, c:c + 1], first=br == 0,
                                    last=br == 2, p0=HD * (h % 2), place=mixT[HD * (h % 2):HD * (h % 2) + HD, h // 2, :],
                                    ready=[(act_done, at("act", "compressed", l)),
                                           (dve_done, at("dve", "rope", ("2", l), "nq2"))] if (h, br) == (0, 0) else [],
                                    mask_ready=[]))
            for h in range(5):
                p0 = HD * (h % 2)
                out.append(dict(q=l_q[0:96, h, :], k=l_k[0:96, h, :], v=lambda t, h=h: l_v[:, t, HD * h:HD * h + HD],
                                mask=K("causal"), kind="causal", scale=96.0 ** -0.5, gate=None, first=True, last=True, p0=p0,
                                place=mixT[p0:p0 + HD, 3 + h // 2, :], mask_ready=[],
                                ready=[(act_done, at("act", "mla", l, "mk4")), (dve_done, at("dve", "rope", ("mla", l), "mq4"))] if h == 0 else [],
                                v_ready=[(act_done, at("act", "mla", l, "mv1"))] if h == 0 else []))
            return out

        t_a = a_prob["2"]
        UPPER = slice(HD, P)

        def ret_at(h):
            return (h + 1) // 2, HD * ((h + 1) % 2)

        def ret_pe(pe, l):
            units = len(branches2(l))
            pe.wait_ge(act_done, at("act", "probT", ("2", l), units - 1))
            pe.wait_ge(dve_done, at("dve", "head out", ("2", l), 10))
            for h in range(6):
                if h < 5:
                    j, p0 = ret_at(h)
                    q, k = t_q[p0:p0 + HD, j, :], t_k[p0:p0 + HD, j, :]
                    if h >= 2:
                        pe.wait_ge(dve_done, at("dve", "decayed", l, h - 2))
                    pe.matmul(wrk[:, h % 2, 0:S], k[:, T0], q, start=True, stop=True)
                    pe.matmul(wrk[:, h % 2, S:384], k[:, T1], q[:, T1], start=True, stop=True).then_inc(pe_done, up("pe", "ret scores", l, h))
                if h >= 1:
                    j, p0 = ret_at(h - 1)
                    if h < 5:
                        pe.wait_ge(dve_done, at("dve", "decayed", l, h - 1))
                    else:
                        pe.wait_ge(*free_of(PLACE[("decay", l)]))
                    a = t_a[(h - 1) % 2]
                    pe.matmul(acc[p0:p0 + HD, j, 0:S], t_v[:, 0, HD * (h - 1):HD * h], a[:, 0:S], start=True, stop=False, skip_group_check=True)
                    pe.matmul(acc[p0:p0 + HD, j, P:S], t_v[:, 1, HD * (h - 1):HD * h], a[:, S:384], start=False, stop=True,
                              skip_group_check=True).then_inc(pe_done, up("pe", "ret out", l, h - 1))

            def head_sums(src, name):
                pe.matmul(wrk[UPPER, 2, 0:S], headsum[UPPER, UPPER], src[UPPER, 0, :], start=True, stop=True)
                pe.matmul(wrk[:, 3, :], headsum, src[:, 1:3, :].rearrange("p a t -> p (a t)"), start=True, stop=True)\
                  .then_inc(pe_done, up("pe", name, l))

            pe.wait_ge(act_done, at("act", "ret o", l))
            head_sums(t_q, "ret means")
            pe.wait_ge(act_done, at("act", "ret squares", l))
            head_sums(t_k, "ret variances")

        def ret_act(act, l):
            act.wait_ge(pe_done, at("pe", "ret out", l, 4))
            act.activation(t_q[UPPER, 0, :], acc[UPPER, 0, 0:S], ACT.Copy).then_inc(act_done, up("act"))
            act.activation(t_q[:, 1:3, :], acc[:, 1:3, 0:S], ACT.Copy).then_inc(act_done, up("act", "ret o", l))
            act.wait_ge(dve_done, at("dve", "ret centred", l))
            act.activation(t_k[UPPER, 0, :], t_q[UPPER, 0, :], ACT.Square).then_inc(act_done, up("act"))
            act.activation(t_k[:, 1:3, :], t_q[:, 1:3, :], ACT.Square).then_inc(act_done, up("act", "ret squares", l))
            act.wait_ge(dve_done, at("dve", "ret spreads", l))
            act.activation(t_k[UPPER, 0, :], t_k[UPPER, 0, :], ACT.Sqrt).then_inc(act_done, up("act"))
            act.activation(t_k[:, 1:3, :], t_k[:, 1:3, :], ACT.Sqrt).then_inc(act_done, up("act", "ret roots", l))

        def ret_dve(dve, l):
            decay = slot_of(("decay", l))[:, 0:5 * 384].rearrange("p (h n) -> p h n", h=5)
            dve.wait_ge(*landing(("decay", l)))
            for h in range(5):
                dve.wait_ge(pe_done, at("pe", "ret scores", l, h))
                if h >= 2:
                    dve.wait_ge(pe_done, at("pe", "ret out", l, h - 2))
                ins = dve.tensor_tensor(t_a[h % 2], wrk[:, h % 2, 0:384], decay[:, h, :], ALU.mult)
                if h < 4:
                    ins.then_inc(dve_done, up("dve", "decayed", l, h))
                else:
                    ins.then_inc(freed_by_dve, 1)
            parts = ((UPPER, slice(0, 1), wrk[UPPER, 2:3, 0:S]),
                     (slice(0, P), slice(1, 3), wrk[:, 3, :].rearrange("p (a t) -> p a t", a=2)))
            dve.wait_ge(pe_done, at("pe", "ret means", l))
            for i, (rows, tiles, sums) in enumerate(parts):
                dve.scalar_tensor_tensor(t_q[rows, tiles, :], sums, -1.0 / HD, t_q[rows, tiles, :], ALU.mult, ALU.add)\
                   .then_inc(dve_done, up("dve", "ret centred", l) if i else up("dve"))
            dve.wait_ge(pe_done, at("pe", "ret variances", l))
            for i, (rows, tiles, sums) in enumerate(parts):
                dve.tensor_scalar(t_k[rows, tiles, :], sums, 1.0 / HD, EPS, ALU.mult, ALU.add)\
                   .then_inc(dve_done, up("dve", "ret spreads", l) if i else up("dve"))
            dve.wait_ge(act_done, at("act", "ret roots", l))
            for rows, tiles, sums in parts:
                dve.reciprocal(t_k[rows, tiles, :], t_k[rows, tiles, :]).then_inc(dve_done, up("dve"))
            settle(dve, "dve", dve_done)
            for rows, tiles, sums in parts:
                dve.tensor_tensor(t_q[rows, tiles, :], t_q[rows, tiles, :], t_k[rows, tiles, :], ALU.mult).then_inc(dve_done, up("dve"))
            settle(dve, "dve", dve_done)
            for j in range(3):
                rows = UPPER if j == 0 else slice(0, P)
                col = column("ret_gain", 3 * l + j)[rows]
                dve.scalar_tensor_tensor(mixT[rows, 5 + j, :], t_q[rows, j, :], col, t_g[rows, j, :], ALU.mult, ALU.mult)\
                   .then_inc(dve_done, up("dve", "r out", l) if j == 2 else up("dve"))

        def mlp_pe(pe, l):
            n = len(ffn_groups(D_FF))
            base = tile_base("mlp", l)
            for g_ in range(n + 1):
                if g_ < n:
                    item = ("mup", l, g_)
                    pe.wait_ge(*landing(item))
                    w = w_cols(item, 512)
                    for j in range(4):
                        i = base + 4 * g_ + j
                        pe.wait_ge(ffn_act, i - 3)
                        for k in range(KD):
                            if g_ == 0 and j == 0:
                                pe.wait_ge(act_done, at("act", "h", ("mlp", l), k))
                            mm = pe.matmul(wrk[:, j, 0:S], w[:, k, j * P:(j + 1) * P], hT[:, k, :], start=(k == 0), stop=(k == KD - 1))
                        mm.then_inc(ffn_up, 1)
                if g_ >= 1:
                    ffn_down_pe(pe, g_ - 1, D_FF, ("mdown", l, g_ - 1), base, 0, ("mlp", l))

        def mlp_dve(dve, l):
            base = tile_base("mlp", l)
            groups = ffn_groups(D_FF)
            for g_ in range(len(groups)):
                if g_ >= 2:
                    dve.wait_ge(freed_by_pe, freeing(("mdown", l, g_ - 2)))
                for j in range(4):
                    i = base + 4 * g_ + j
                    dve.wait_ge(ffn_up, i + 1)
                    dve.tensor_scalar(F_SIL[:, j, :], wrk[:, j, 0:S], 0.0, None, ALU.max).then_inc(dve_done, up("dve"))
                    settle(dve, "dve", dve_done)
                    dve.tensor_tensor(F_ACT[:, 4 * (g_ % 2) + j, :], F_SIL[:, j, :], F_SIL[:, j, :], ALU.mult).then_inc(ffn_act, 1)
            for m in range(KD):
                dve.wait_ge(*down_wait(("mlp", l), ("mdown", l, len(groups) - 1), m))
                dve.tensor_tensor(xT[:, m, :], accv[:, m, :], xT[:, m, :], ALU.add).then_inc(dve_done, up("dve", "residual", ("mlp", l), m))

        def vec_cols(name, l):
            return lambda k: column(name, 8 * l + k)

        def x_ready2(l):
            return residual_of(("mlp", 0)) if l else (lambda k: (act_done, at("act", "h", ("between",), k)))

        LATENTS_AT, SHARED_KEY_AT = 0, 11
        assert STEPS[-1] == "m mv1" and "p rg2" in STEPS[:steps_beside(SHARED_KEY_AT)[0]]

        def block2_pe(pe, l):
            tag = ("2", l)
            norm_pe(pe, ("ln1", l))
            for n in range(len(STEPS_FIRST)):
                if STEPS[n] == "p cq0":
                    cmp_hidden_pe(pe, l)
                step_pe(pe, l, n)
            cmp_out_pe(pe, l)

            def beside(u):
                for n in steps_beside(u):
                    step_pe(pe, l, n)

            att_pe(pe, tag, branches2(l), beside)
            ret_pe(pe, l)
            outproj_pe(pe, tag, out_items("out2", l), [(dve_done, at("dve", "r out", l))])
            norm_pe(pe, ("mlp", l))
            mlp_pe(pe, l)

        def block2_act(act, l):
            tag = ("2", l)
            norm_act(act, ("ln1", l), x_ready2(l), vec_cols("ln1_gain_2", l), None)
            for n in range(len(STEPS_FIRST)):
                step_act(act, l, n)
                if STEPS[n] == "p nkw":
                    cmp_blocks_act(act, l)
            cmp_act(act, l)

            def beside(u):
                for n in steps_beside(u):
                    step_act(act, l, n)
                if u == LATENTS_AT:
                    latent_squares_act(act, l)
                if u == LATENTS_AT + 2:
                    root_act(act, at("dve", "latent mean squares", l), ("latent root", l), l_tmp[:, 0:512])
                if u == SHARED_KEY_AT:
                    shared_key_act(act, l)

            att_act(act, tag, branches2(l), beside)
            ret_act(act, l)
            norm_act(act, ("mlp", l), residual_of(("out2", l)), vec_cols("ln2_gain_2", l), None)

        def block2_dve(dve, l):
            tag = ("2", l)
            norm_dve(dve, ("ln1", l))
            for n in range(len(STEPS_FIRST)):
                step_dve(dve, l, n)
                if STEPS[n] == "r nkw":
                    cmp_dve(dve, l)

            def beside(u):
                if u == LATENTS_AT + 3:
                    latents_dve(dve, l)
                for n in steps_beside(u):
                    step_dve(dve, l, n)

            att_dve(dve, tag, branches2(l), beside)
            ret_dve(dve, l)
            residual_dve(dve, ("out2", l), None, out_waits(tag, out_items("out2", l)))
            norm_dve(dve, ("mlp", l))
            mlp_dve(dve, l)

        y_tok = flat_mix.rearrange("p (t d) -> p t d", t=2)

        def end_pe(pe):
            pe.wait_ge(act_done, at("act", "h", ("end",), KD - 1))
            for t in range(2):
                for k in range(KD):
                    mm = pe.transpose(flat_acc[:, t * D + k * P:t * D + (k + 1) * P], hT[:, k, t * P:(t + 1) * P], ident)
                mm.then_inc(pe_done, up("pe", "result", t))

        def end_act(act):
            for t in range(2):
                act.wait_ge(pe_done, at("pe", "result", t))
                act.activation(y_tok[:, t, :], flat_acc[:, t * D:(t + 1) * D], ACT.Copy).then_inc(act_done, up("act", "result", t))

        @block.sync
        def _(sp):
            body_sync(sp)
            for t in range(2):
                sp.wait_ge(act_done, at("act", "result", t))
                sp.dma_start(out[0, t * P:(t + 1) * P, :], y_tok[:, t, :]).then_inc(out_landed, 16)
            sp.wait_ge(out_landed, 32)

        @block.scalar
        def _(act):
            start_act(act)
            block1_act(act, 0)
            dense_act(act)
            block1_act(act, 1)
            route_act(act)
            experts_act(act)
            norm_act(act, ("between",), residual_of(("ffn", 1)), vec_cols("g_final", 0), None, xT)
            for l in range(DEPTH):
                block2_act(act, l)
            norm_act(act, ("end",), residual_of(("mlp", 1)), vec_cols("final_gain_2", 0), None)
            end_act(act)

        @block.tensor
        def _(pe):
            start_pe(pe)
            block1_pe(pe, 0)
            dense_pe(pe)
            block1_pe(pe, 1)
            route_pe(pe)
            experts_pe(pe)
            norm_pe(pe, ("between",))
            for l in range(DEPTH):
                block2_pe(pe, l)
            norm_pe(pe, ("end",))
            end_pe(pe)

        @block.vector
        def _(dve):
            start_dve(dve)
            block1_dve(dve, 0)
            dense_dve(dve)
            block1_dve(dve, 1)
            route_dve(dve)
            experts_dve(dve)
            experts_end_dve(dve)
            norm_dve(dve, ("between",))
            for l in range(DEPTH):
                block2_dve(dve, l)
            norm_dve(dve, ("end",))

    return count


_INS = ["x", "c", "positions", "w_ada", "b_ada", "g_norm_mix", "g_norm_ffn", "w_in", "w_out", "hgrn_lb_logits",
        "hgrn_out_norm", "gmlp_vnorm_g", "gmlp_vnorm_b", "gmlp_w_s", "gmlp_b_s", "ffn_w_gate", "ffn_w_up", "ffn_w_down",
        "moe_w_router", "moe_w_gate", "moe_w_up", "moe_w_down", "g_final", "positions_2", "ln1_gain_2", "w_in_2",
        "cmp_pos_k_2", "cmp_w1_k_2", "cmp_w2_k_2", "cmp_pos_v_2", "cmp_w1_v_2", "cmp_w2_v_2", "mla_q_norm_2", "mla_w_uq_2",
        "mla_kv_norm_2", "mla_w_ukv_2", "ret_gn_gain_2", "w_out_2", "ln2_gain_2", "w_up_2", "w_down_2", "final_gain_2"]


def written(known, arrays, bacc):
    nc = bacc.Bacc("TRN2", target_bir_lowering=False, num_devices=1)
    given = {}
    for name, a in arrays.items():
        given[name] = nc.dram_tensor(f"in_{name}_dram", a.shape, mybir.dt.from_np(a.dtype), kind="ExternalInput").ap()
    out = nc.dram_tensor("out_0_dram", (1, S, D), F32, kind="ExternalOutput").ap()
    return nc, program(nc, given, out, known)


def kernel(**inputs):
    import concourse.bacc as _bacc
    from concourse.bass_utils import run_bass_kernel_spmd as _run

    arrays = {name: np.ascontiguousarray(inputs[name]) for name in _INS}
    arrays["consts"], arrays["decay"] = CONSTS, DECAY
    _, count = written(None, arrays, _bacc)
    nc, _ = written(count.names, arrays, _bacc)
    r = _run(nc, [{f"in_{name}_dram": a for name, a in arrays.items()}], core_ids=[0])
    return r.results[0]["out_0_dram"]
```
